# Optimizing a Trainium2 kernel written in Bass

```python
import math
import jax
import jax.numpy as jnp
from jax import lax
import numpy as np

D_MODEL = 1024
BATCH = 1
SEQ = 256
DEPTH = 1

HEAD_DIM = 64
A_HEADS = 8
B_HEADS = 8
N_SELF_HEADS = A_HEADS + B_HEADS
W_A = A_HEADS * HEAD_DIM
W_B = B_HEADS * HEAD_DIM
MOBA_BLOCK = 256
MOBA_TOPK = 3
MOBA_Q_CHUNK = 64
Q_BLOCK = 128
DSA_KV_RANK = 256
IDX_HEADS = 8
IDX_DIM = 32
DSA_TOPK = 256
REL_BUCKETS = 32
REL_MAX_DIST = 128
X_HEADS = 4
W_X = X_HEADS * HEAD_DIM
MEM_LEN = 256
N_GROUPS = 4
EXPERTS_PER_GROUP = 8
N_EXPERTS = N_GROUPS * EXPERTS_PER_GROUP
EXPERT_TOPK = 2
D_EXPERT = 512
MOE_BLOCK = 256
EPS = 1e-6
NEG = -1e30

OFF_AQ = 0
OFF_AK = OFF_AQ + W_A
OFF_AV = OFF_AK + W_A
OFF_BQ = OFF_AV + W_A
OFF_CKV = OFF_BQ + W_B
OFF_IQ = OFF_CKV + DSA_KV_RANK
OFF_IK = OFF_IQ + IDX_HEADS * IDX_DIM
OFF_IW = OFF_IK + IDX_DIM
OFF_GA = OFF_IW + IDX_HEADS
OFF_GB = OFF_GA + D_MODEL
IN_COLS = OFF_GB + D_MODEL

kernel_name = 'hybrid_moba_dsa_hmoe_block'

def rms_norm(x, g):
    xf = x.astype(jnp.float32)
    y = xf * lax.rsqrt(jnp.mean(xf * xf, axis=-1, keepdims=True) + EPS)
    return (y * g.astype(jnp.float32)).astype(x.dtype)

def t5_bucket(dist):
    n = jnp.maximum(dist, 0)
    max_exact = REL_BUCKETS // 2
    nf = jnp.maximum(n, 1).astype(jnp.float32)
    large = max_exact + (jnp.log(nf / max_exact) / math.log(REL_MAX_DIST / max_exact)
                         * (REL_BUCKETS - max_exact)).astype(jnp.int32)
    large = jnp.minimum(large, REL_BUCKETS - 1)
    return jnp.where(n < max_exact, n, large)

def moba_attention(q, k, v, bias_tab):
    Bn, T, H, Dh = q.shape
    nkb = -(-T // MOBA_BLOCK)
    tp = nkb * MOBA_BLOCK
    pad = ((0, 0), (0, tp - T), (0, 0), (0, 0))
    kb = jnp.pad(k, pad).reshape(Bn, nkb, MOBA_BLOCK, H, Dh).transpose(0, 3, 1, 2, 4)
    vb = jnp.pad(v, pad).reshape(Bn, nkb, MOBA_BLOCK, H, Dh).transpose(0, 3, 1, 2, 4)
    kmean = jnp.mean(kb, axis=3)
    tk = min(MOBA_TOPK, nkb)
    scale = Dh ** -0.5
    bidx = jnp.arange(Bn)[:, None, None, None]
    hidx = jnp.arange(H)[None, None, :, None]
    hidx5 = jnp.arange(H)[None, None, :, None, None]
    inblk = jnp.arange(MOBA_BLOCK)
    blk_ids = jnp.arange(nkb)

    def chunk(i):
        q0 = i * MOBA_Q_CHUNK
        qb = lax.dynamic_slice_in_dim(q, q0, MOBA_Q_CHUNK, axis=1)
        tq = q0 + jnp.arange(MOBA_Q_CHUNK)
        own = q0 // MOBA_BLOCK
        gs = jnp.einsum('bchd,bhnd->bchn', qb, kmean).astype(jnp.float32)
        gs = jnp.where(blk_ids < own, gs, -jnp.inf)
        _, idx = lax.top_k(gs, tk)
        valid = idx < own
        k_sel = kb[bidx, hidx, idx]
        v_sel = vb[bidx, hidx, idx]
        pos = idx[..., None] * MOBA_BLOCK + inblk
        b_sel = bias_tab[hidx5, t5_bucket(tq[None, :, None, None, None] - pos)]
        l_sel = jnp.einsum('bchd,bchnkd->bchnk', qb, k_sel).astype(jnp.float32) * scale + b_sel
        l_sel = jnp.where(valid[..., None], l_sel, NEG).reshape(Bn, MOBA_Q_CHUNK, H, tk * MOBA_BLOCK)
        k_own = lax.dynamic_slice_in_dim(kb, own, 1, axis=2)[:, :, 0]
        v_own = lax.dynamic_slice_in_dim(vb, own, 1, axis=2)[:, :, 0]
        dist_own = tq[:, None] - (own * MOBA_BLOCK + inblk)[None, :]
        b_own = bias_tab[:, t5_bucket(dist_own)].transpose(1, 0, 2)[None]
        l_own = jnp.einsum('bchd,bhkd->bchk', qb, k_own).astype(jnp.float32) * scale + b_own
        l_own = jnp.where((dist_own >= 0)[None, :, None, :], l_own, NEG)
        p = jax.nn.softmax(jnp.concatenate([l_sel, l_own], axis=-1), axis=-1)
        n_sel = tk * MOBA_BLOCK
        p_sel = p[..., :n_sel].reshape(Bn, MOBA_Q_CHUNK, H, tk, MOBA_BLOCK).astype(v.dtype)
        p_own = p[..., n_sel:].astype(v.dtype)
        return (jnp.einsum('bchnk,bchnkd->bchd', p_sel, v_sel)
                + jnp.einsum('bchk,bhkd->bchd', p_own, v_own))

    out = lax.map(chunk, jnp.arange(T // MOBA_Q_CHUNK))
    return out.transpose(1, 0, 2, 3, 4).reshape(Bn, T, H, Dh)

def dsa_attention(q, k, v, q_idx, k_idx, w_idx, bias_tab):
    Bn, T, H, Dh = q.shape
    ksel = min(DSA_TOPK, T // 4)
    scale = Dh ** -0.5
    bidx = jnp.arange(Bn)[:, None, None]
    spos = jnp.arange(T)

    def chunk(i):
        q0 = i * Q_BLOCK
        qb = lax.dynamic_slice_in_dim(q, q0, Q_BLOCK, axis=1)
        qi = lax.dynamic_slice_in_dim(q_idx, q0, Q_BLOCK, axis=1)
        wi = lax.dynamic_slice_in_dim(w_idx, q0, Q_BLOCK, axis=1)
        tq = q0 + jnp.arange(Q_BLOCK)
        s = jax.nn.relu(jnp.einsum('bchd,bsd->bchs', qi, k_idx).astype(jnp.float32))
        s = jnp.einsum('bchs,bch->bcs', s, wi.astype(jnp.float32))
        s = jnp.where((spos[None, :] <= tq[:, None])[None], s, -jnp.inf)
        _, idx = lax.top_k(s, ksel)
        dist = tq[None, :, None] - idx
        k_g = k[bidx, idx]
        v_g = v[bidx, idx]
        bias = jnp.moveaxis(bias_tab[:, t5_bucket(dist)], 0, 2)
        l = jnp.einsum('bchd,bckhd->bchk', qb, k_g).astype(jnp.float32) * scale + bias
        l = jnp.where((dist >= 0)[:, :, None, :], l, NEG)
        p = jax.nn.softmax(l, axis=-1).astype(v.dtype)
        return jnp.einsum('bchk,bckhd->bchd', p, v_g)

    out = lax.map(chunk, jnp.arange(T // Q_BLOCK))
    return out.transpose(1, 0, 2, 3, 4).reshape(Bn, T, H, Dh)

def memory_cross_attention(h, m, wq, wk, wv, wo):
    Bn, T, _ = h.shape
    q = (h @ wq).reshape(Bn, T, X_HEADS, HEAD_DIM)
    km = (m @ wk).reshape(Bn, -1, X_HEADS, HEAD_DIM)
    vm = (m @ wv).reshape(Bn, -1, X_HEADS, HEAD_DIM)
    l = jnp.einsum('bthd,bmhd->bhtm', q, km).astype(jnp.float32) * HEAD_DIM ** -0.5
    p = jax.nn.softmax(l, axis=-1).astype(vm.dtype)
    o = jnp.einsum('bhtm,bmhd->bthd', p, vm).reshape(Bn, T, W_X)
    return o @ wo

def hier_moe(h, w_group, b_group, w_router, b_router, w1, w3, w2):
    Bn, T, D = h.shape
    N = Bn * T
    hf = h.reshape(N, D)
    g_logits = (hf @ w_group + b_group).astype(jnp.float32)
    g_prob = jax.nn.softmax(g_logits, axis=-1)
    g_sel = jnp.argmax(g_logits, axis=-1)
    g_w = jnp.take_along_axis(g_prob, g_sel[:, None], axis=1)
    e_logits = (hf @ w_router + b_router).astype(jnp.float32).reshape(N, N_GROUPS, EXPERTS_PER_GROUP)
    within = jnp.take_along_axis(e_logits, g_sel[:, None, None], axis=1)[:, 0]
    top_v, top_i = lax.top_k(within, EXPERT_TOPK)
    top_p = jax.nn.softmax(top_v, axis=-1)
    weight = g_w * top_p
    eid = g_sel[:, None] * EXPERTS_PER_GROUP + top_i
    A = N * EXPERT_TOPK
    e_flat = eid.reshape(A)
    tok = jnp.repeat(jnp.arange(N, dtype=jnp.int32), EXPERT_TOPK)
    w_flat = weight.reshape(A)
    counts = jax.ops.segment_sum(jnp.ones((A,), jnp.int32), e_flat, num_segments=N_EXPERTS)
    padded = ((counts + MOE_BLOCK - 1) // MOE_BLOCK) * MOE_BLOCK
    seg_end = jnp.cumsum(padded)
    seg_start = seg_end - padded
    first = jnp.cumsum(counts) - counts
    order = jnp.argsort(e_flat, stable=True)
    e_s = e_flat[order]
    dest = seg_start[e_s] + (jnp.arange(A) - first[e_s])
    R = A + N_EXPERTS * MOE_BLOCK
    NB = R // MOE_BLOCK
    row_tok = jnp.full((R,), N, jnp.int32).at[dest].set(tok[order])
    row_w = jnp.zeros((R,), jnp.float32).at[dest].set(w_flat[order])
    hpad = jnp.concatenate([hf, jnp.zeros((1, D), hf.dtype)], axis=0)
    xr = hpad[row_tok].reshape(NB, MOE_BLOCK, D)
    blk_e = jnp.minimum(jnp.searchsorted(seg_end, jnp.arange(NB) * MOE_BLOCK, side='right'),
                        N_EXPERTS - 1)

    def expert_block(args):
        xb, e = args
        return (jax.nn.silu(xb @ w1[e]) * (xb @ w3[e])) @ w2[e]

    yr = lax.map(expert_block, (xr, blk_e)).reshape(R, D)
    out = jnp.zeros((N + 1, D), jnp.float32).at[row_tok].add(yr.astype(jnp.float32) * row_w[:, None])
    return out[:N].astype(h.dtype).reshape(Bn, T, D)

def setup_inputs(seed: int = 0) -> dict:
    key = jax.random.key(seed)
    ks = jax.random.split(key, 26)

    def nrm(k, shape, scale):
        return jax.random.normal(k, shape, jnp.float32) * scale

    def gain(k, shape):
        return 1.0 + 0.02 * jax.random.normal(k, shape, jnp.float32)

    L = DEPTH
    return {
        'x': nrm(ks[0], (BATCH, SEQ, D_MODEL), 1.0),
        'mem': nrm(ks[1], (BATCH, MEM_LEN, D_MODEL), 1.0),
        'rel_bias': nrm(ks[2], (REL_BUCKETS, N_SELF_HEADS), 0.5),
        'final_norm': gain(ks[3], (D_MODEL,)),
        'norm_mix': gain(ks[4], (L, D_MODEL)),
        'w_in': nrm(ks[5], (L, D_MODEL, IN_COLS), D_MODEL ** -0.5),
        'ckv_norm': gain(ks[6], (L, DSA_KV_RANK)),
        'w_uk': nrm(ks[7], (L, DSA_KV_RANK, W_B), DSA_KV_RANK ** -0.5),
        'w_uv': nrm(ks[8], (L, DSA_KV_RANK, W_B), DSA_KV_RANK ** -0.5),
        'w_oa': nrm(ks[9], (L, W_A, D_MODEL), W_A ** -0.5),
        'w_ob': nrm(ks[10], (L, W_B, D_MODEL), W_B ** -0.5),
        'w_out': nrm(ks[11], (L, D_MODEL, D_MODEL), D_MODEL ** -0.5),
        'norm_x': gain(ks[12], (L, D_MODEL)),
        'mem_norm': gain(ks[13], (L, D_MODEL)),
        'wq_x': nrm(ks[14], (L, D_MODEL, W_X), D_MODEL ** -0.5),
        'wk_x': nrm(ks[15], (L, D_MODEL, W_X), D_MODEL ** -0.5),
        'wv_x': nrm(ks[16], (L, D_MODEL, W_X), D_MODEL ** -0.5),
        'wo_x': nrm(ks[17], (L, W_X, D_MODEL), W_X ** -0.5),
        'norm_moe': gain(ks[18], (L, D_MODEL)),
        'w_group': nrm(ks[19], (L, D_MODEL, N_GROUPS), D_MODEL ** -0.5),
        'b_group': nrm(ks[20], (L, N_GROUPS), 0.01),
        'w_router': nrm(ks[21], (L, D_MODEL, N_EXPERTS), D_MODEL ** -0.5),
        'b_router': nrm(ks[22], (L, N_EXPERTS), 0.01),
        'w1': nrm(ks[23], (L, N_EXPERTS, D_MODEL, D_EXPERT), D_MODEL ** -0.5),
        'w3': nrm(ks[24], (L, N_EXPERTS, D_MODEL, D_EXPERT), D_MODEL ** -0.5),
        'w2': nrm(ks[25], (L, N_EXPERTS, D_EXPERT, D_MODEL), D_EXPERT ** -0.5),
    }

def reference(x, mem, rel_bias, final_norm, norm_mix, w_in, ckv_norm, w_uk, w_uv, w_oa, w_ob,
              w_out, norm_x, mem_norm, wq_x, wk_x, wv_x, wo_x, norm_moe, w_group, b_group,
              w_router, b_router, w1, w3, w2):
    Bn, T, _ = x.shape
    bias_a = rel_bias[:, :A_HEADS].T
    bias_b = rel_bias[:, A_HEADS:].T
    idx_scale = (IDX_HEADS ** -0.5) * (IDX_DIM ** -0.5)
    for l in range(DEPTH):
        h = rms_norm(x, norm_mix[l])
        z = h @ w_in[l]
        qa = z[..., OFF_AQ:OFF_AK].reshape(Bn, T, A_HEADS, HEAD_DIM)
        ka = z[..., OFF_AK:OFF_AV].reshape(Bn, T, A_HEADS, HEAD_DIM)
        va = z[..., OFF_AV:OFF_BQ].reshape(Bn, T, A_HEADS, HEAD_DIM)
        oa = moba_attention(qa, ka, va, bias_a).reshape(Bn, T, W_A) @ w_oa[l]
        qb = z[..., OFF_BQ:OFF_CKV].reshape(Bn, T, B_HEADS, HEAD_DIM)
        ckv = rms_norm(z[..., OFF_CKV:OFF_IQ], ckv_norm[l])
        kb = (ckv @ w_uk[l]).reshape(Bn, T, B_HEADS, HEAD_DIM)
        vb = (ckv @ w_uv[l]).reshape(Bn, T, B_HEADS, HEAD_DIM)
        q_idx = z[..., OFF_IQ:OFF_IK].reshape(Bn, T, IDX_HEADS, IDX_DIM)
        k_idx = z[..., OFF_IK:OFF_IW]
        w_idx = z[..., OFF_IW:OFF_GA] * idx_scale
        ob = dsa_attention(qb, kb, vb, q_idx, k_idx, w_idx, bias_b).reshape(Bn, T, W_B) @ w_ob[l]
        ga = jax.nn.sigmoid(z[..., OFF_GA:OFF_GB])
        gb = jax.nn.sigmoid(z[..., OFF_GB:IN_COLS])
        x = x + (ga * oa + gb * ob) @ w_out[l]
        x = x + memory_cross_attention(rms_norm(x, norm_x[l]), rms_norm(mem, mem_norm[l]),
                                       wq_x[l], wk_x[l], wv_x[l], wo_x[l])
        x = x + hier_moe(rms_norm(x, norm_moe[l]), w_group[l], b_group[l], w_router[l],
                         b_router[l], w1[l], w3[l], w2[l])
    return rms_norm(x, final_norm)


_drawn_inputs = setup_inputs


def setup_inputs(seed=0):
    import zlib

    import numpy as np

    out = dict(_drawn_inputs(seed))
    spreads = {}
    factors = {'final_norm': 9.034,
     'ckv_norm': 4.828,
     'norm_x': 4.887,
     'mem_norm': 4.769,
     'b_group': 33.496,
     'b_router': 43.473,
     'norm_moe': 8.0}
    for name, (base, spread) in spreads.items():
        noise = np.random.default_rng([zlib.crc32(name.encode()), seed]).standard_normal(out[name].shape)
        drawn = base * np.exp(spread * noise) if base else spread * noise
        out[name] = jnp.asarray(drawn.astype(out[name].dtype))
    for name, factor in factors.items():
        out[name] = (out[name] * factor).astype(out[name].dtype)
    return out
```

```python
import math
from contextlib import ExitStack

import numpy as np

import concourse.bass as bass
from concourse import mybir

ALU = mybir.AluOpType
ACT = mybir.ActivationFunctionType
AX_X = mybir.AxisListType.X
F32 = mybir.dt.float32
I32 = mybir.dt.int32

P = 128
T, D = 256, 1024
TT = T // P
KD = D // P
HEADS, HD = 8, 64
W_HEADS = HEADS * HD
RANK = 256
IDX_HEADS, IDX_DIM = 8, 32
TOPK = min(256, T // 4)
BUCKETS, MAX_DIST = 32, 128
MEM, X_HEADS = 256, 4
W_X = X_HEADS * HD
GROUPS, PER_GROUP = 4, 8
EXPERTS = GROUPS * PER_GROUP
D_E = 512
FC = D_E // P
EPS = 1e-6
NEG = -1e30
TAKEN = -3e38
SCALE = HD ** -0.5

C_AQ, C_AK, C_AV, C_BQ = (i * W_HEADS for i in range(4))
C_CKV = 4 * W_HEADS
C_IQ = C_CKV + RANK
C_IK = C_IQ + IDX_HEADS * IDX_DIM
C_GA = C_IK + IDX_DIM + IDX_HEADS
C_GB = C_GA + D

SLOTS = 32
SHARE = P // SLOTS
STEPS = EXPERTS // SHARE
ROUNDS = T // SLOTS

RING = 6
SLOT = 4096
MOE_CHUNKS = 12
assert MOE_CHUNKS % RING == 0

K_ID, K_LT, K_ONE, K_CAUSAL = 0, P, 2 * P, 3 * P
K_SLOT = K_CAUSAL + 3 * P
K_DESC = K_SLOT + SLOTS
K_N = K_DESC + EXPERTS


def shape_constants():
    c = np.zeros((P, K_N), np.float32)
    p = np.arange(P)[:, None]
    i = np.arange(P)[None, :]
    c[:, K_ID:K_ID + P] = p == i
    c[:, K_LT:K_LT + P] = p < i
    c[:, K_ONE:K_ONE + P] = 1.0
    c[:, K_CAUSAL:K_CAUSAL + P] = np.where(i > p, NEG, 0.0)
    c[:, K_CAUSAL + P:K_CAUSAL + 3 * P] = np.where(np.arange(T)[None, :] > p + P, NEG, 0.0)
    c[:, K_SLOT:K_SLOT + SLOTS] = np.arange(SLOTS)
    c[:, K_DESC:K_DESC + EXPERTS] = EXPERTS - np.arange(EXPERTS)
    dist = T - 1 - np.arange(T + P)
    exact = BUCKETS // 2
    b = np.zeros((BUCKETS, T + P), np.float32)
    for m, n in enumerate(dist):
        if n < 0:
            continue
        if n >= exact:
            n = min(exact + int(math.log(n / exact) / math.log(MAX_DIST / exact) * (BUCKETS - exact)), BUCKETS - 1)
        b[n, m] = 1.0
    below = np.broadcast_to(np.where(dist < 0, NEG, 0.0).astype(np.float32), (2 * HEADS, T + P))
    return c, b, np.ascontiguousarray(below)


JOBS = (["iq", "ikw", "ckv", "ckvT", "aq0", "aq1", "ak0", "ak1", "av0", "av1"]
        + ["km", "vm"] + [f"ga{i}" for i in range(4)] + ["gb0", "gb1"]
        + ["kb0", "kb1", "vb0", "vb1", "bq0", "bq1", "gb2", "gb3"]
        + [f"oa{i}" for i in range(4)] + [f"ob{i}" for i in range(4)]
        + [f"out{i}" for i in range(4)] + ["qx", "ox0", "ox1"] + [f"xo{i}" for i in range(4)]
        + ["router", "count"])

CHUNKS = ["ckv_iq", "aq", "ak", "av", "kx_vx", "ga0", "ga1", "gb0", "uk_uv", "bq", "gb1",
          "oa", "ob", "out0", "out1", "qx_ox"]
FIRST_MOE = len(CHUNKS)
LAST_JOB = {"ckv_iq": "ckv", "aq": "aq1", "ak": "ak1", "av": "av1", "ga0": "ga1", "ga1": "ga3", "gb0": "gb1",
            "gb1": "gb3", "uk_uv": "vb1", "bq": "bq1", "kx_vx": "vm", "oa": "oa3", "ob": "ob3", "out0": "out1",
            "out1": "out3", "qx_ox": "xo3"}
PARTS = {"uk_uv": 2, "kx_vx": 2, "qx_ox": 2}


def landed(position):
    slot = position % RING
    parts = sum(PARTS.get(CHUNKS[c], 1) if c < FIRST_MOE else 1 for c in range(slot, position + 1, RING))
    return slot, 16 * parts


def decoder_layer(nc, x, mem, rel_bias, final_norm, norm_mix, w_in, ckv_norm, w_uk, w_uv, w_oa, w_ob,
                  w_out, norm_x, mem_norm, wq_x, wk_x, wv_x, wo_x, norm_moe, w_group, b_group,
                  w_router, b_router, w1, w3, w2, consts, buckets, below, out):
    with ExitStack() as ctx:
        def sb(name, shape, dt=F32):
            return ctx.enter_context(nc.sbuf_tensor(name, shape, dt))

        def sem(name):
            return ctx.enter_context(nc.semaphore(name))

        ring = sb("ring", [P, RING, SLOT])
        x_sb = sb("x_sb", [P, TT, D])
        xn = sb("xn", [P, TT, D])
        hT = sb("hT", [P, KD, T])
        ga = sb("ga", [P, KD, T])
        gb = sb("gb", [P, KD, T])
        aqT, akT, bqT, kbT = (sb(n, [P, 4, T]) for n in ("aqT", "akT", "bqT", "kbT"))
        av, vb = (sb(n, [P, TT, W_HEADS]) for n in ("av", "vb"))
        iqT = sb("iqT", [P, 2, T])
        ikT = sb("ikT", [P, T])
        iw = sb("iw", [P, TT, IDX_HEADS])
        ckvn = sb("ckvn", [P, TT, RANK])
        kmT = sb("kmT", [P, 2, MEM])
        vm = sb("vm", [P, 2, W_X])
        bias = sb("bias", [P, 2 * HEADS, T])
        score = sb("score", [P, 3 * P])
        logit = sb("logit", [P, 2, 2, 3 * P])
        probT = sb("probT", [P, 2, 2, 3 * P])
        const = sb("const", [P, K_N])
        w_ikw = sb("w_ikw", [P, KD, IDX_DIM + IDX_HEADS])
        w_rt = sb("w_rt", [P, KD, GROUPS + EXPERTS])
        b_rt = sb("b_rt", [P, GROUPS + EXPERTS])
        gain = sb("gain", [P, 4, KD])
        gain_c = sb("gain_c", [P, 2])
        rel_sb = sb("rel_sb", [BUCKETS, 2 * HEADS])
        half = sb("half", [P, 2])
        ssq = sb("ssq", [P, 6, 2])
        var = sb("var", [P, 6, 2])
        rstd = sb("rstd", [P, 6, 2])
        top8 = sb("top8", [P, 2, 8])
        nmax = sb("nmax", [P, 8, 4])
        esum = sb("esum", [P, 8, 4])
        erec = sb("erec", [P, 8, 4])
        xnmax = sb("xnmax", [P, X_HEADS, 2])
        xsum = sb("xsum", [P, X_HEADS, 2])
        xrec = sb("xrec", [P, X_HEADS, 2])
        rs = sb("rs", [P, 16, TT])
        rl = sb("rl", [P, TT, GROUPS + EXPERTS])
        most = sb("most", [P, 1])
        most_i = sb("most_i", [P, 1], I32)
        mem_sb = ga[:].rearrange("p a b -> p (a b)").rearrange("p (t d) -> p t d", t=TT)
        memT = gb
        relu = xn
        relu4 = relu[:].rearrange("p a b -> p (a b)")[:, 0:4 * 3 * P].rearrange("p (h c) -> p h c", h=4)
        bias_rows = probT[0:2 * HEADS, 0, 0, :]
        one_hot = probT[0:BUCKETS, 1, 0, :]
        below_sb = probT[0:2 * HEADS, 1, 1, :]
        ckvT = iqT
        qxT = iqT
        unpicked = score
        oxT = ckvn
        merged = hT
        bias_flat = bias[:].rearrange("p h c -> p (h c)")
        xprob = bias_flat[:, 0:2048].rearrange("p (h t m) -> p h t m", h=X_HEADS, t=TT)
        xprobT = bias_flat[:, 2048:4096].rearrange("p (h m t) -> p h m t", h=X_HEADS, m=2)
        xeT = aqT[:].rearrange("p a b -> p (a b)").rearrange("p (k s) -> p k s", k=KD)
        silu_sb = akT[:].rearrange("p a b -> p (a b)")[:, 0:D_E]
        act_sb = akT[:].rearrange("p a b -> p (a b)")[:, D_E:2 * D_E]
        actT = bqT[:].rearrange("p a b -> p (a b)")[:, 0:D_E].rearrange("p (f s) -> p f s", f=FC)
        selwT = bqT[:].rearrange("p a b -> p (a b)")[:, D_E:D_E + T]
        y_sb = kbT[:].rearrange("p a b -> p (a b)")
        sel = av[:].rearrange("p a b -> p (a b)")[:, 0:T].rearrange("p (t e s) -> p t e s", t=TT, e=SHARE)
        selw = av[:].rearrange("p a b -> p (a b)")[:, T:2 * T].rearrange("p (t e s) -> p t e s", t=TT, e=SHARE)
        fgain = ga[:, 0:4, :].rearrange("p a b -> p (a b)")
        rt = gb[:].rearrange("p a b -> p (a b)")[:, 0:14 * TT * EXPERTS].rearrange(
            "p (n t e) -> p n t e", n=14, t=TT)
        ident = const[:, K_ID:K_ID + P]

        ps = ctx.enter_context(nc.psum_tensor("ps", [P, 8, 512], F32))
        turned = ps[:, 2:6, :].rearrange("p b (k t) -> p (b k) t", k=2)

        bias_dram = nc.dram_tensor("bias_rows_dram", [2 * HEADS, T + P], F32).ap()
        bias_rep = nc.dram_tensor("bias_rep_dram", [2 * HEADS, P, T + P], F32).ap()

        x_in, mem_in, const_in, gain_in = sem("x_in"), sem("mem_in"), sem("const_in"), sem("gain_in")
        small_in, tab_in, bias_out, bias_repeated, bias_in, fgain_in = (
            sem("small_in"), sem("tab_in"), sem("bias_out"), sem("bias_repeated"), sem("bias_in"), sem("fgain_in"))
        slot_in = [sem(f"slot_in{i}") for i in range(RING)]
        chunk_used = sem("chunk_used")
        half_set = sem("half_set")
        squares = sem("squares")
        rstd_set = sem("rstd_set")
        xn_set = sem("xn_set")
        mem_scaled = sem("mem_scaled")
        turn_done = sem("turn_done")
        turn_copied_a, turn_copied_v = sem("turn_copied_a"), sem("turn_copied_v")
        biasrow_done, biasrow_set = sem("biasrow_done"), sem("biasrow_set")
        proj_done = [sem(f"proj_done{i}") for i in range(2)]
        proj_free = [sem(f"proj_free{i}") for i in range(2)]
        idx_done, relu_set, idx_added = sem("idx_done"), sem("relu_set"), sem("idx_added")
        csq_done, crstd_set = sem("csq_done"), sem("crstd_set")
        s_done, s_read, max_set, exp_set, prob_set = (
            sem("s_done"), sem("s_read"), sem("max_set"), sem("exp_set"), sem("prob_set"))
        probT_done, probT_copied_a, probT_copied_v = (
            sem("probT_done"), sem("probT_copied_a"), sem("probT_copied_v"))
        o_done, o_copied = sem("o_done"), sem("o_copied")
        gates_set = sem("gates_set")
        merged_set = sem("merged_set")
        resid_set = sem("resid_set")
        xs_done, xmax_set, xexp_set, xprob_set = (
            sem("xs_done"), sem("xmax_set"), sem("xexp_set"), sem("xprob_set"))
        xpT_done, xpT_copied_a, xpT_copied_v = sem("xpT_done"), sem("xpT_copied_a"), sem("xpT_copied_v")
        rexp_asked, rexp_set = sem("rexp_asked"), sem("rexp_set")
        routed, placed, most_set = sem("routed"), sem("placed"), sem("most_set")
        sel_set, xe_done, xe_copied, selwT_done, selwT_copied = (
            sem("sel_set"), sem("xe_done"), sem("xe_copied"), sem("selwT_done"), sem("selwT_copied"))
        silu_set, act_set, actT_done, actT_copied = (
            sem("silu_set"), sem("act_set"), sem("actT_done"), sem("actT_copied"))
        y_copied_a, y_copied_v, added = (
            sem("y_copied_a"), sem("y_copied_v"), sem("added"))
        moe_done, fsq, frstd_set, out_set, out_written = (
            sem("moe_done"), sem("fsq"), sem("frstd_set"), sem("out_set"), sem("out_written"))
        dve_step, pool_step = sem("dve_step"), sem("pool_step")
        sel_made, moved = sem("sel_made"), sem("moved")
        ikw_in = sem("ikw_in")
        chunk_asked = sem("chunk_asked")

        def job(name):
            j = JOBS.index(name)
            return j % 2, j // 2 + 1

        def job_computed(eng, name):
            b, n = job(name)
            eng.wait_ge(proj_done[b], n)
            return ps[:, b, :]

        def job_evacuated(eng, name):
            b, n = job(name)
            eng.wait_ge(proj_free[b], n)

        def evacuates(ins, name):
            ins.then_inc(proj_free[job(name)[0]], 1)

        def chunk(name):
            return ring[:, CHUNKS.index(name) % RING, :]

        def chunk_landed(eng, name):
            s, v = landed(CHUNKS.index(name))
            eng.wait_ge(slot_in[s], v)

        w_in2, w_out2 = w_in[0], w_out[0]
        block = ctx.enter_context(nc.Block())

        @block.sync
        def _(sp):
            def cols(c0, n):
                return w_in2.rearrange("(p k) n -> p k n", k=KD)[:, :, c0:c0 + n]

            def fill(name, parts):
                c = CHUNKS.index(name)
                if c >= RING:
                    job_computed(sp, LAST_JOB[CHUNKS[c - RING]])
                at = 0
                for src in parts:
                    n = src.shape[1] * src.shape[2]
                    dst = chunk(name)[:, at:at + n].rearrange("p (k n) -> p k n", n=src.shape[2])
                    sp.dma_start(dst, src).then_inc(slot_in[c % RING], 16)
                    at += n

            sp.dma_start(x_sb[:], x[0].rearrange("(t p) d -> p t d", p=P)).then_inc(x_in, 16)
            fill("ckv_iq", [cols(C_CKV, 512)])
            fill("aq", [cols(C_AQ, 512)])
            sp.dma_start(mem_sb, mem[0].rearrange("(t p) d -> p t d", p=P)).then_inc(mem_in, 16)
            fill("ak", [cols(C_AK, 512)])
            fill("av", [cols(C_AV, 512)])
            sp.wait_ge(biasrow_set, 1)
            sp.dma_start(bias_dram, bias_rows).then_inc(bias_out, 16)
            fill("kx_vx", [w[0].rearrange("(k p) n -> p k n", k=KD) for w in (wk_x, wv_x)])
            fill("ga0", [cols(C_GA, 512)])
            fill("ga1", [cols(C_GA + 512, 512)])
            sp.wait_ge(bias_out, 16)
            sp.dma_start(bias_rep, bias_dram.unsqueeze(1).to_broadcast([2 * HEADS, P, T + P])).then_inc(bias_repeated, 16)
            fill("gb0", [cols(C_GB, 512)])
            sp.wait_ge(bias_repeated, 16)
            toeplitz = bass.AP(tensor=bias_rep.tensor, offset=P - 1,
                               ap=[[T + P - 1, P], [P * (T + P), 2 * HEADS], [1, T]])
            sp.dma_start(bias[:], toeplitz).then_inc(bias_in, 16)
            fill("uk_uv", [w[0].rearrange("(p k) n -> p k n", k=2) for w in (w_uk, w_uv)])
            fill("bq", [cols(C_BQ, 512)])
            fill("gb1", [cols(C_GB + 512, 512)])
            fill("oa", [w_oa[0].rearrange("(k p) n -> p k n", p=P)])
            fill("ob", [w_ob[0].rearrange("(k p) n -> p k n", p=P)])
            for i in range(2):
                fill(f"out{i}", [w_out2.rearrange("(k p) n -> p k n", p=P)[:, :, 512 * i:512 * i + 512]])
            fill("qx_ox", [wq_x[0].rearrange("(p k) n -> p k n", k=KD), wo_x[0].rearrange("(k p) n -> p k n", p=P)])

            w1v = w1[0].rearrange("e (p k) n -> p e (k n)", k=KD)
            w3v = w3[0].rearrange("e (p k) n -> p e (k n)", k=KD)
            w2v = w2[0].rearrange("e (p f) n -> p e (f n)", f=FC)

            def load(q, e0):
                if q < 8:
                    src = (w1v, w3v)[q % 2][:, bass.ds(e0, SHARE), (q // 2) * 2 * D_E:(q // 2 + 1) * 2 * D_E]
                else:
                    src = w2v[:, bass.ds(e0, SHARE), (q - 8) * D:(q - 7) * D]
                s = (FIRST_MOE + q) % RING
                sp.dma_start(ring[:, s, :].rearrange("p (e n) -> p e n", e=SHARE), src).then_inc(slot_in[s], 16)

            def load_part(step, expert, first):
                used = [sp.snap(step * MOE_CHUNKS + (q - RING + 1)) for q in range(first, first + RING)]
                e0 = sp.snap(expert)
                for q in range(first, first + RING):
                    sp.wait_ge(chunk_used, used[q - first])
                    sp.sem_inc(chunk_asked, 1)
                    load(q, e0)

            def load_rest(r, first_part_loaded):
                if not first_part_loaded:
                    load_part(r * STEPS, 0, 0)
                with sp.Fori(0, STEPS - 1) as g:
                    load_part(r * STEPS + g, g * SHARE, RING)
                    load_part(r * STEPS + g + 1, g * SHARE + SHARE, 0)
                load_part(r * STEPS + (STEPS - 1), (STEPS - 1) * SHARE, RING)

            for q in range(RING):
                job_computed(sp, LAST_JOB[CHUNKS[FIRST_MOE + q - RING]])
                if q == RING - 1:
                    sp.wait_ge(merged_set, 4)
                    sp.dma_start(fgain, final_norm.rearrange("(a d) -> a d", a=1).to_broadcast([P, D])).then_inc(fgain_in, 16)
                load(q, 0)
            load_rest(0, True)
            sp.wait_ge(most_set, 1)
            fullest = sp.value_load(most_i[0:1, 0:1], min_val=0, max_val=T)
            with sp.Fori(1, ROUNDS) as r:
                with sp.If(fullest > r * SLOTS):
                    load_rest(r, False)
            out_v = out[0].rearrange("(t p) d -> p t d", p=P)
            for t in range(TT):
                sp.wait_ge(out_set, t + 1)
                sp.dma_start(out_v[:, t, :], xn[:, t, :]).then_inc(out_written, 16)
            sp.wait_ge(out_written, 16 * TT)

        @block.tensor
        def _(pe):
            def turn(src, n):
                for b in range(4):
                    for k in range(2 * b, 2 * b + 2):
                        for t in range(TT):
                            m = pe.transpose(turned[:, k, t * P:(t + 1) * P], src[:, t, k * P:(k + 1) * P], ident)
                    m.then_inc(turn_done, 1)

            def hT_ready(n):
                pe.wait_ge(turn_copied_a, 2 * n)
                pe.wait_ge(turn_copied_v, 2 * n)

            def begin(name):
                b, n = job(name)
                if n > 1:
                    pe.wait_ge(proj_free[b], n - 1)
                return ps[:, b, :]

            def end(ins, name):
                ins.then_inc(proj_done[job(name)[0]], 1)

            def columns(name, w, src, blocks, width):
                o = begin(name)
                kk = w.shape[1]
                for i, c in enumerate(blocks):
                    for k in range(kk):
                        m = pe.matmul(o[:, i * width:(i + 1) * width], w[:, k, c * P:(c + 1) * P], src[:, k, :],
                                      start=(k == 0), stop=(k == kk - 1))
                end(m, name)
                return m

            def rows(name, w, src, tiles, c0, n):
                o = begin(name)
                kk = w.shape[1]
                for i, t in enumerate(tiles):
                    for k in range(kk):
                        m = pe.matmul(o[:, i * n:(i + 1) * n], src[:, k, t * P:(t + 1) * P], w[:, k, c0:c0 + n],
                                      start=(k == 0), stop=(k == kk - 1))
                end(m, name)
                return m

            def w512(name):
                return chunk(name)[:, 0:4096].rearrange("p (k n) -> p k n", k=KD)

            pe.wait_ge(const_in, 16)
            pe.wait_ge(tab_in, 48)
            m = pe.matmul(ps[0:2 * HEADS, 7, 0:3 * P], rel_sb[:], one_hot, start=True, stop=True)
            m.then_inc(biasrow_done, 1)
            pe.wait_ge(xn_set, 2)
            turn(xn, 0)
            hT_ready(1)
            chunk_landed(pe, "ckv_iq")
            w = w512("ckv_iq")
            columns("iq", w[:, :, RANK:2 * RANK], hT, (0, 1), T)
            pe.wait_ge(ikw_in, 16)
            o = begin("ikw")
            for j in range(4):
                for k in range(KD):
                    m = pe.matmul(o[32 * j:32 * j + 32, 0:T], w_ikw[:, k, 0:IDX_DIM], hT[:, k, :],
                                  start=(k == 0), stop=(k == KD - 1))
            for t in range(TT):
                for k in range(KD):
                    m = pe.matmul(o[:, T + 8 * t:T + 8 * t + 8], hT[:, k, t * P:(t + 1) * P],
                                  w_ikw[:, k, IDX_DIM:IDX_DIM + IDX_HEADS], start=(k == 0), stop=(k == KD - 1))
            end(m, "ikw")

            def index_logits(b):
                for h in range(4):
                    q = 32 * h
                    pe.matmul(ps[:, 2 + h, 0:P], iqT[q:q + 32, b, 0:P], ikT[q:q + 32, 0:P], start=True, stop=True)
                    m = pe.matmul(ps[:, 2 + h, P:3 * P], iqT[q:q + 32, b, P:T], ikT[q:q + 32, :],
                                  start=True, stop=True)
                m.then_inc(idx_done, 1)

            job_evacuated(pe, "iq")
            job_evacuated(pe, "ikw")
            index_logits(0)
            rows("ckv", w, hT, (0, 1), 0, RANK)
            pe.wait_ge(relu_set, 1)
            index_logits(1)
            pe.wait_ge(mem_scaled, 2)
            pe.wait_ge(relu_set, 2)
            turn(mem_sb, 1)
            job_evacuated(pe, "ckv")
            o = begin("ckvT")
            for r in range(2):
                for t in range(TT):
                    m = pe.transpose(o[:, r * T + t * P:r * T + (t + 1) * P],
                                     ckvn[:, t, r * P:(r + 1) * P], ident)
            end(m, "ckvT")
            for name in ("aq", "ak"):
                chunk_landed(pe, name)
                columns(name + "0", w512(name), hT, (0, 1), T)
                columns(name + "1", w512(name), hT, (2, 3), T)
            chunk_landed(pe, "av")
            rows("av0", w512("av"), hT, (0,), 0, 512)
            rows("av1", w512("av"), hT, (1,), 0, 512)
            hT_ready(2)

            def scores(n):
                if n == 0:
                    for name in ("aq0", "aq1", "ak0", "ak1"):
                        job_evacuated(pe, name)
                if n == 4:
                    for name in ("bq0", "bq1", "kb0", "kb1"):
                        job_evacuated(pe, name)
                if n >= 2:
                    pe.wait_ge(s_read, n - 1)
                q, k = (aqT, akT) if n < 4 else (bqT, kbT)
                for h in range(2):
                    r, b = HD * h, 2 + 2 * (n % 2) + h
                    pe.matmul(ps[:, b, 0:P], q[r:r + HD, n % 4, 0:P], k[r:r + HD, n % 4, 0:P], start=True, stop=True)
                    m = pe.matmul(ps[:, b, P:3 * P], q[r:r + HD, n % 4, P:T], k[r:r + HD, n % 4, :],
                                  start=True, stop=True)
                m.then_inc(s_done, 1)

            def turn_probs(n):
                pe.wait_ge(prob_set, n + 1)
                if n >= 1:
                    pe.wait_ge(o_copied, n)
                for h in range(2):
                    if n >= 1:
                        pe.wait_ge((probT_copied_a, probT_copied_v)[h], n)
                    for c in range(3):
                        m = pe.transpose(ps[:, 6 + h, c * P:(c + 1) * P], logit[:, n % 2, h, c * P:(c + 1) * P], ident)
                    m.then_inc(probT_done, 1)

            def weigh(n):
                if n == 0:
                    job_evacuated(pe, "av0")
                    job_evacuated(pe, "av1")
                if n == 4:
                    job_evacuated(pe, "vb0")
                    job_evacuated(pe, "vb1")
                pe.wait_ge(probT_copied_a, n + 1)
                pe.wait_ge(probT_copied_v, n + 1)
                v = av if n < 4 else vb
                c0 = (n % 4) * P
                for h in range(2):
                    r = slice(HD * h, HD * h + HD)
                    vs = [v[:, s, c0 + HD * h:c0 + HD * h + HD] for s in range(2)]
                    pT = probT[:, n % 2, h, :]
                    pe.matmul(ps[r, 6, 3 * P:4 * P], vs[0], pT[:, 0:P], start=True, stop=True)
                    pe.matmul(ps[r, 7, 3 * P:4 * P], vs[0], pT[:, P:2 * P], start=True, stop=False)
                    m = pe.matmul(ps[r, 7, 3 * P:4 * P], vs[1], pT[:, 2 * P:3 * P], start=False, stop=True)
                m.then_inc(o_done, 1)

            def gate(branch, i):
                name = f"{branch}{i // 2}"
                if i % 2 == 0:
                    chunk_landed(pe, name)
                m = columns(f"{branch}{i}", w512(name), hT, (2 * (i % 2), 2 * (i % 2) + 1), T)

            def latent():
                job_evacuated(pe, "ckvT")
                chunk_landed(pe, "uk_uv")
                w = chunk("uk_uv")[:, 0:2048].rearrange("p (a k n) -> p a k n", a=2, k=2)
                columns("kb0", w[:, 0], ckvT, (0, 1), T)
                columns("kb1", w[:, 0], ckvT, (2, 3), T)
                rows("vb0", w[:, 1], ckvT, (0,), 0, 512)
                rows("vb1", w[:, 1], ckvT, (1,), 0, 512)
                chunk_landed(pe, "bq")
                columns("bq0", w512("bq"), hT, (0, 1), T)
                columns("bq1", w512("bq"), hT, (2, 3), T)

            def memory_kv():
                chunk_landed(pe, "kx_vx")
                w = chunk("kx_vx").rearrange("p (a k n) -> p a k n", a=2, k=KD)
                columns("km", w[:, 0], memT, (0, 1), MEM)
                rows("vm", w[:, 1], memT, (0, 1), 0, W_X)

            def branch_out(name, src):
                chunk_landed(pe, name)
                w = chunk(name).rearrange("p (k n) -> p k n", k=4)
                for i in range(4):
                    m = columns(f"{name}{i}", w, src, (2 * i, 2 * i + 1), T)

            for n in range(9):
                if n == 1:
                    memory_kv()
                    gate("ga", 0)
                    gate("ga", 1)
                if n == 2:
                    gate("ga", 2)
                    gate("ga", 3)
                    gate("gb", 0)
                    gate("gb", 1)
                if n == 3:
                    latent()
                if n == 5:
                    gate("gb", 2)
                    gate("gb", 3)
                if n == 7:
                    pe.wait_ge(o_copied, 4)
                    branch_out("oa", aqT)
                if n < 8:
                    scores(n)
                if n >= 1:
                    turn_probs(n - 1)
                    weigh(n - 1)
            pe.wait_ge(o_copied, 8)
            branch_out("ob", bqT)
            pe.wait_ge(merged_set, 4)
            for i in range(4):
                if i % 2 == 0:
                    chunk_landed(pe, f"out{i // 2}")
                m = rows(f"out{i}", w512(f"out{i // 2}"), merged, (i % 2,), 0, 512)

            pe.wait_ge(xn_set, 4)
            turn(xn, 2)
            hT_ready(3)
            chunk_landed(pe, "qx_ox")
            wq = chunk("qx_ox")[:, 0:2048].rearrange("p (k n) -> p k n", k=KD)
            wo = chunk("qx_ox")[:, 2048:4096].rearrange("p (k n) -> p k n", k=2)
            columns("qx", wq, hT, (0, 1), T)
            for name in ("qx", "km", "vm"):
                job_evacuated(pe, name)
            for h in range(X_HEADS):
                r = HD * (h % 2)
                for t in range(TT):
                    m = pe.matmul(ps[:, 2 + h, t * MEM:(t + 1) * MEM], qxT[r:r + HD, h // 2, t * P:(t + 1) * P],
                                  kmT[r:r + HD, h // 2, :], start=True, stop=True)
                m.then_inc(xs_done, 1)
            for h in range(X_HEADS):
                pe.wait_ge(xprob_set, h + 1)
                if h >= 2:
                    pe.wait_ge((xpT_copied_a, xpT_copied_v)[h % 2], 1)
                for j in range(2):
                    for t in range(TT):
                        m = pe.transpose(ps[:, 6 + h % 2, j * T + t * P:j * T + (t + 1) * P],
                                         xprob[:, h, t, j * P:(j + 1) * P], ident)
                m.then_inc(xpT_done, 1)
            for c in range(2):
                o = begin(f"ox{c}")
                pe.wait_ge(xpT_copied_a, c + 1)
                pe.wait_ge(xpT_copied_v, c + 1)
                for h in range(2):
                    for j in range(2):
                        m = pe.matmul(o[HD * h:HD * h + HD, 0:T], vm[:, j, c * P + HD * h:c * P + HD * h + HD],
                                      xprobT[:, 2 * c + h, j, :], start=(j == 0), stop=(j == 1))
                end(m, f"ox{c}")
            job_evacuated(pe, "ox0")
            job_evacuated(pe, "ox1")
            for i in range(4):
                m = rows(f"xo{i}", wo, oxT, (i % 2,), 512 * (i // 2), 512)

            pe.wait_ge(xn_set, 6)
            pe.wait_ge(xexp_set, X_HEADS)
            turn(xn, 3)
            hT_ready(4)
            pe.wait_ge(small_in, 16 * 4)
            rows("router", w_rt, hT, (0, 1), 0, GROUPS + EXPERTS)
            pe.wait_ge(routed, 1)
            o = begin("count")
            lt, one = const[:, K_LT:K_LT + P], const[:, K_ONE:K_ONE + P]
            chosen = rt[:, 8]
            pe.matmul(o[:, 0:EXPERTS], lt, chosen[:, 0, :], start=True, stop=True)
            pe.matmul(o[:, EXPERTS:2 * EXPERTS], lt, chosen[:, 1, :], start=True, stop=False)
            pe.matmul(o[:, EXPERTS:2 * EXPERTS], one, chosen[:, 0, :], start=False, stop=True)
            pe.matmul(o[:, 2 * EXPERTS:3 * EXPERTS], one, chosen[:, 0, :], start=True, stop=False)
            m = pe.matmul(o[:, 2 * EXPERTS:3 * EXPERTS], one, chosen[:, 1, :], start=False, stop=True)
            end(m, "count")

            pe.wait_ge(resid_set, 8)
            job_evacuated(pe, "count")
            for t in range(TT):
                for c in range(2):
                    pe.matmul(ps[:, 2 * t + c, :], ident, x_sb[:, t, 512 * c:512 * c + 512],
                              start=True, stop=True, skip_group_check=True)

            def expert_step(it):
                pe.wait_ge(sel_set, it + 1)
                pe.wait_ge(actT_copied, it + 1)
                pe.wait_ge(selwT_copied, it + 1)
                for k in range(KD):
                    for t in range(TT):
                        m = pe.matmul(ps[:, 6 + k // 4, (k % 4) * P:(k % 4 + 1) * P], xn[:, t, k * P:(k + 1) * P],
                                      sel[:, t], start=(t == 0), stop=(t == TT - 1))
                m.then_inc(xe_done, 1)
                pe.wait_ge(xe_copied, it + 1)
                for t in range(TT):
                    m = pe.transpose(ps[:, 7, t * P:(t + 1) * P], selw[:, t], ident)
                m.then_inc(selwT_done, 1)
                pe.wait_ge(y_copied_a, it + 1)
                pe.wait_ge(y_copied_v, it + 1)
                for q in range(8):
                    s, v = landed(FIRST_MOE + q)
                    pe.wait_ge(slot_in[s], it * (16 * MOE_CHUNKS // RING) + v)
                    w = ring[:, s, :].rearrange("p (e k n) -> p e k n", e=SHARE, k=2)
                    for kk in range(2):
                        k = 2 * (q // 2) + kk
                        for e in range(SHARE):
                            m = pe.matmul(ps[SLOTS * e:SLOTS * e + SLOTS, 4 + q % 2, :],
                                          xeT[:, k, SLOTS * e:SLOTS * e + SLOTS], w[:, e, kk, :],
                                          start=(k == 0), stop=(k == KD - 1), skip_group_check=True)
                    m.then_inc(chunk_used, 1)
                pe.wait_ge(act_set, it + 2)
                for f in range(FC):
                    m = pe.transpose(ps[:, 6, f * P:(f + 1) * P], act_sb[:, f * P:(f + 1) * P], ident)
                m.then_inc(actT_done, 1)
                pe.wait_ge(actT_copied, it + 2)
                for f in range(FC):
                    s, v = landed(FIRST_MOE + 8 + f)
                    pe.wait_ge(slot_in[s], it * (16 * MOE_CHUNKS // RING) + v)
                    w = ring[:, s, :].rearrange("p (e n) -> p e n", e=SHARE)
                    for c in range(2):
                        for e in range(SHARE):
                            m = pe.matmul(ps[SLOTS * e:SLOTS * e + SLOTS, 4 + c, :],
                                          actT[:, f, SLOTS * e:SLOTS * e + SLOTS], w[:, e, 512 * c:512 * c + 512],
                                          start=(f == 0), stop=(f == FC - 1), skip_group_check=True)
                    m.then_inc(chunk_used, 1)
                pe.wait_ge(y_copied_a, it + 2)
                pe.wait_ge(y_copied_v, it + 2)
                pe.wait_ge(selwT_copied, it + 2)
                for c in range(2):
                    for t in range(TT):
                        m = pe.matmul(ps[:, 2 * t + c, :], selwT[:, t * P:(t + 1) * P], y_sb[:, 512 * c:512 * c + 512],
                                      start=False, stop=True, skip_group_check=True)
                m.then_inc(added, 1)

            for signal in (added, actT_done, selwT_done):
                pe.sem_inc(signal, 1)
            pe.wait_ge(most_set, 1)
            fullest = pe.value_load(most_i[0:1, 0:1], min_val=0, max_val=T)
            with pe.Fori(0, ROUNDS) as r:
                with pe.If(fullest > r * SLOTS):
                    with pe.Fori(0, STEPS) as g:
                        expert_step(r * STEPS + g)
            pe.matmul(ps[0:1, 6, 0:1], ident[:, 0:1], ident[:, 0:1], start=True, stop=True).then_inc(moe_done, 1)

        @block.scalar
        def _(act):
            act.dma_start(const[:], consts).then_inc(const_in, 16)
            act.dma_start(gain[:, 0, :], norm_mix[0].rearrange("(p k) -> p k", k=KD)).then_inc(gain_in, 16)
            act.dma_start(rel_sb[:], rel_bias).then_inc(tab_in, 16)
            act.dma_start(one_hot, buckets).then_inc(tab_in, 16)
            act.dma_start(below_sb, below).then_inc(tab_in, 16)
            act.dma_start(w_ikw[:], w_in2.rearrange("(p k) n -> p k n", k=KD)[:, :, C_IK:C_GA]).then_inc(ikw_in, 16)
            act.dma_start(w_rt[:, :, 0:GROUPS], w_group[0].rearrange("(p k) n -> p k n", k=KD)).then_inc(small_in, 16)
            act.dma_start(w_rt[:, :, GROUPS:], w_router[0].rearrange("(p k) n -> p k n", k=KD)).then_inc(small_in, 16)
            act.dma_start(gain[:, 2, :], norm_x[0].rearrange("(p k) -> p k", k=KD)).then_inc(gain_in, 16)
            act.dma_start(gain[:, 3, :], norm_moe[0].rearrange("(p k) -> p k", k=KD)).then_inc(gain_in, 16)
            act.dma_start(gain_c[:], ckv_norm[0].rearrange("(p k) -> p k", k=2)).then_inc(gain_in, 16)
            with nc.allow_non_contiguous_dma(reason="a gain of 1024 numbers, once"):
                act.dma_start(gain[:, 1, :], mem_norm[0].rearrange("(k p) -> p k", p=P)).then_inc(gain_in, 16)
            act.dma_start(b_rt[:, 0:GROUPS], b_group.to_broadcast([P, GROUPS])).then_inc(small_in, 16)
            act.dma_start(b_rt[:, GROUPS:], b_router.to_broadcast([P, EXPERTS])).then_inc(small_in, 16)

            def square(src, n, t, junk, signal):
                return act.activation(junk, src, ACT.Square, accum_out=ssq[:, n, t:t + 1]).then_inc(signal, 1)

            def scaled(src, n, t):
                return act.activation(xn[:, t, :].rearrange("p (k q) -> p k q", k=KD),
                                      src.rearrange("p (q k) -> p k q", k=KD), ACT.Copy, scale=rstd[:, n, t:t + 1])

            def copy_turned(dst, n, g):
                for b in range(2):
                    act.wait_ge(turn_done, 4 * n + b + 1)
                    for k in range(2 * b, 2 * b + 2):
                        m = act.activation(dst[:, k, :], turned[:, k, :], ACT.Copy, scale=gain[:, g, k:k + 1])
                    m.then_inc(turn_copied_a, 1)

            def copy_job(name, dst, src=None):
                o = job_computed(act, name)
                evacuates(act.activation(dst, o if src is None else src(o), ACT.Copy), name)

            act.wait_ge(x_in, 16)
            square(x_sb[:, 0, :], 0, 0, xn[:, 0, :], squares)
            act.wait_ge(rstd_set, 1)
            scaled(x_sb[:, 0, :], 0, 0).then_inc(xn_set, 1)
            act.wait_ge(gain_in, 16 * 5)
            copy_turned(hT, 0, 0)
            act.wait_ge(mem_in, 16)
            square(mem_sb[:, 0, :], 1, 0, memT[:, 0:4, :].rearrange("p a b -> p (a b)"), squares)
            copy_job("iq", iqT[:].rearrange("p a b -> p (a b)"))
            act.wait_ge(idx_done, 1)
            act.activation(relu4, ps[:, 2:6, 0:3 * P], ACT.Relu).then_inc(relu_set, 1)
            act.wait_ge(rstd_set, 2)
            act.activation(mem_sb[:, 0, :], mem_sb[:, 0, :], ACT.Copy, scale=rstd[:, 1, 0:1]).then_inc(mem_scaled, 1)
            o = job_computed(act, "ckv")
            for t in range(TT):
                square(o[:, t * RANK:(t + 1) * RANK], 4, t, memT[:, 4 + t, :], csq_done)
            act.wait_ge(idx_done, 2)
            act.wait_ge(idx_added, 1)
            act.activation(relu4, ps[:, 2:6, 0:3 * P], ACT.Relu).then_inc(relu_set, 1)
            act.wait_ge(crstd_set, 1)
            for t in range(TT):
                m = act.activation(ckvn[:, t, :].rearrange("p (k q) -> p k q", k=2),
                                   o[:, t * RANK:(t + 1) * RANK].rearrange("p (q k) -> p k q", k=2),
                                   ACT.Copy, scale=rstd[:, 4, t:t + 1])
            evacuates(m, "ckv")
            copy_turned(memT, 1, 1)
            o = job_computed(act, "ckvT")
            for r in range(2):
                m = act.activation(ckvT[:, r, :], o[:, r * T:(r + 1) * T], ACT.Copy, scale=gain_c[:, r:r + 1])
            evacuates(m, "ckvT")

            def pair(buf, i):
                return buf[:, 2 * i:2 * i + 2, :].rearrange("p a b -> p (a b)")

            for name, buf in (("aq", aqT), ("ak", akT)):
                copy_job(name + "0", pair(buf, 0))
                copy_job(name + "1", pair(buf, 1))
            copy_job("av0", av[:, 0, :])
            copy_job("av1", av[:, 1, :])

            def exps(n):
                act.wait_ge(max_set, n + 1)
                for h in range(2):
                    for t in range(TT):
                        seg = slice(0, P) if t == 0 else slice(P, 3 * P)
                        j = 2 * h + t
                        m = act.activation(logit[:, n % 2, h, seg], logit[:, n % 2, h, seg], ACT.Exp,
                                           bias=nmax[:, n, j:j + 1], accum_out=esum[:, n, j:j + 1])
                m.then_inc(exp_set, 1)

            def copy_probT(n):
                act.wait_ge(probT_done, 2 * n + 1)
                if n >= 2:
                    act.wait_ge(o_done, n - 1)
                act.activation(probT[:, n % 2, 0, :], ps[:, 6, 0:3 * P], ACT.Copy).then_inc(probT_copied_a, 1)

            def copy_o(n):
                act.wait_ge(o_done, n + 1)
                dst = (aqT if n < 4 else bqT)[:, n % 4, :]
                act.activation(dst.rearrange("p (t c) -> p t c", t=TT), ps[:, 6:8, 3 * P:4 * P],
                               ACT.Copy).then_inc(o_copied, 1)

            def gate_job(branch, i):
                o = job_computed(act, f"{branch}{i}")
                buf = ga if branch == "ga" else gb
                m = act.activation(pair(buf, i), o, ACT.Tanh, scale=0.5)
                evacuates(m, f"{branch}{i}")

            def memory_kv():
                copy_job("km", kmT[:].rearrange("p a b -> p (a b)"))
                copy_job("vm", vm[:].rearrange("p a b -> p (a b)"))

            for n in range(9):
                if n == 1:
                    memory_kv()
                    gate_job("ga", 0)
                    gate_job("ga", 1)
                if n == 2:
                    gate_job("ga", 2)
                    gate_job("ga", 3)
                    gate_job("gb", 0)
                    gate_job("gb", 1)
                if n == 3:
                    copy_job("kb0", pair(kbT, 0))
                    copy_job("kb1", pair(kbT, 1))
                    copy_job("vb0", vb[:, 0, :])
                    copy_job("vb1", vb[:, 1, :])
                    copy_job("bq0", pair(bqT, 0))
                    copy_job("bq1", pair(bqT, 1))
                if n == 5:
                    gate_job("gb", 2)
                    gate_job("gb", 3)
                if n < 8:
                    exps(n)
                if n >= 1:
                    copy_probT(n - 1)
                    copy_o(n - 1)

            def renorm(n, quarters):
                act.wait_ge(resid_set, quarters)
                square(x_sb[:, 0, :], n, 0, xn[:, 0, :], squares)
                act.wait_ge(rstd_set, n + 1)
                scaled(x_sb[:, 0, :], n, 0).then_inc(xn_set, 1)
                copy_turned(hT, n, n)

            renorm(2, 4)
            copy_job("qx", qxT[:].rearrange("p a b -> p (a b)"))
            for h in range(X_HEADS):
                act.wait_ge(xmax_set, h + 1)
                for t in range(TT):
                    m = act.activation(xprob[:, h, t, :], ps[:, 2 + h, t * MEM:(t + 1) * MEM], ACT.Exp, scale=SCALE,
                                       bias=xnmax[:, h, t:t + 1], accum_out=xsum[:, h, t:t + 1])
                m.then_inc(xexp_set, 1)
            for h in (0, 2):
                act.wait_ge(xpT_done, h + 1)
                act.activation(xprobT[:, h].rearrange("p a b -> p (a b)"), ps[:, 6, :], ACT.Copy).then_inc(xpT_copied_a, 1)
            for c in range(2):
                copy_job(f"ox{c}", oxT[:].rearrange("p a b -> p (a b)")[:, c * T:(c + 1) * T], lambda o: o[:, 0:T])
            renorm(3, 8)
            act.wait_ge(rexp_asked, 1)
            act.activation(rs[:, 15, :], rs[:, 14, :], ACT.Exp)
            act.activation(rt[:, 13, :, 0:GROUPS], rt[:, 12, :, 0:GROUPS], ACT.Exp).then_inc(rexp_set, 1)

            def expert_step(it):
                act.wait_ge(selwT_done, it + 2)
                act.wait_ge(added, it + 1)
                act.activation(selwT, ps[:, 7, 0:T], ACT.Copy).then_inc(selwT_copied, 1)
                act.wait_ge(chunk_used, it * MOE_CHUNKS + 8)
                act.wait_ge(act_set, it + 1)
                act.activation(silu_sb, ps[:, 4, :].rearrange("p (q f) -> p f q", f=FC), ACT.Silu).then_inc(silu_set, 1)
                act.wait_ge(chunk_used, it * MOE_CHUNKS + MOE_CHUNKS)
                act.activation(y_sb[:, 0:512], ps[:, 4, :], ACT.Copy).then_inc(y_copied_a, 1)

            for signal in (selwT_copied, y_copied_a):
                act.sem_inc(signal, 1)
            act.wait_ge(most_set, 1)
            fullest = act.value_load(most_i[0:1, 0:1], min_val=0, max_val=T)
            with act.Fori(0, ROUNDS) as r:
                with act.If(fullest > r * SLOTS):
                    with act.Fori(0, STEPS) as g:
                        expert_step(r * STEPS + g)
            act.wait_ge(moe_done, 1)
            square(ps[:, 0:2, :], 5, 0, hT[:, 0:4, :].rearrange("p a b -> p (a b)").rearrange("p (a b) -> p a b", a=2), fsq)
            square(ps[:, 2:4, :], 5, 1, hT[:, 4:8, :].rearrange("p a b -> p (a b)").rearrange("p (a b) -> p a b", a=2), fsq)

        @block.vector
        def _(dve):
            steps = [0]

            def mark(ins):
                steps[0] += 1
                ins.then_inc(dve_step, 1)

            def then(ins):
                mark(ins)
                dve.wait_ge(dve_step, steps[0])

            def wait_marked():
                dve.wait_ge(dve_step, steps[0])

            def square(src, n, junk):
                dve.tensor_tensor_reduce(junk, src, src, 1.0, 0.0, ALU.mult, ALU.add,
                                         ssq[:, n, 1:2]).then_inc(squares, 1)

            def scaled(src, n):
                return dve.tensor_scalar(xn[:, 1, :].rearrange("p (k q) -> p k q", k=KD),
                                         src.rearrange("p (q k) -> p k q", k=KD), rstd[:, n, 1:2], None, ALU.mult)

            def copy_turned(dst, n, g):
                for b in range(2, 4):
                    dve.wait_ge(turn_done, 4 * n + b + 1)
                    gb_ = gain[:, g, 2 * b:2 * b + 2].unsqueeze(2).to_broadcast([P, 2, T])
                    dve.tensor_tensor(dst[:, 2 * b:2 * b + 2, :], turned[:, 2 * b:2 * b + 2, :], gb_,
                                      ALU.mult).then_inc(turn_copied_v, 1)

            dve.memset(half[:], -0.5).then_inc(half_set, 1)
            dve.wait_ge(x_in, 16)
            square(x_sb[:, 1, :], 0, xn[:, 1, :])
            dve.wait_ge(tab_in, 48)
            dve.wait_ge(biasrow_done, 1)
            dve.tensor_tensor(bias_rows, ps[0:2 * HEADS, 7, 0:3 * P], below_sb, ALU.add).then_inc(biasrow_set, 1)
            dve.wait_ge(rstd_set, 1)
            scaled(x_sb[:, 1, :], 0).then_inc(xn_set, 1)
            dve.wait_ge(gain_in, 16 * 5)
            copy_turned(hT, 0, 0)
            dve.wait_ge(mem_in, 16)
            square(mem_sb[:, 1, :], 1, memT[:, 4:8, :].rearrange("p a b -> p (a b)"))
            o = job_computed(dve, "ikw")
            dve.tensor_copy(ikT[:], o[:, 0:T])
            evacuates(dve.tensor_scalar(iw[:], o[:, T:T + 16].rearrange("p (t h) -> p t h", t=TT),
                                        IDX_HEADS ** -0.5 * IDX_DIM ** -0.5, None, ALU.mult), "ikw")
            dve.wait_ge(rstd_set, 2)
            dve.tensor_scalar(mem_sb[:, 1, :], mem_sb[:, 1, :], rstd[:, 1, 1:2], None, ALU.mult).then_inc(mem_scaled, 1)
            dve.wait_ge(const_in, 16)
            job_evacuated(dve, "ikw")
            for b in range(2):
                dve.wait_ge(relu_set, b + 1)
                for h in range(4):
                    if b + h:
                        wait_marked()
                    for t in range(TT):
                        seg = slice(0, P) if t == 0 else slice(P, 3 * P)
                        first = const[:, K_CAUSAL:K_CAUSAL + 3 * P][:, seg]
                        m = dve.scalar_tensor_tensor(score[:, seg], relu4[:, h, seg], iw[:, t, 4 * b + h:4 * b + h + 1],
                                                     first if b + h == 0 else score[:, seg], ALU.mult, ALU.add)
                    if h < 3 or b == 1:
                        mark(m)
                    else:
                        m.then_inc(idx_added, 1)
                        dve.wait_ge(idx_added, 1)
            wait_marked()
            copy_turned(memT, 1, 1)
            segs = (slice(0, P), slice(P, 3 * P))
            for _ in range(TOPK // 8):
                for t in range(TT):
                    m = dve.max(top8[:, t, :], score[:, segs[t]])
                mark(m)
                wait_marked()
                for t in range(TT):
                    m = dve.match_replace(score[:, segs[t]], top8[:, t, :], score[:, segs[t]], TAKEN)
                mark(m)
                wait_marked()
            then(dve.tensor_scalar(unpicked[:], score[:], TAKEN / 2, NEG, ALU.is_gt, ALU.mult))

            def logits(n):
                if n == 0:
                    dve.wait_ge(bias_in, 16)
                dve.wait_ge(s_done, n + 1)
                if n >= 2:
                    dve.wait_ge(probT_done, 2 * (n - 1))
                b0 = 2 + 2 * (n % 2)
                buf = logit[:, n % 2]
                dve.scalar_tensor_tensor(buf[:, :, P:3 * P], ps[:, b0:b0 + 2, P:3 * P], SCALE,
                                         bias[:, 2 * n:2 * n + 2, :], ALU.mult, ALU.add)
                dve.scalar_tensor_tensor(buf[:, :, 0:P], ps[:, b0:b0 + 2, 0:P], SCALE,
                                         bias[:, 2 * n:2 * n + 2, P:T], ALU.mult, ALU.add).then_inc(s_read, 1)
                dve.wait_ge(s_read, n + 1)
                if n >= 4:
                    then(dve.tensor_tensor(buf, buf, unpicked[:].unsqueeze(1).to_broadcast([P, 2, 3 * P]), ALU.add))
                dve.tensor_reduce(nmax[:, n, 0:4:2], buf[:, :, 0:P], AX_X, ALU.max, negate=True)
                dve.tensor_reduce(nmax[:, n, 1:4:2], buf[:, :, P:3 * P], AX_X, ALU.max, negate=True).then_inc(max_set, 1)

            def normalise(n):
                dve.wait_ge(exp_set, n + 1)
                then(dve.reciprocal(erec[:, n, :], esum[:, n, :]))
                for h in range(2):
                    for t in range(TT):
                        m = dve.tensor_scalar(logit[:, n % 2, h, segs[t]], logit[:, n % 2, h, segs[t]],
                                              erec[:, n, 2 * h + t:2 * h + t + 1], None, ALU.mult)
                m.then_inc(prob_set, 1)

            def copy_probT(n):
                dve.wait_ge(probT_done, 2 * n + 2)
                if n >= 2:
                    dve.wait_ge(o_done, n - 1)
                dve.tensor_copy(probT[:, n % 2, 1, :], ps[:, 7, 0:3 * P]).then_inc(probT_copied_v, 1)

            def finish_gates(buf, branch):
                job_evacuated(dve, f"{branch}2")
                job_evacuated(dve, f"{branch}3")
                dve.tensor_scalar(buf[:], buf[:], 0.5, 0.5, ALU.mult, ALU.add).then_inc(gates_set, 1)

            for n in range(9):
                if n == 3:
                    finish_gates(ga, "ga")
                if n == 6:
                    finish_gates(gb, "gb")
                if n == 7:
                    dve.wait_ge(gates_set, 2)
                    for i in range(4):
                        o = job_computed(dve, f"oa{i}")
                        evacuates(dve.tensor_tensor(merged[:, 2 * i:2 * i + 2, :].rearrange("p a b -> p (a b)"), o,
                                                    ga[:, 2 * i:2 * i + 2, :].rearrange("p a b -> p (a b)"), ALU.mult), f"oa{i}")
                if n < 8:
                    logits(n)
                    normalise(n)
                if n >= 1:
                    copy_probT(n - 1)
            for i in range(4):
                part = gb[:, 2 * i:2 * i + 2, :].rearrange("p a b -> p (a b)")
                o = job_computed(dve, f"ob{i}")
                evacuates(dve.tensor_tensor(part, o, part, ALU.mult), f"ob{i}")
                job_evacuated(dve, f"ob{i}")
                job_evacuated(dve, f"oa{i}")
                m_ = merged[:, 2 * i:2 * i + 2, :].rearrange("p a b -> p (a b)")
                dve.tensor_tensor(m_, m_, part, ALU.add).then_inc(merged_set, 1)

            def add_residual(stem):
                for i in range(4):
                    o = job_computed(dve, f"{stem}{i}")
                    part = x_sb[:, i % 2, 512 * (i // 2):512 * (i // 2) + 512]
                    ins = dve.tensor_tensor(part, o, part, ALU.add)
                    evacuates(ins, f"{stem}{i}")
                    dve.wait_ge(proj_free[job(f"{stem}{i}")[0]], job(f"{stem}{i}")[1])
                    dve.sem_inc(resid_set, 1)

            def renorm(n):
                square(x_sb[:, 1, :], n, xn[:, 1, :])
                dve.wait_ge(rstd_set, n + 1)
                scaled(x_sb[:, 1, :], n).then_inc(xn_set, 1)
                copy_turned(hT, n, n)

            add_residual("out")
            renorm(2)
            for h in range(X_HEADS):
                dve.wait_ge(xs_done, h + 1)
                then(dve.tensor_reduce(xnmax[:, h, :], ps[:, 2 + h, :].rearrange("p (t m) -> p t m", t=TT), AX_X,
                                       ALU.max, negate=True))
                dve.tensor_scalar(xnmax[:, h, :], xnmax[:, h, :], SCALE, None, ALU.mult).then_inc(xmax_set, 1)
            for h in range(X_HEADS):
                dve.wait_ge(xexp_set, h + 1)
                then(dve.reciprocal(xrec[:, h, :], xsum[:, h, :]))
                for t in range(TT):
                    m = dve.tensor_scalar(xprob[:, h, t, :], xprob[:, h, t, :], xrec[:, h, t:t + 1], None, ALU.mult)
                m.then_inc(xprob_set, 1)
                if h % 2:
                    dve.wait_ge(xpT_done, h + 1)
                    dve.tensor_copy(xprobT[:, h].rearrange("p a b -> p (a b)"), ps[:, 7, :]).then_inc(xpT_copied_v, 1)
            add_residual("xo")
            renorm(3)

            def wide(s):
                return rs[:, s, :].unsqueeze(2).to_broadcast([P, TT, EXPERTS])

            o = job_computed(dve, "router")
            dve.wait_ge(small_in, 16 * 4)
            n_rt = GROUPS + EXPERTS
            evacuates(dve.tensor_tensor(rl[:], o[:, 0:TT * n_rt].rearrange("p (t n) -> p t n", t=TT),
                                        b_rt[:].unsqueeze(1).to_broadcast([P, TT, n_rt]), ALU.add), "router")
            job_evacuated(dve, "router")
            group = rl[:, :, 0:GROUPS]
            gwide = lambda s: rs[:, s, :].unsqueeze(2).to_broadcast([P, TT, GROUPS])
            fall4 = const[:, K_DESC:K_DESC + GROUPS].unsqueeze(1).to_broadcast([P, TT, GROUPS])
            fall = const[:, K_DESC:K_DESC + EXPERTS].unsqueeze(1).to_broadcast([P, TT, EXPERTS])
            then(dve.tensor_reduce(rs[:, 0, :], group, AX_X, ALU.max))
            dve.tensor_tensor(rt[:, 12, :, 0:GROUPS], group, gwide(0), ALU.subtract)
            then(dve.tensor_tensor(rt[:, 0, :, 0:GROUPS], group, gwide(0), ALU.is_equal))
            then(dve.tensor_tensor(rt[:, 1, :, 0:GROUPS], rt[:, 0, :, 0:GROUPS], fall4, ALU.mult))
            then(dve.tensor_reduce(rs[:, 1, :], rt[:, 1, :, 0:GROUPS], AX_X, ALU.max))
            then(dve.tensor_tensor(rt[:, 0, :, 0:GROUPS], rt[:, 1, :, 0:GROUPS], gwide(1), ALU.is_equal))
            then(dve.tensor_scalar(rt[:, 1, :, 0:GROUPS], rt[:, 0, :, 0:GROUPS], 1.0, -NEG, ALU.subtract, ALU.mult))
            em = rt[:, 2]
            then(dve.tensor_tensor(em.rearrange("p t (g e) -> p t g e", g=GROUPS),
                                   rl[:, :, GROUPS:].rearrange("p t (g e) -> p t g e", g=GROUPS),
                                   rt[:, 1, :, 0:GROUPS].unsqueeze(3).to_broadcast([P, TT, GROUPS, PER_GROUP]), ALU.add))
            for i, src in ((0, rt[:, 2]), (1, rt[:, 3])):
                then(dve.tensor_reduce(rs[:, 2 + i, :], src, AX_X, ALU.max))
                then(dve.tensor_tensor(rt[:, 4], src, wide(2 + i), ALU.is_equal))
                then(dve.tensor_tensor(rt[:, 4], rt[:, 4], fall, ALU.mult))
                then(dve.tensor_reduce(rs[:, 4, :], rt[:, 4], AX_X, ALU.max))
                then(dve.tensor_tensor(rt[:, 6 + i], rt[:, 4], wide(4), ALU.is_equal))
                if i == 0:
                    then(dve.scalar_tensor_tensor(rt[:, 3], rt[:, 6], 2 * NEG, rt[:, 2], ALU.mult, ALU.add))
            dve.tensor_tensor(rt[:, 8], rt[:, 6], rt[:, 7], ALU.add).then_inc(routed, 1)
            dve.tensor_tensor(rs[:, 14, :], rs[:, 3, :], rs[:, 2, :], ALU.subtract).then_inc(rexp_asked, 1)
            o = job_computed(dve, "count")
            then(dve.tensor_reduce(most[:], o[:, 2 * EXPERTS:3 * EXPERTS], AX_X, ALU.max))
            dve.tensor_copy(most_i[:], most[:]).then_inc(most_set, 1)
            dve.wait_ge(routed, 1)
            then(dve.scalar_tensor_tensor(rt[:, 9], o[:, 0:2 * EXPERTS].rearrange("p (t e) -> p t e", t=TT), 1.0, rt[:, 8],
                                          ALU.add, ALU.mult))
            place = rt[:, 10]
            evacuates(dve.tensor_scalar(place, rt[:, 9], -1.0, None, ALU.add), "count")
            dve.wait_ge(rexp_set, 1)
            then(dve.tensor_reduce(rs[:, 5, :], rt[:, 13, :, 0:GROUPS], AX_X, ALU.add))
            then(dve.reciprocal(rs[:, 6, :], rs[:, 5, :]))
            then(dve.tensor_scalar(rs[:, 7, :], rs[:, 15, :], 1.0, None, ALU.add))
            then(dve.reciprocal(rs[:, 8, :], rs[:, 7, :]))
            then(dve.tensor_tensor(rs[:, 9, :], rs[:, 15, :], rs[:, 8, :], ALU.mult))
            then(dve.tensor_tensor(rs[:, 10, :], rs[:, 8, :], rs[:, 6, :], ALU.mult))
            then(dve.tensor_tensor(rs[:, 11, :], rs[:, 9, :], rs[:, 6, :], ALU.mult))
            then(dve.tensor_tensor(rt[:, 4], rt[:, 6], wide(10), ALU.mult))
            then(dve.tensor_tensor(rt[:, 5], rt[:, 7], wide(11), ALU.mult))
            weight = rt[:, 11]
            then(dve.tensor_tensor(weight, rt[:, 4], rt[:, 5], ALU.add))
            job_evacuated(dve, "count")

            slots = const[:, K_SLOT:K_SLOT + SLOTS].unsqueeze(1).unsqueeze(1).to_broadcast([P, TT, SHARE, SLOTS])

            def expert_step(it, expert, r):
                e0 = dve.snap(expert)
                dve.wait_ge(moved, r + 1)
                dve.wait_ge(selwT_done, it + 1)
                dve.tensor_tensor(sel, place[:, :, bass.ds(e0, SHARE)].unsqueeze(3).to_broadcast([P, TT, SHARE, SLOTS]),
                                  slots, ALU.is_equal).then_inc(sel_made, 1)
                dve.wait_ge(sel_made, it + 1)
                dve.tensor_tensor(selw, sel, weight[:, :, bass.ds(e0, SHARE)].unsqueeze(3).to_broadcast(
                    [P, TT, SHARE, SLOTS]), ALU.mult).then_inc(sel_set, 1)
                dve.wait_ge(xe_done, it + 1)
                for b in range(2):
                    m = dve.tensor_tensor(xeT[:, 4 * b:4 * b + 4, :], ps[:, 6 + b, :].rearrange("p (k s) -> p k s", k=4),
                                          gain[:, 3, 4 * b:4 * b + 4].unsqueeze(2).to_broadcast([P, 4, P]), ALU.mult)
                m.then_inc(xe_copied, 1)
                dve.wait_ge(silu_set, it + 1)
                dve.wait_ge(actT_done, it + 1)
                dve.tensor_tensor(act_sb, ps[:, 5, :].rearrange("p (q f) -> p f q", f=FC),
                                  silu_sb.rearrange("p (f q) -> p f q", f=FC), ALU.mult).then_inc(act_set, 1)
                dve.wait_ge(actT_done, it + 2)
                dve.tensor_copy(actT.rearrange("p f s -> p (f s)"), ps[:, 6, :]).then_inc(actT_copied, 1)
                dve.wait_ge(chunk_used, it * MOE_CHUNKS + MOE_CHUNKS)
                dve.wait_ge(added, it + 1)
                dve.tensor_copy(y_sb[:, 512:1024], ps[:, 5, :]).then_inc(y_copied_v, 1)

            for signal in (actT_copied, y_copied_v, act_set, moved):
                dve.sem_inc(signal, 1)
            dve.wait_ge(most_set, 1)
            fullest = dve.value_load(most_i[0:1, 0:1], min_val=0, max_val=T)
            with dve.Fori(0, ROUNDS) as r:
                with dve.If(fullest > r * SLOTS):
                    with dve.Fori(0, STEPS) as g:
                        expert_step(r * STEPS + g, g * SHARE, r)
                    dve.tensor_scalar(place, place, -float(SLOTS), None, ALU.add).then_inc(moved, 1)

            dve.wait_ge(fgain_in, 16)
            dve.wait_ge(moe_done, 1)
            dve.wait_ge(frstd_set, 1)
            for t in range(TT):
                dve.scalar_tensor_tensor(xn[:, t, :].rearrange("p (c n) -> p c n", c=2), ps[:, 2 * t:2 * t + 2, :],
                                         rstd[:, 5, t:t + 1], fgain.rearrange("p (c n) -> p c n", c=2),
                                         ALU.mult, ALU.mult).then_inc(out_set, 1)

        @block.gpsimd
        def _(pool):
            steps = [0]

            def inverse_rms(n, width, signal):
                steps[0] += 1
                pool.tensor_scalar(var[:, n, :], ssq[:, n, :], 1.0 / width, EPS, ALU.mult, ALU.add).then_inc(pool_step, 1)
                pool.wait_ge(pool_step, steps[0])
                pool.tensor_tensor(rstd[:, n, :], var[:, n, :], half[:], ALU.pow).then_inc(signal, 1)

            pool.wait_ge(half_set, 1)
            pool.wait_ge(squares, 2)
            inverse_rms(0, D, rstd_set)
            pool.wait_ge(squares, 4)
            inverse_rms(1, D, rstd_set)
            pool.wait_ge(csq_done, 2)
            inverse_rms(4, RANK, crstd_set)
            for n in (2, 3):
                pool.wait_ge(squares, 2 * n + 2)
                inverse_rms(n, D, rstd_set)
            pool.wait_ge(fsq, 2)
            inverse_rms(5, D, frstd_set)


NAMES = ["x", "mem", "rel_bias", "final_norm", "norm_mix", "w_in", "ckv_norm", "w_uk", "w_uv", "w_oa", "w_ob",
         "w_out", "norm_x", "mem_norm", "wq_x", "wk_x", "wv_x", "wo_x", "norm_moe", "w_group", "b_group",
         "w_router", "b_router", "w1", "w3", "w2"]


def kernel(**inputs):
    import concourse.bacc as bacc
    from concourse.bass_utils import run_bass_kernel_spmd

    nc = bacc.Bacc("TRN2", target_bir_lowering=False, num_devices=1)
    arrays = {name: np.ascontiguousarray(inputs[name]) for name in NAMES}
    arrays["consts"], arrays["buckets"], arrays["below"] = shape_constants()
    args = [nc.dram_tensor(f"in_{n}", a.shape, mybir.dt.from_np(a.dtype), kind="ExternalInput").ap()
            for n, a in arrays.items()]
    out = nc.dram_tensor("out", (1, T, D), F32, kind="ExternalOutput").ap()
    decoder_layer(nc, *args, out)
    r = run_bass_kernel_spmd(nc, [{f"in_{n}": a for n, a in arrays.items()}], core_ids=[0])
    return r.results[0]["out"]
```

```python
import math
from contextlib import ExitStack

import numpy as np

import concourse.bass as bass
from concourse import mybir

ALU = mybir.AluOpType
ACT = mybir.ActivationFunctionType
AX_X = mybir.AxisListType.X
F32 = mybir.dt.float32
I32 = mybir.dt.int32

P = 128
T, D = 256, 1024
TT = T // P
KD = D // P
HEADS, HD = 8, 64
W_HEADS = HEADS * HD
RANK = 256
IDX_HEADS, IDX_DIM = 8, 32
TOPK = min(256, T // 4)
BUCKETS, MAX_DIST = 32, 128
MEM, X_HEADS = 256, 4
W_X = X_HEADS * HD
GROUPS, PER_GROUP = 4, 8
EXPERTS = GROUPS * PER_GROUP
D_E = 512
FC = D_E // P
EPS = 1e-6
NEG = -1e30
TAKEN = -3e38
SCALE = HD ** -0.5

C_AQ, C_AK, C_AV, C_BQ = (i * W_HEADS for i in range(4))
C_CKV = 4 * W_HEADS
C_IQ = C_CKV + RANK
C_IK = C_IQ + IDX_HEADS * IDX_DIM
C_GA = C_IK + IDX_DIM + IDX_HEADS
C_GB = C_GA + D

SLOTS = 32
SHARE = P // SLOTS
STEPS = EXPERTS // SHARE
ROUNDS = T // SLOTS

RING = 6
MOE_SLOTS = [4, 5, 6, 7, 0, 1, 2, 3]
MOE_RING = len(MOE_SLOTS)
SLOT = 4096
MOE_CHUNKS = 12
UNROLL = 2
TURNS = STEPS // UNROLL
TURN_CHUNKS = UNROLL * MOE_CHUNKS
assert TURN_CHUNKS % MOE_RING == 0

K_ID, K_LT, K_ONE, K_CAUSAL = 0, P, 2 * P, 3 * P
K_SLOT = K_CAUSAL + 3 * P
K_DESC = K_SLOT + SLOTS
K_N = K_DESC + EXPERTS


def shape_constants():
    c = np.zeros((P, K_N), np.float32)
    p = np.arange(P)[:, None]
    i = np.arange(P)[None, :]
    c[:, K_ID:K_ID + P] = p == i
    c[:, K_LT:K_LT + P] = p < i
    c[:, K_ONE:K_ONE + P] = 1.0
    c[:, K_CAUSAL:K_CAUSAL + P] = np.where(i > p, NEG, 0.0)
    c[:, K_CAUSAL + P:K_CAUSAL + 3 * P] = np.where(np.arange(T)[None, :] > p + P, NEG, 0.0)
    c[:, K_SLOT:K_SLOT + SLOTS] = np.arange(SLOTS)
    c[:, K_DESC:K_DESC + EXPERTS] = EXPERTS - np.arange(EXPERTS)
    dist = T - 1 - np.arange(T + P)
    exact = BUCKETS // 2
    b = np.zeros((BUCKETS, T + P), np.float32)
    for m, n in enumerate(dist):
        if n < 0:
            continue
        if n >= exact:
            n = min(exact + int(math.log(n / exact) / math.log(MAX_DIST / exact) * (BUCKETS - exact)), BUCKETS - 1)
        b[n, m] = 1.0
    below = np.broadcast_to(np.where(dist < 0, NEG, 0.0).astype(np.float32), (2 * HEADS, T + P))
    return c, b, np.ascontiguousarray(below)


JOBS = (["iq", "ikw", "ckv", "ckvT", "aq0", "aq1", "ak0", "ak1", "av0", "av1", "km", "vm"]
        + [f"ga{i}" for i in range(4)]
        + ["kb0", "kb1", "vb0", "vb1", "bq0", "bq1"]
        + [f"gb{i}" for i in range(4)]
        + [f"oa{i}" for i in range(4)] + [f"ob{i}" for i in range(4)]
        + [f"out{i}" for i in range(4)] + ["qx", "ox0", "ox1"] + [f"xo{i}" for i in range(4)]
        + ["router", "count"])

CHUNKS = ["ckv_iq", "aq", "ak", "av", "kx_vx", "ga0", "ga1", "uk_uv", "bq", "gb0", "gb1",
          "oa", "ob", "out0", "out1", "qx_ox"]
LAST_JOB = {"ckv_iq": "ckv", "aq": "aq1", "ak": "ak1", "av": "av1", "kx_vx": "vm", "ga0": "ga1", "ga1": "ga3",
            "uk_uv": "vb1", "bq": "bq1", "gb0": "gb1", "gb1": "gb3", "oa": "oa3", "ob": "ob3", "out0": "out2",
            "out1": "out3", "qx_ox": "xo3"}
PARTS = {"uk_uv": 2, "kx_vx": 2, "qx_ox": 2, "ckv_iq": 2}
assert (len(CHUNKS) - 1) % RING == MOE_SLOTS[-1]


def landed(name):
    c = CHUNKS.index(name)
    return c % RING, 16 * sum(PARTS.get(CHUNKS[i], 1) for i in range(c % RING, c + 1, RING))


def moe_landed(q):
    s = MOE_SLOTS[q % MOE_RING]
    own = sum(PARTS.get(CHUNKS[i], 1) for i in range(s, len(CHUNKS), RING)) if s < RING else 0
    return s, 16 * (own + q // MOE_RING + 1)


MOE_LANDED = 16 * TURN_CHUNKS // MOE_RING


def decoder_layer(nc, x, mem, rel_bias, final_norm, norm_mix, w_in, ckv_norm, w_uk, w_uv, w_oa, w_ob,
                  w_out, norm_x, mem_norm, wq_x, wk_x, wv_x, wo_x, norm_moe, w_group, b_group,
                  w_router, b_router, w1, w3, w2, consts, buckets, below, out):
    with ExitStack() as ctx:
        def sb(name, shape, dt=F32):
            return ctx.enter_context(nc.sbuf_tensor(name, shape, dt))

        def sem(name):
            return ctx.enter_context(nc.semaphore(name))

        slots_own = sb("slots_own", [P, RING, SLOT])
        attn_data = sb("attn_data", [P, 2, SLOT])
        ring = [slots_own[:, i, :] for i in range(RING)] + [attn_data[:, i, :] for i in range(2)]
        x_sb = sb("x_sb", [P, TT, D])
        xn = sb("xn", [P, TT, D])
        hT = sb("hT", [P, KD, T])
        ga = sb("ga", [P, KD, T])
        gb = sb("gb", [P, KD, T])
        bias = attn_data[:, 0, :].rearrange("p (h c) -> p h c", h=2 * HEADS)
        aqT, akT, kbT = (attn_data[:, 1, i * 1024:(i + 1) * 1024].rearrange("p (a b) -> p a b", a=4) for i in range(3))
        av = attn_data[:, 1, 3072:4096].rearrange("p (a b) -> p a b", a=TT)
        bqT = sb("bqT", [P, 4, T])
        vb = sb("vb", [P, TT, W_HEADS])
        iqT = sb("iqT", [P, 2, T])
        ikT = sb("ikT", [P, T])
        iw = sb("iw", [P, TT, IDX_HEADS])
        ckvn = sb("ckvn", [P, TT, RANK])
        memory_kv_data = sb("memory_kv_data", [P, D])
        kmT = memory_kv_data[:, 0:512].rearrange("p (a b) -> p a b", a=2)
        vm = memory_kv_data[:, 512:1024].rearrange("p (a b) -> p a b", a=2)
        score = sb("score", [P, 3 * P])
        logit = sb("logit", [P, 2, 2, 3 * P])
        probT = sb("probT", [P, 2, 2, 3 * P])
        const = sb("const", [P, K_N])
        w_ikw = sb("w_ikw", [P, KD, IDX_DIM + IDX_HEADS])
        w_rt = sb("w_rt", [P, KD, GROUPS + EXPERTS])
        b_rt = sb("b_rt", [P, GROUPS + EXPERTS])
        gain = sb("gain", [P, 4, KD])
        gain_c = sb("gain_c", [P, 2])
        rel_sb = sb("rel_sb", [BUCKETS, 2 * HEADS])
        half = sb("half", [P, 2])
        ssq = sb("ssq", [P, 6, 2])
        var = sb("var", [P, 6, 2])
        rstd = sb("rstd", [P, 6, 2])
        top8 = sb("top8", [P, 2, 8])
        nmax = sb("nmax", [P, 8, 4])
        esum = sb("esum", [P, 8, 4])
        erec = sb("erec", [P, 8, 4])
        xnmax = sb("xnmax", [P, X_HEADS, 2])
        xsum = sb("xsum", [P, X_HEADS, 2])
        xrec = sb("xrec", [P, X_HEADS, 2])
        rs = sb("rs", [P, 16, TT])
        rl = sb("rl", [P, TT, GROUPS + EXPERTS])
        most = sb("most", [P, 1])
        most_i = sb("most_i", [P, 1], I32)
        mem_sb = ga[:].rearrange("p a b -> p (a b)").rearrange("p (t d) -> p t d", t=TT)
        memT = gb
        relu = xn
        relu4 = relu[:].rearrange("p a b -> p (a b)")[:, 0:4 * 3 * P].rearrange("p (h c) -> p h c", h=4)
        bias_rows = probT[0:2 * HEADS, 0, 0, :]
        one_hot = probT[0:BUCKETS, 1, 0, :]
        below_sb = probT[0:2 * HEADS, 1, 1, :]
        ckvT = iqT
        qxT = iqT
        unpicked = score
        oxT = ckvn
        merged = hT
        def flat(buf):
            return buf.rearrange("p a b -> p (a b)")

        xprob = flat(ga[:]).rearrange("p (h t m) -> p h t m", h=X_HEADS, t=TT)
        xprobT = flat(gb[:]).rearrange("p (h m t) -> p h m t", h=X_HEADS, m=2)
        rt = flat(gb[:])[:, 0:14 * TT * EXPERTS].rearrange(
            "p (n t e) -> p n t e", n=14, t=TT)
        fgain = memory_kv_data[:]
        xeT = flat(hT[:, 0:4]).rearrange("p (k s) -> p k s", k=KD)
        y_sb = flat(hT[:, 4:8])
        silu_sb = flat(bqT[:])[:, 0:D_E]
        act_sb = flat(bqT[:])[:, D_E:2 * D_E]
        actT = flat(vb[:])[:, 0:D_E].rearrange("p (f s) -> p f s", f=FC)
        selwT = flat(vb[:])[:, D_E:D_E + T]
        sel = iqT[:, 0].rearrange("p (t e s) -> p t e s", t=TT, e=SHARE)
        selw = iqT[:, 1].rearrange("p (t e s) -> p t e s", t=TT, e=SHARE)
        ident = const[:, K_ID:K_ID + P]

        ps = ctx.enter_context(nc.psum_tensor("ps", [P, 8, 512], F32))
        turned = ps[:, 2:6, :].rearrange("p b (k t) -> p (b k) t", k=2)

        bias_dram = nc.dram_tensor("bias_rows_dram", [2 * HEADS, T + P], F32).ap()
        bias_rep = nc.dram_tensor("bias_rep_dram", [2 * HEADS, P, T + P], F32).ap()

        mem_in, const_in, gain_in = sem("mem_in"), sem("const_in"), sem("gain_in")
        x_in = [sem(f"x_in{t}") for t in range(TT)]
        gain0_in = sem("gain0_in")
        small_in, tab_in, bias_out, bias_repeated, bias_in, fgain_in = (
            sem("small_in"), sem("tab_in"), sem("bias_out"), sem("bias_repeated"), sem("bias_in"), sem("fgain_in"))
        slot_in = [sem(f"slot_in{i}") for i in range(MOE_RING)]
        chunk_used = sem("chunk_used")
        half_set = sem("half_set")
        squares = [sem(f"squares{t}") for t in range(TT)]
        rstd_set = [sem(f"rstd_set{t}") for t in range(TT)]
        xn_set = [sem(f"xn_set{t}") for t in range(TT)]
        mem_scaled = [sem(f"mem_scaled{t}") for t in range(TT)]
        turn_done = sem("turn_done")
        turn_copied_a, turn_copied_v = sem("turn_copied_a"), sem("turn_copied_v")
        biasrow_done, biasrow_set = sem("biasrow_done"), sem("biasrow_set")
        proj_done = [sem(f"proj_done{i}") for i in range(2)]
        proj_free = [sem(f"proj_free{i}") for i in range(2)]
        idx_done, relu_set, idx_added = sem("idx_done"), sem("relu_set"), sem("idx_added")
        csq_done, crstd_set = sem("csq_done"), sem("crstd_set")
        s_done, s_read, max_set, exp_set, prob_set = (
            sem("s_done"), sem("s_read"), sem("max_set"), sem("exp_set"), sem("prob_set"))
        probT_done, probT_copied_a, probT_copied_v = (
            sem("probT_done"), sem("probT_copied_a"), sem("probT_copied_v"))
        o_done, o_copied = sem("o_done"), sem("o_copied")
        gates_set = sem("gates_set")
        merged_set = sem("merged_set")
        resid_set = sem("resid_set")
        xs_done, xmax_set, xexp_set, xprob_set = (
            sem("xs_done"), sem("xmax_set"), sem("xexp_set"), sem("xprob_set"))
        xpT_done, xpT_copied_a, xpT_copied_v = sem("xpT_done"), sem("xpT_copied_a"), sem("xpT_copied_v")
        rexp_asked, rexp_set = sem("rexp_asked"), sem("rexp_set")
        routed, placed, most_set = sem("routed"), sem("placed"), sem("most_set")
        sel_set, xe_done, xe_copied, selwT_done, selwT_copied = (
            sem("sel_set"), sem("xe_done"), sem("xe_copied"), sem("selwT_done"), sem("selwT_copied"))
        silu_set, act_set, actT_done, actT_copied = (
            sem("silu_set"), sem("act_set"), sem("actT_done"), sem("actT_copied"))
        y_copied_a, y_copied_v, added = (
            sem("y_copied_a"), sem("y_copied_v"), sem("added"))
        moe_done, fsq, frstd_set, out_set, out_written = (
            sem("moe_done"), sem("fsq"), sem("frstd_set"), sem("out_set"), sem("out_written"))
        dve_step, pool_step = sem("dve_step"), sem("pool_step")
        sel_made, moved = sem("sel_made"), sem("moved")
        ikw_in = sem("ikw_in")
        chunk_asked = sem("chunk_asked")

        def job(name):
            j = JOBS.index(name)
            return j % 2, j // 2 + 1

        def job_computed(eng, name):
            b, n = job(name)
            eng.wait_ge(proj_done[b], n)
            return ps[:, b, :]

        def job_evacuated(eng, name):
            b, n = job(name)
            eng.wait_ge(proj_free[b], n)

        def evacuates(ins, name):
            ins.then_inc(proj_free[job(name)[0]], 1)

        def chunk(name):
            return ring[CHUNKS.index(name) % RING]

        def chunk_landed(eng, name):
            s, v = landed(name)
            eng.wait_ge(slot_in[s], v)

        w_in2, w_out2 = w_in[0], w_out[0]
        block = ctx.enter_context(nc.Block())

        @block.sync
        def _(sp):
            def cols(c0, n):
                return w_in2.rearrange("(p k) n -> p k n", k=KD)[:, :, c0:c0 + n]

            def fill(name, parts):
                c = CHUNKS.index(name)
                if c >= RING:
                    job_computed(sp, LAST_JOB[CHUNKS[c - RING]])
                at = 0
                for src in parts:
                    n = src.shape[1] * src.shape[2]
                    dst = chunk(name)[:, at:at + n].rearrange("p (k n) -> p k n", n=src.shape[2])
                    sp.dma_start(dst, src).then_inc(slot_in[c % RING], 16)
                    at += n

            x_v = x[0].rearrange("(t p) d -> p t d", p=P)
            sp.dma_start(x_sb[:, 0, :], x_v[:, 0, :]).then_inc(x_in[0], 16)
            sp.dma_start(x_sb[:, 1, :], x_v[:, 1, :]).then_inc(x_in[1], 16)
            sp.dma_start(const[:], consts).then_inc(const_in, 16)
            sp.dma_start(gain[:, 0, :], norm_mix[0].rearrange("(p k) -> p k", k=KD)).then_inc(gain0_in, 16)
            fill("ckv_iq", [cols(C_IQ, 256), cols(C_CKV, 256)])
            sp.dma_start(w_ikw[:], cols(C_IK, IDX_DIM + IDX_HEADS)).then_inc(ikw_in, 16)
            sp.dma_start(mem_sb, mem[0].rearrange("(t p) d -> p t d", p=P)).then_inc(mem_in, 16)
            fill("aq", [cols(C_AQ, 512)])
            fill("ak", [cols(C_AK, 512)])
            sp.wait_ge(biasrow_set, 1)
            sp.dma_start(bias_dram, bias_rows).then_inc(bias_out, 16)
            fill("av", [cols(C_AV, 512)])
            sp.wait_ge(bias_out, 16)
            sp.dma_start(bias_rep, bias_dram.unsqueeze(1).to_broadcast([2 * HEADS, P, T + P])).then_inc(bias_repeated, 16)
            fill("kx_vx", [w[0].rearrange("(k p) n -> p k n", k=KD) for w in (wk_x, wv_x)])
            sp.wait_ge(bias_repeated, 16)
            toeplitz = bass.AP(tensor=bias_rep.tensor, offset=P - 1,
                               ap=[[T + P - 1, P], [P * (T + P), 2 * HEADS], [1, T]])
            sp.dma_start(bias, toeplitz).then_inc(bias_in, 16)
            fill("ga0", [cols(C_GA, 512)])
            fill("ga1", [cols(C_GA + 512, 512)])
            fill("uk_uv", [w[0].rearrange("(p k) n -> p k n", k=2) for w in (w_uk, w_uv)])
            fill("bq", [cols(C_BQ, 512)])
            fill("gb0", [cols(C_GB, 512)])
            fill("gb1", [cols(C_GB + 512, 512)])
            fill("oa", [w_oa[0].rearrange("(k p) n -> p k n", p=P)])
            fill("ob", [w_ob[0].rearrange("(k p) n -> p k n", p=P)])
            for i in range(2):
                fill(f"out{i}", [w_out2.rearrange("(k p) n -> p k n", p=P)[:, :, 512 * i:512 * i + 512]])
            fill("qx_ox", [wq_x[0].rearrange("(p k) n -> p k n", k=KD), wo_x[0].rearrange("(k p) n -> p k n", p=P)])

            w1v = w1[0].rearrange("e (p k) n -> p e (k n)", k=KD)
            w3v = w3[0].rearrange("e (p k) n -> p e (k n)", k=KD)
            w2v = w2[0].rearrange("e (p f) n -> p e (f n)", f=FC)

            def load(q, e0):
                e = e0 + (q // MOE_CHUNKS) * SHARE
                j = q % MOE_CHUNKS
                if j < 8:
                    src = (w1v, w3v)[j % 2][:, bass.ds(e, SHARE), (j // 2) * 2 * D_E:(j // 2 + 1) * 2 * D_E]
                else:
                    src = w2v[:, bass.ds(e, SHARE), (j - 8) * D:(j - 7) * D]
                s = MOE_SLOTS[q % MOE_RING]
                sp.dma_start(ring[s].rearrange("p (e n) -> p e n", e=SHARE), src).then_inc(slot_in[s], 16)

            def load_part(turn, expert, first, end):
                used = [sp.snap(turn * TURN_CHUNKS + (q - MOE_RING + 1)) for q in range(first, end)]
                e0 = sp.snap(expert)
                for q in range(first, end):
                    sp.wait_ge(chunk_used, used[q - first])
                    sp.sem_inc(chunk_asked, 1)
                    load(q, e0)

            def load_rest(r, first_part_loaded):
                per_turn = UNROLL * SHARE
                if not first_part_loaded:
                    load_part(r * TURNS, 0, 0, MOE_RING)
                with sp.Fori(0, TURNS - 1) as g:
                    load_part(r * TURNS + g, g * per_turn, MOE_RING, TURN_CHUNKS)
                    load_part(r * TURNS + g + 1, g * per_turn + per_turn, 0, MOE_RING)
                load_part(r * TURNS + (TURNS - 1), (TURNS - 1) * per_turn, MOE_RING, TURN_CHUNKS)

            for q in range(MOE_RING):
                s = MOE_SLOTS[q]
                if s < RING:
                    job_computed(sp, LAST_JOB[[c for i, c in enumerate(CHUNKS) if i % RING == s][-1]])
                else:
                    sp.wait_ge(o_copied, 8)
                    job_computed(sp, "oa3")
                load(q, 0)
            sp.dma_start(fgain, final_norm.rearrange("(a d) -> a d", a=1).to_broadcast([P, D])).then_inc(fgain_in, 16)
            load_rest(0, True)
            sp.wait_ge(most_set, 1)
            fullest = sp.value_load(most_i[0:1, 0:1], min_val=0, max_val=T)
            with sp.Fori(1, ROUNDS) as r:
                with sp.If(fullest > r * SLOTS):
                    load_rest(r, False)
            out_v = out[0].rearrange("(t p) d -> p t d", p=P)
            for t in range(TT):
                sp.wait_ge(out_set, t + 1)
                sp.dma_start(out_v[:, t, :], xn[:, t, :]).then_inc(out_written, 16)
            sp.wait_ge(out_written, 16 * TT)

        @block.tensor
        def _(pe):
            def turn(src, n):
                for t in range(TT):
                    if src is mem_sb:
                        pe.wait_ge(mem_scaled[t], 1)
                    else:
                        pe.wait_ge(xn_set[t], (1, None, 2, 3)[n])
                    for b in range(4):
                        for k in range(2 * b, 2 * b + 2):
                            m = pe.transpose(turned[:, k, t * P:(t + 1) * P], src[:, t, k * P:(k + 1) * P], ident)
                        if t == TT - 1:
                            m.then_inc(turn_done, 1)

            def hT_ready(n):
                pe.wait_ge(turn_copied_a, 2 * n)
                pe.wait_ge(turn_copied_v, 2 * n)

            def begin(name):
                b, n = job(name)
                if n > 1:
                    pe.wait_ge(proj_free[b], n - 1)
                return ps[:, b, :]

            def end(ins, name):
                ins.then_inc(proj_done[job(name)[0]], 1)

            def columns(name, w, src, blocks, width):
                o = begin(name)
                kk = w.shape[1]
                for i, c in enumerate(blocks):
                    for k in range(kk):
                        m = pe.matmul(o[:, i * width:(i + 1) * width], w[:, k, c * P:(c + 1) * P], src[:, k, :],
                                      start=(k == 0), stop=(k == kk - 1))
                end(m, name)
                return m

            def rows(name, w, src, tiles, c0, n):
                o = begin(name)
                kk = w.shape[1]
                for i, t in enumerate(tiles):
                    for k in range(kk):
                        m = pe.matmul(o[:, i * n:(i + 1) * n], src[:, k, t * P:(t + 1) * P], w[:, k, c0:c0 + n],
                                      start=(k == 0), stop=(k == kk - 1))
                end(m, name)
                return m

            def w512(name):
                return chunk(name)[:, 0:4096].rearrange("p (k n) -> p k n", k=KD)

            pe.wait_ge(const_in, 16)
            turn(xn, 0)
            pe.wait_ge(tab_in, 48)
            m = pe.matmul(ps[0:2 * HEADS, 7, 0:3 * P], rel_sb[:], one_hot, start=True, stop=True)
            m.then_inc(biasrow_done, 1)
            hT_ready(1)
            chunk_landed(pe, "ckv_iq")
            w = chunk("ckv_iq").rearrange("p (a k n) -> p a k n", a=2, k=KD)
            columns("iq", w[:, 0], hT, (0, 1), T)
            pe.wait_ge(ikw_in, 16)
            o = begin("ikw")
            for j in range(4):
                for k in range(KD):
                    m = pe.matmul(o[32 * j:32 * j + 32, 0:T], w_ikw[:, k, 0:IDX_DIM], hT[:, k, :],
                                  start=(k == 0), stop=(k == KD - 1))
            for t in range(TT):
                for k in range(KD):
                    m = pe.matmul(o[:, T + 8 * t:T + 8 * t + 8], hT[:, k, t * P:(t + 1) * P],
                                  w_ikw[:, k, IDX_DIM:IDX_DIM + IDX_HEADS], start=(k == 0), stop=(k == KD - 1))
            end(m, "ikw")

            def index_logits(b):
                for h in range(4):
                    q = 32 * h
                    pe.matmul(ps[:, 2 + h, 0:P], iqT[q:q + 32, b, 0:P], ikT[q:q + 32, 0:P], start=True, stop=True)
                    m = pe.matmul(ps[:, 2 + h, P:3 * P], iqT[q:q + 32, b, P:T], ikT[q:q + 32, :],
                                  start=True, stop=True)
                m.then_inc(idx_done, 1)

            job_evacuated(pe, "iq")
            job_evacuated(pe, "ikw")
            index_logits(0)
            rows("ckv", w[:, 1], hT, (0, 1), 0, RANK)
            pe.wait_ge(relu_set, 1)
            index_logits(1)
            pe.wait_ge(relu_set, 2)
            turn(mem_sb, 1)
            job_evacuated(pe, "ckv")
            o = begin("ckvT")
            for r in range(2):
                for t in range(TT):
                    m = pe.transpose(o[:, r * T + t * P:r * T + (t + 1) * P],
                                     ckvn[:, t, r * P:(r + 1) * P], ident)
            end(m, "ckvT")
            for name in ("aq", "ak"):
                chunk_landed(pe, name)
                columns(name + "0", w512(name), hT, (0, 1), T)
                columns(name + "1", w512(name), hT, (2, 3), T)
            chunk_landed(pe, "av")
            rows("av0", w512("av"), hT, (0,), 0, 512)
            rows("av1", w512("av"), hT, (1,), 0, 512)
            hT_ready(2)

            def scores(n):
                if n == 0:
                    for name in ("aq0", "aq1", "ak0", "ak1"):
                        job_evacuated(pe, name)
                if n == 4:
                    for name in ("bq0", "bq1", "kb0", "kb1"):
                        job_evacuated(pe, name)
                if n >= 2:
                    pe.wait_ge(s_read, n - 1)
                q, k = (aqT, akT) if n < 4 else (bqT, kbT)
                for h in range(2):
                    r, b = HD * h, 2 + 2 * (n % 2) + h
                    pe.matmul(ps[:, b, 0:P], q[r:r + HD, n % 4, 0:P], k[r:r + HD, n % 4, 0:P], start=True, stop=True)
                    m = pe.matmul(ps[:, b, P:3 * P], q[r:r + HD, n % 4, P:T], k[r:r + HD, n % 4, :],
                                  start=True, stop=True)
                m.then_inc(s_done, 1)

            def turn_probs(n):
                pe.wait_ge(prob_set, n + 1)
                if n >= 1:
                    pe.wait_ge(o_copied, n)
                for h in range(2):
                    if n >= 1:
                        pe.wait_ge((probT_copied_a, probT_copied_v)[h], n)
                    for c in range(3):
                        m = pe.transpose(ps[:, 6 + h, c * P:(c + 1) * P], logit[:, n % 2, h, c * P:(c + 1) * P], ident)
                    m.then_inc(probT_done, 1)

            def weigh(n):
                if n == 0:
                    job_evacuated(pe, "av0")
                    job_evacuated(pe, "av1")
                if n == 4:
                    job_evacuated(pe, "vb0")
                    job_evacuated(pe, "vb1")
                pe.wait_ge(probT_copied_a, n + 1)
                pe.wait_ge(probT_copied_v, n + 1)
                v = av if n < 4 else vb
                c0 = (n % 4) * P
                for h in range(2):
                    r = slice(HD * h, HD * h + HD)
                    vs = [v[:, s, c0 + HD * h:c0 + HD * h + HD] for s in range(2)]
                    pT = probT[:, n % 2, h, :]
                    pe.matmul(ps[r, 6, 3 * P:4 * P], vs[0], pT[:, 0:P], start=True, stop=True)
                    pe.matmul(ps[r, 7, 3 * P:4 * P], vs[0], pT[:, P:2 * P], start=True, stop=False)
                    m = pe.matmul(ps[r, 7, 3 * P:4 * P], vs[1], pT[:, 2 * P:3 * P], start=False, stop=True)
                m.then_inc(o_done, 1)

            def gate(branch, i):
                name = f"{branch}{i // 2}"
                if i % 2 == 0:
                    chunk_landed(pe, name)
                m = columns(f"{branch}{i}", w512(name), hT, (2 * (i % 2), 2 * (i % 2) + 1), T)

            def latent():
                job_evacuated(pe, "ckvT")
                chunk_landed(pe, "uk_uv")
                w = chunk("uk_uv")[:, 0:2048].rearrange("p (a k n) -> p a k n", a=2, k=2)
                columns("kb0", w[:, 0], ckvT, (0, 1), T)
                columns("kb1", w[:, 0], ckvT, (2, 3), T)
                rows("vb0", w[:, 1], ckvT, (0,), 0, 512)
                rows("vb1", w[:, 1], ckvT, (1,), 0, 512)
                chunk_landed(pe, "bq")
                columns("bq0", w512("bq"), hT, (0, 1), T)
                columns("bq1", w512("bq"), hT, (2, 3), T)

            def memory_kv():
                chunk_landed(pe, "kx_vx")
                w = chunk("kx_vx").rearrange("p (a k n) -> p a k n", a=2, k=KD)
                columns("km", w[:, 0], memT, (0, 1), MEM)
                rows("vm", w[:, 1], memT, (0, 1), 0, W_X)

            def branch_out(name, src, blocks):
                chunk_landed(pe, name)
                w = chunk(name).rearrange("p (k n) -> p k n", k=4)
                for i in blocks:
                    columns(f"{name}{i}", w, src, (2 * i, 2 * i + 1), T)

            for n in range(9):
                if n == 1:
                    memory_kv()
                if n == 2 or n == 3:
                    gate("ga", 2 * n - 4)
                    gate("ga", 2 * n - 3)
                if n == 4:
                    latent()
                if n == 5 or n == 6:
                    gate("gb", 2 * n - 10)
                    gate("gb", 2 * n - 9)
                if n == 7:
                    branch_out("oa", aqT, (0, 1))
                if n == 8:
                    branch_out("oa", aqT, (2, 3))
                if n >= 1:
                    turn_probs(n - 1)
                if n < 8:
                    scores(n)
                if n >= 1:
                    weigh(n - 1)
            pe.wait_ge(o_copied, 8)
            branch_out("ob", bqT, range(4))
            pe.wait_ge(merged_set, 4)
            for i in range(4):
                if i < 2:
                    chunk_landed(pe, f"out{i}")
                rows(f"out{i}", w512(f"out{i % 2}"), merged, (i // 2,), 0, 512)

            turn(xn, 2)
            hT_ready(3)
            chunk_landed(pe, "qx_ox")
            wq = chunk("qx_ox")[:, 0:2048].rearrange("p (k n) -> p k n", k=KD)
            wo = chunk("qx_ox")[:, 2048:4096].rearrange("p (k n) -> p k n", k=2)
            columns("qx", wq, hT, (0, 1), T)
            for name in ("qx", "km", "vm"):
                job_evacuated(pe, name)
            for h in range(X_HEADS):
                r = HD * (h % 2)
                for t in range(TT):
                    m = pe.matmul(ps[:, 2 + h, t * MEM:(t + 1) * MEM], qxT[r:r + HD, h // 2, t * P:(t + 1) * P],
                                  kmT[r:r + HD, h // 2, :], start=True, stop=True)
                m.then_inc(xs_done, 1)
            for h in range(X_HEADS):
                pe.wait_ge(xprob_set, h + 1)
                if h >= 2:
                    pe.wait_ge((xpT_copied_a, xpT_copied_v)[h % 2], 1)
                for j in range(2):
                    for t in range(TT):
                        m = pe.transpose(ps[:, 6 + h % 2, j * T + t * P:j * T + (t + 1) * P],
                                         xprob[:, h, t, j * P:(j + 1) * P], ident)
                m.then_inc(xpT_done, 1)
            for c in range(2):
                o = begin(f"ox{c}")
                pe.wait_ge(xpT_copied_a, c + 1)
                pe.wait_ge(xpT_copied_v, c + 1)
                for h in range(2):
                    for j in range(2):
                        m = pe.matmul(o[HD * h:HD * h + HD, 0:T], vm[:, j, c * P + HD * h:c * P + HD * h + HD],
                                      xprobT[:, 2 * c + h, j, :], start=(j == 0), stop=(j == 1))
                end(m, f"ox{c}")
            job_evacuated(pe, "ox0")
            job_evacuated(pe, "ox1")
            for i in range(4):
                rows(f"xo{i}", wo, oxT, (i // 2,), 512 * (i % 2), 512)

            pe.wait_ge(xexp_set, X_HEADS)
            turn(xn, 3)
            hT_ready(4)
            pe.wait_ge(small_in, 16 * 4)
            rows("router", w_rt, hT, (0, 1), 0, GROUPS + EXPERTS)
            pe.wait_ge(routed, 1)
            o = begin("count")
            lt, one = const[:, K_LT:K_LT + P], const[:, K_ONE:K_ONE + P]
            chosen = rt[:, 8]
            pe.matmul(o[:, 0:EXPERTS], lt, chosen[:, 0, :], start=True, stop=True)
            pe.matmul(o[:, EXPERTS:2 * EXPERTS], lt, chosen[:, 1, :], start=True, stop=False)
            pe.matmul(o[:, EXPERTS:2 * EXPERTS], one, chosen[:, 0, :], start=False, stop=True)
            pe.matmul(o[:, 2 * EXPERTS:3 * EXPERTS], one, chosen[:, 0, :], start=True, stop=False)
            m = pe.matmul(o[:, 2 * EXPERTS:3 * EXPERTS], one, chosen[:, 1, :], start=False, stop=True)
            end(m, "count")

            pe.wait_ge(resid_set, 8)
            job_evacuated(pe, "count")
            for t in range(TT):
                for c in range(2):
                    pe.matmul(ps[:, 2 * t + c, :], ident, x_sb[:, t, 512 * c:512 * c + 512],
                              start=True, stop=True, skip_group_check=True)

            def expert_step(turn, u):
                it = turn * UNROLL + u
                pe.wait_ge(sel_set, it + 1)
                pe.wait_ge(actT_copied, it + 1)
                pe.wait_ge(selwT_copied, it + 1)
                for k in range(KD):
                    for t in range(TT):
                        m = pe.matmul(ps[:, 6 + k // 4, (k % 4) * P:(k % 4 + 1) * P], xn[:, t, k * P:(k + 1) * P],
                                      sel[:, t], start=(t == 0), stop=(t == TT - 1))
                m.then_inc(xe_done, 1)
                pe.wait_ge(xe_copied, it + 1)
                for t in range(TT):
                    m = pe.transpose(ps[:, 7, t * P:(t + 1) * P], selw[:, t], ident)
                m.then_inc(selwT_done, 1)
                pe.wait_ge(y_copied_a, it + 1)
                pe.wait_ge(y_copied_v, it + 1)
                for q in range(8):
                    s, v = moe_landed(u * MOE_CHUNKS + q)
                    pe.wait_ge(slot_in[s], turn * MOE_LANDED + v)
                    w = ring[s].rearrange("p (e k n) -> p e k n", e=SHARE, k=2)
                    for kk in range(2):
                        k = 2 * (q // 2) + kk
                        for e in range(SHARE):
                            m = pe.matmul(ps[SLOTS * e:SLOTS * e + SLOTS, 4 + q % 2, :],
                                          xeT[:, k, SLOTS * e:SLOTS * e + SLOTS], w[:, e, kk, :],
                                          start=(k == 0), stop=(k == KD - 1), skip_group_check=True)
                    m.then_inc(chunk_used, 1)
                pe.wait_ge(act_set, it + 2)
                for f in range(FC):
                    m = pe.transpose(ps[:, 6, f * P:(f + 1) * P], act_sb[:, f * P:(f + 1) * P], ident)
                m.then_inc(actT_done, 1)
                pe.wait_ge(actT_copied, it + 2)
                for f in range(FC):
                    s, v = moe_landed(u * MOE_CHUNKS + 8 + f)
                    pe.wait_ge(slot_in[s], turn * MOE_LANDED + v)
                    w = ring[s].rearrange("p (e n) -> p e n", e=SHARE)
                    for c in range(2):
                        for e in range(SHARE):
                            m = pe.matmul(ps[SLOTS * e:SLOTS * e + SLOTS, 4 + c, :],
                                          actT[:, f, SLOTS * e:SLOTS * e + SLOTS], w[:, e, 512 * c:512 * c + 512],
                                          start=(f == 0), stop=(f == FC - 1), skip_group_check=True)
                    m.then_inc(chunk_used, 1)
                pe.wait_ge(y_copied_a, it + 2)
                pe.wait_ge(y_copied_v, it + 2)
                pe.wait_ge(selwT_copied, it + 2)
                for c in range(2):
                    for t in range(TT):
                        m = pe.matmul(ps[:, 2 * t + c, :], selwT[:, t * P:(t + 1) * P], y_sb[:, 512 * c:512 * c + 512],
                                      start=False, stop=True, skip_group_check=True)
                m.then_inc(added, 1)

            for signal in (added, actT_done, selwT_done):
                pe.sem_inc(signal, 1)
            pe.wait_ge(most_set, 1)
            fullest = pe.value_load(most_i[0:1, 0:1], min_val=0, max_val=T)
            with pe.Fori(0, ROUNDS) as r:
                with pe.If(fullest > r * SLOTS):
                    with pe.Fori(0, TURNS) as g:
                        for u in range(UNROLL):
                            expert_step(r * TURNS + g, u)
            pe.matmul(ps[0:1, 6, 0:1], ident[:, 0:1], ident[:, 0:1], start=True, stop=True).then_inc(moe_done, 1)

        @block.scalar
        def _(act):
            act.dma_start(rel_sb[:], rel_bias).then_inc(tab_in, 16)
            act.dma_start(one_hot, buckets).then_inc(tab_in, 16)
            act.dma_start(below_sb, below).then_inc(tab_in, 16)
            act.dma_start(w_rt[:, :, 0:GROUPS], w_group[0].rearrange("(p k) n -> p k n", k=KD)).then_inc(small_in, 16)
            act.dma_start(w_rt[:, :, GROUPS:], w_router[0].rearrange("(p k) n -> p k n", k=KD)).then_inc(small_in, 16)
            act.dma_start(gain[:, 2, :], norm_x[0].rearrange("(p k) -> p k", k=KD)).then_inc(gain_in, 16)
            act.dma_start(gain[:, 3, :], norm_moe[0].rearrange("(p k) -> p k", k=KD)).then_inc(gain_in, 16)
            act.dma_start(gain_c[:], ckv_norm[0].rearrange("(p k) -> p k", k=2)).then_inc(gain_in, 16)
            with nc.allow_non_contiguous_dma(reason="a gain of 1024 numbers, once"):
                act.dma_start(gain[:, 1, :], mem_norm[0].rearrange("(k p) -> p k", p=P)).then_inc(gain_in, 16)
            act.dma_start(b_rt[:, 0:GROUPS], b_group.to_broadcast([P, GROUPS])).then_inc(small_in, 16)
            act.dma_start(b_rt[:, GROUPS:], b_router.to_broadcast([P, EXPERTS])).then_inc(small_in, 16)

            def square(src, n, t, junk, signal):
                return act.activation(junk, src, ACT.Square, accum_out=ssq[:, n, t:t + 1]).then_inc(signal, 1)

            def scaled(src, n, t):
                return act.activation(xn[:, t, :].rearrange("p (k q) -> p k q", k=KD),
                                      src.rearrange("p (q k) -> p k q", k=KD), ACT.Copy, scale=rstd[:, n, t:t + 1])

            def copy_turned(dst, n, g):
                for b in range(2):
                    act.wait_ge(turn_done, 4 * n + b + 1)
                    for k in range(2 * b, 2 * b + 2):
                        m = act.activation(dst[:, k, :], turned[:, k, :], ACT.Copy, scale=gain[:, g, k:k + 1])
                    m.then_inc(turn_copied_a, 1)

            def copy_job(name, dst, src=None):
                o = job_computed(act, name)
                evacuates(act.activation(dst, o if src is None else src(o), ACT.Copy), name)

            act.wait_ge(x_in[0], 16)
            square(x_sb[:, 0, :], 0, 0, xn[:, 0, :], squares[0])
            act.wait_ge(rstd_set[0], 1)
            scaled(x_sb[:, 0, :], 0, 0).then_inc(xn_set[0], 1)
            act.wait_ge(gain0_in, 16)
            copy_turned(hT, 0, 0)
            act.wait_ge(mem_in, 16)
            square(mem_sb[:, 0, :], 1, 0, memT[:, 0:4, :].rearrange("p a b -> p (a b)"), squares[0])
            copy_job("iq", iqT[:].rearrange("p a b -> p (a b)"))
            act.wait_ge(idx_done, 1)
            act.activation(relu4, ps[:, 2:6, 0:3 * P], ACT.Relu).then_inc(relu_set, 1)
            act.wait_ge(rstd_set[0], 2)
            act.activation(mem_sb[:, 0, :], mem_sb[:, 0, :], ACT.Copy, scale=rstd[:, 1, 0:1]).then_inc(mem_scaled[0], 1)
            act.wait_ge(gain_in, 16 * 4)
            o = job_computed(act, "ckv")
            for t in range(TT):
                square(o[:, t * RANK:(t + 1) * RANK], 4, t, memT[:, 4 + t, :], csq_done)
            act.wait_ge(idx_done, 2)
            act.wait_ge(idx_added, 1)
            act.activation(relu4, ps[:, 2:6, 0:3 * P], ACT.Relu).then_inc(relu_set, 1)
            act.wait_ge(crstd_set, 1)
            for t in range(TT):
                m = act.activation(ckvn[:, t, :].rearrange("p (k q) -> p k q", k=2),
                                   o[:, t * RANK:(t + 1) * RANK].rearrange("p (q k) -> p k q", k=2),
                                   ACT.Copy, scale=rstd[:, 4, t:t + 1])
            evacuates(m, "ckv")
            copy_turned(memT, 1, 1)
            o = job_computed(act, "ckvT")
            for r in range(2):
                m = act.activation(ckvT[:, r, :], o[:, r * T:(r + 1) * T], ACT.Copy, scale=gain_c[:, r:r + 1])
            evacuates(m, "ckvT")

            def pair(buf, i):
                return buf[:, 2 * i:2 * i + 2, :].rearrange("p a b -> p (a b)")

            for name, buf in (("aq", aqT), ("ak", akT)):
                copy_job(name + "0", pair(buf, 0))
                copy_job(name + "1", pair(buf, 1))
            copy_job("av0", av[:, 0, :])
            copy_job("av1", av[:, 1, :])

            def exps(n):
                act.wait_ge(max_set, n + 1)
                for h in range(2):
                    for t in range(TT):
                        seg = slice(0, P) if t == 0 else slice(P, 3 * P)
                        j = 2 * h + t
                        m = act.activation(logit[:, n % 2, h, seg], logit[:, n % 2, h, seg], ACT.Exp,
                                           bias=nmax[:, n, j:j + 1], accum_out=esum[:, n, j:j + 1])
                m.then_inc(exp_set, 1)

            def copy_probT(n):
                act.wait_ge(probT_done, 2 * n + 1)
                if n >= 2:
                    act.wait_ge(o_done, n - 1)
                act.activation(probT[:, n % 2, 0, :], ps[:, 6, 0:3 * P], ACT.Copy).then_inc(probT_copied_a, 1)

            def copy_o(n):
                act.wait_ge(o_done, n + 1)
                dst = (aqT if n < 4 else bqT)[:, n % 4, :]
                act.activation(dst.rearrange("p (t c) -> p t c", t=TT), ps[:, 6:8, 3 * P:4 * P],
                               ACT.Copy).then_inc(o_copied, 1)

            def gate_job(branch, i):
                o = job_computed(act, f"{branch}{i}")
                buf = ga if branch == "ga" else gb
                m = act.activation(pair(buf, i), o, ACT.Tanh, scale=0.5)
                evacuates(m, f"{branch}{i}")

            def memory_kv():
                copy_job("km", kmT.rearrange("p a b -> p (a b)"))
                copy_job("vm", vm.rearrange("p a b -> p (a b)"))

            for n in range(9):
                if n == 1:
                    memory_kv()
                if n == 2 or n == 3:
                    gate_job("ga", 2 * n - 4)
                    gate_job("ga", 2 * n - 3)
                if n == 4:
                    copy_job("kb0", pair(kbT, 0))
                    copy_job("kb1", pair(kbT, 1))
                    copy_job("vb0", vb[:, 0, :])
                    copy_job("vb1", vb[:, 1, :])
                    copy_job("bq0", pair(bqT, 0))
                    copy_job("bq1", pair(bqT, 1))
                if n == 5 or n == 6:
                    gate_job("gb", 2 * n - 10)
                    gate_job("gb", 2 * n - 9)
                if n >= 1:
                    copy_probT(n - 1)
                    copy_o(n - 1)
                if n < 8:
                    exps(n)

            def renorm(n, quarters):
                act.wait_ge(resid_set, quarters)
                square(x_sb[:, 0, :], n, 0, xn[:, 0, :], squares[0])
                act.wait_ge(rstd_set[0], n + 1)
                scaled(x_sb[:, 0, :], n, 0).then_inc(xn_set[0], 1)
                copy_turned(hT, n, n)

            renorm(2, 2)
            copy_job("qx", qxT[:].rearrange("p a b -> p (a b)"))
            for h in range(X_HEADS):
                act.wait_ge(xmax_set, h + 1)
                for t in range(TT):
                    m = act.activation(xprob[:, h, t, :], ps[:, 2 + h, t * MEM:(t + 1) * MEM], ACT.Exp, scale=SCALE,
                                       bias=xnmax[:, h, t:t + 1], accum_out=xsum[:, h, t:t + 1])
                m.then_inc(xexp_set, 1)
            for h in (0, 2):
                act.wait_ge(xpT_done, h + 1)
                act.activation(xprobT[:, h].rearrange("p a b -> p (a b)"), ps[:, 6, :], ACT.Copy).then_inc(xpT_copied_a, 1)
            for c in range(2):
                copy_job(f"ox{c}", oxT[:].rearrange("p a b -> p (a b)")[:, c * T:(c + 1) * T], lambda o: o[:, 0:T])
            renorm(3, 6)
            act.wait_ge(rexp_asked, 1)
            act.activation(rs[:, 15, :], rs[:, 14, :], ACT.Exp)
            act.activation(rt[:, 13, :, 0:GROUPS], rt[:, 12, :, 0:GROUPS], ACT.Exp).then_inc(rexp_set, 1)

            def expert_step(turn, u):
                it = turn * UNROLL + u
                act.wait_ge(selwT_done, it + 2)
                act.wait_ge(added, it + 1)
                act.activation(selwT, ps[:, 7, 0:T], ACT.Copy).then_inc(selwT_copied, 1)
                act.wait_ge(chunk_used, it * MOE_CHUNKS + 8)
                act.wait_ge(act_set, it + 1)
                act.activation(silu_sb, ps[:, 4, :].rearrange("p (q f) -> p f q", f=FC), ACT.Silu).then_inc(silu_set, 1)
                act.wait_ge(chunk_used, it * MOE_CHUNKS + MOE_CHUNKS)
                act.activation(y_sb[:, 0:512], ps[:, 4, :], ACT.Copy).then_inc(y_copied_a, 1)

            for signal in (selwT_copied, y_copied_a):
                act.sem_inc(signal, 1)
            act.wait_ge(most_set, 1)
            fullest = act.value_load(most_i[0:1, 0:1], min_val=0, max_val=T)
            with act.Fori(0, ROUNDS) as r:
                with act.If(fullest > r * SLOTS):
                    with act.Fori(0, TURNS) as g:
                        for u in range(UNROLL):
                            expert_step(r * TURNS + g, u)
            act.wait_ge(moe_done, 1)
            square(ps[:, 0:2, :], 5, 0, hT[:, 0:4, :].rearrange("p a b -> p (a b)").rearrange("p (a b) -> p a b", a=2), fsq)
            square(ps[:, 2:4, :], 5, 1, hT[:, 4:8, :].rearrange("p a b -> p (a b)").rearrange("p (a b) -> p a b", a=2), fsq)

        @block.vector
        def _(dve):
            steps = [0]

            def mark(ins):
                steps[0] += 1
                ins.then_inc(dve_step, 1)

            def then(ins):
                mark(ins)
                dve.wait_ge(dve_step, steps[0])

            def wait_marked():
                dve.wait_ge(dve_step, steps[0])

            def square(src, n, junk):
                dve.tensor_tensor_reduce(junk, src, src, 1.0, 0.0, ALU.mult, ALU.add,
                                         ssq[:, n, 1:2]).then_inc(squares[1], 1)

            def scaled(src, n):
                return dve.tensor_scalar(xn[:, 1, :].rearrange("p (k q) -> p k q", k=KD),
                                         src.rearrange("p (q k) -> p k q", k=KD), rstd[:, n, 1:2], None, ALU.mult)

            def copy_turned(dst, n, g):
                for b in range(2, 4):
                    dve.wait_ge(turn_done, 4 * n + b + 1)
                    gb_ = gain[:, g, 2 * b:2 * b + 2].unsqueeze(2).to_broadcast([P, 2, T])
                    dve.tensor_tensor(dst[:, 2 * b:2 * b + 2, :], turned[:, 2 * b:2 * b + 2, :], gb_,
                                      ALU.mult).then_inc(turn_copied_v, 1)

            dve.memset(half[:], -0.5).then_inc(half_set, 1)
            dve.wait_ge(x_in[1], 16)
            square(x_sb[:, 1, :], 0, xn[:, 1, :])
            dve.wait_ge(rstd_set[1], 1)
            scaled(x_sb[:, 1, :], 0).then_inc(xn_set[1], 1)
            dve.wait_ge(gain0_in, 16)
            copy_turned(hT, 0, 0)
            dve.wait_ge(tab_in, 48)
            dve.wait_ge(biasrow_done, 1)
            dve.tensor_tensor(bias_rows, ps[0:2 * HEADS, 7, 0:3 * P], below_sb, ALU.add).then_inc(biasrow_set, 1)
            dve.wait_ge(mem_in, 16)
            square(mem_sb[:, 1, :], 1, memT[:, 4:8, :].rearrange("p a b -> p (a b)"))
            o = job_computed(dve, "ikw")
            dve.tensor_copy(ikT[:], o[:, 0:T])
            evacuates(dve.tensor_scalar(iw[:], o[:, T:T + 16].rearrange("p (t h) -> p t h", t=TT),
                                        IDX_HEADS ** -0.5 * IDX_DIM ** -0.5, None, ALU.mult), "ikw")
            dve.wait_ge(rstd_set[1], 2)
            dve.tensor_scalar(mem_sb[:, 1, :], mem_sb[:, 1, :], rstd[:, 1, 1:2], None, ALU.mult).then_inc(mem_scaled[1], 1)
            dve.wait_ge(gain_in, 16 * 4)
            dve.wait_ge(const_in, 16)
            job_evacuated(dve, "ikw")
            for b in range(2):
                dve.wait_ge(relu_set, b + 1)
                for h in range(4):
                    if b + h:
                        wait_marked()
                    for t in range(TT):
                        seg = slice(0, P) if t == 0 else slice(P, 3 * P)
                        first = const[:, K_CAUSAL:K_CAUSAL + 3 * P][:, seg]
                        m = dve.scalar_tensor_tensor(score[:, seg], relu4[:, h, seg], iw[:, t, 4 * b + h:4 * b + h + 1],
                                                     first if b + h == 0 else score[:, seg], ALU.mult, ALU.add)
                    if h < 3 or b == 1:
                        mark(m)
                    else:
                        m.then_inc(idx_added, 1)
                        dve.wait_ge(idx_added, 1)
            wait_marked()
            copy_turned(memT, 1, 1)
            segs = (slice(0, P), slice(P, 3 * P))
            for _ in range(TOPK // 8):
                for t in range(TT):
                    m = dve.max(top8[:, t, :], score[:, segs[t]])
                mark(m)
                wait_marked()
                for t in range(TT):
                    m = dve.match_replace(score[:, segs[t]], top8[:, t, :], score[:, segs[t]], TAKEN)
                mark(m)
                wait_marked()
            then(dve.tensor_scalar(unpicked[:], score[:], TAKEN / 2, NEG, ALU.is_gt, ALU.mult))

            def logits(n):
                if n == 0:
                    dve.wait_ge(bias_in, 16)
                dve.wait_ge(s_done, n + 1)
                if n >= 2:
                    dve.wait_ge(probT_done, 2 * (n - 1))
                b0 = 2 + 2 * (n % 2)
                buf = logit[:, n % 2]
                dve.scalar_tensor_tensor(buf[:, :, P:3 * P], ps[:, b0:b0 + 2, P:3 * P], SCALE,
                                         bias[:, 2 * n:2 * n + 2, :], ALU.mult, ALU.add)
                dve.scalar_tensor_tensor(buf[:, :, 0:P], ps[:, b0:b0 + 2, 0:P], SCALE,
                                         bias[:, 2 * n:2 * n + 2, P:T], ALU.mult, ALU.add).then_inc(s_read, 1)
                dve.wait_ge(s_read, n + 1)
                if n >= 4:
                    then(dve.tensor_tensor(buf, buf, unpicked[:].unsqueeze(1).to_broadcast([P, 2, 3 * P]), ALU.add))
                dve.tensor_reduce(nmax[:, n, 0:4:2], buf[:, :, 0:P], AX_X, ALU.max, negate=True)
                dve.tensor_reduce(nmax[:, n, 1:4:2], buf[:, :, P:3 * P], AX_X, ALU.max, negate=True).then_inc(max_set, 1)

            def normalise(n):
                dve.wait_ge(exp_set, n + 1)
                then(dve.reciprocal(erec[:, n, :], esum[:, n, :]))
                for h in range(2):
                    for t in range(TT):
                        m = dve.tensor_scalar(logit[:, n % 2, h, segs[t]], logit[:, n % 2, h, segs[t]],
                                              erec[:, n, 2 * h + t:2 * h + t + 1], None, ALU.mult)
                m.then_inc(prob_set, 1)

            def copy_probT(n):
                dve.wait_ge(probT_done, 2 * n + 2)
                if n >= 2:
                    dve.wait_ge(o_done, n - 1)
                dve.tensor_copy(probT[:, n % 2, 1, :], ps[:, 7, 0:3 * P]).then_inc(probT_copied_v, 1)

            def finish_gates(buf, branch):
                job_evacuated(dve, f"{branch}2")
                job_evacuated(dve, f"{branch}3")
                dve.tensor_scalar(buf[:], buf[:], 0.5, 0.5, ALU.mult, ALU.add).then_inc(gates_set, 1)

            for n in range(9):
                if n == 4:
                    finish_gates(ga, "ga")
                if n == 7:
                    finish_gates(gb, "gb")
                    dve.wait_ge(gates_set, 2)
                if n >= 7:
                    for i in (2 * n - 14, 2 * n - 13):
                        o = job_computed(dve, f"oa{i}")
                        evacuates(dve.tensor_tensor(merged[:, 2 * i:2 * i + 2, :].rearrange("p a b -> p (a b)"), o,
                                                    ga[:, 2 * i:2 * i + 2, :].rearrange("p a b -> p (a b)"), ALU.mult), f"oa{i}")
                if n >= 1:
                    copy_probT(n - 1)
                if n < 8:
                    logits(n)
                    normalise(n)
            for i in range(4):
                part = gb[:, 2 * i:2 * i + 2, :].rearrange("p a b -> p (a b)")
                o = job_computed(dve, f"ob{i}")
                evacuates(dve.tensor_tensor(part, o, part, ALU.mult), f"ob{i}")
                job_evacuated(dve, f"ob{i}")
                job_evacuated(dve, f"oa{i}")
                m_ = merged[:, 2 * i:2 * i + 2, :].rearrange("p a b -> p (a b)")
                dve.tensor_tensor(m_, m_, part, ALU.add).then_inc(merged_set, 1)

            def add_residual(stem):
                for i in range(4):
                    o = job_computed(dve, f"{stem}{i}")
                    part = x_sb[:, i // 2, 512 * (i % 2):512 * (i % 2) + 512]
                    ins = dve.tensor_tensor(part, o, part, ALU.add)
                    evacuates(ins, f"{stem}{i}")
                    dve.wait_ge(proj_free[job(f"{stem}{i}")[0]], job(f"{stem}{i}")[1])
                    dve.sem_inc(resid_set, 1)

            def renorm(n):
                square(x_sb[:, 1, :], n, xn[:, 1, :])
                dve.wait_ge(rstd_set[1], n + 1)
                scaled(x_sb[:, 1, :], n).then_inc(xn_set[1], 1)
                copy_turned(hT, n, n)

            add_residual("out")
            renorm(2)
            for h in range(X_HEADS):
                dve.wait_ge(xs_done, h + 1)
                then(dve.tensor_reduce(xnmax[:, h, :], ps[:, 2 + h, :].rearrange("p (t m) -> p t m", t=TT), AX_X,
                                       ALU.max, negate=True))
                dve.tensor_scalar(xnmax[:, h, :], xnmax[:, h, :], SCALE, None, ALU.mult).then_inc(xmax_set, 1)
            for h in range(X_HEADS):
                dve.wait_ge(xexp_set, h + 1)
                then(dve.reciprocal(xrec[:, h, :], xsum[:, h, :]))
                for t in range(TT):
                    m = dve.tensor_scalar(xprob[:, h, t, :], xprob[:, h, t, :], xrec[:, h, t:t + 1], None, ALU.mult)
                m.then_inc(xprob_set, 1)
                if h % 2:
                    dve.wait_ge(xpT_done, h + 1)
                    dve.tensor_copy(xprobT[:, h].rearrange("p a b -> p (a b)"), ps[:, 7, :]).then_inc(xpT_copied_v, 1)
            add_residual("xo")
            renorm(3)

            def wide(s):
                return rs[:, s, :].unsqueeze(2).to_broadcast([P, TT, EXPERTS])

            o = job_computed(dve, "router")
            dve.wait_ge(small_in, 16 * 4)
            n_rt = GROUPS + EXPERTS
            evacuates(dve.tensor_tensor(rl[:], o[:, 0:TT * n_rt].rearrange("p (t n) -> p t n", t=TT),
                                        b_rt[:].unsqueeze(1).to_broadcast([P, TT, n_rt]), ALU.add), "router")
            job_evacuated(dve, "router")
            group = rl[:, :, 0:GROUPS]
            gwide = lambda s: rs[:, s, :].unsqueeze(2).to_broadcast([P, TT, GROUPS])
            fall4 = const[:, K_DESC:K_DESC + GROUPS].unsqueeze(1).to_broadcast([P, TT, GROUPS])
            fall = const[:, K_DESC:K_DESC + EXPERTS].unsqueeze(1).to_broadcast([P, TT, EXPERTS])
            then(dve.tensor_reduce(rs[:, 0, :], group, AX_X, ALU.max))
            dve.tensor_tensor(rt[:, 12, :, 0:GROUPS], group, gwide(0), ALU.subtract)
            then(dve.tensor_tensor(rt[:, 0, :, 0:GROUPS], group, gwide(0), ALU.is_equal))
            then(dve.tensor_tensor(rt[:, 1, :, 0:GROUPS], rt[:, 0, :, 0:GROUPS], fall4, ALU.mult))
            then(dve.tensor_reduce(rs[:, 1, :], rt[:, 1, :, 0:GROUPS], AX_X, ALU.max))
            then(dve.tensor_tensor(rt[:, 0, :, 0:GROUPS], rt[:, 1, :, 0:GROUPS], gwide(1), ALU.is_equal))
            then(dve.tensor_scalar(rt[:, 1, :, 0:GROUPS], rt[:, 0, :, 0:GROUPS], 1.0, -NEG, ALU.subtract, ALU.mult))
            em = rt[:, 2]
            then(dve.tensor_tensor(em.rearrange("p t (g e) -> p t g e", g=GROUPS),
                                   rl[:, :, GROUPS:].rearrange("p t (g e) -> p t g e", g=GROUPS),
                                   rt[:, 1, :, 0:GROUPS].unsqueeze(3).to_broadcast([P, TT, GROUPS, PER_GROUP]), ALU.add))
            for i, src in ((0, rt[:, 2]), (1, rt[:, 3])):
                then(dve.tensor_reduce(rs[:, 2 + i, :], src, AX_X, ALU.max))
                then(dve.tensor_tensor(rt[:, 4], src, wide(2 + i), ALU.is_equal))
                then(dve.tensor_tensor(rt[:, 4], rt[:, 4], fall, ALU.mult))
                then(dve.tensor_reduce(rs[:, 4, :], rt[:, 4], AX_X, ALU.max))
                then(dve.tensor_tensor(rt[:, 6 + i], rt[:, 4], wide(4), ALU.is_equal))
                if i == 0:
                    then(dve.scalar_tensor_tensor(rt[:, 3], rt[:, 6], 2 * NEG, rt[:, 2], ALU.mult, ALU.add))
            dve.tensor_tensor(rt[:, 8], rt[:, 6], rt[:, 7], ALU.add).then_inc(routed, 1)
            dve.tensor_tensor(rs[:, 14, :], rs[:, 3, :], rs[:, 2, :], ALU.subtract).then_inc(rexp_asked, 1)
            o = job_computed(dve, "count")
            then(dve.tensor_reduce(most[:], o[:, 2 * EXPERTS:3 * EXPERTS], AX_X, ALU.max))
            dve.tensor_copy(most_i[:], most[:]).then_inc(most_set, 1)
            dve.wait_ge(routed, 1)
            then(dve.scalar_tensor_tensor(rt[:, 9], o[:, 0:2 * EXPERTS].rearrange("p (t e) -> p t e", t=TT), 1.0, rt[:, 8],
                                          ALU.add, ALU.mult))
            place = rt[:, 10]
            evacuates(dve.tensor_scalar(place, rt[:, 9], -1.0, None, ALU.add), "count")
            dve.wait_ge(rexp_set, 1)
            then(dve.tensor_reduce(rs[:, 5, :], rt[:, 13, :, 0:GROUPS], AX_X, ALU.add))
            then(dve.reciprocal(rs[:, 6, :], rs[:, 5, :]))
            then(dve.tensor_scalar(rs[:, 7, :], rs[:, 15, :], 1.0, None, ALU.add))
            then(dve.reciprocal(rs[:, 8, :], rs[:, 7, :]))
            then(dve.tensor_tensor(rs[:, 9, :], rs[:, 15, :], rs[:, 8, :], ALU.mult))
            then(dve.tensor_tensor(rs[:, 10, :], rs[:, 8, :], rs[:, 6, :], ALU.mult))
            then(dve.tensor_tensor(rs[:, 11, :], rs[:, 9, :], rs[:, 6, :], ALU.mult))
            then(dve.tensor_tensor(rt[:, 4], rt[:, 6], wide(10), ALU.mult))
            then(dve.tensor_tensor(rt[:, 5], rt[:, 7], wide(11), ALU.mult))
            weight = rt[:, 11]
            then(dve.tensor_tensor(weight, rt[:, 4], rt[:, 5], ALU.add))
            job_evacuated(dve, "count")

            slots = const[:, K_SLOT:K_SLOT + SLOTS].unsqueeze(1).unsqueeze(1).to_broadcast([P, TT, SHARE, SLOTS])

            def expert_step(turn, u, expert, r):
                it = turn * UNROLL + u
                e0 = dve.snap(expert)
                dve.wait_ge(moved, r + 1)
                dve.wait_ge(selwT_done, it + 1)
                dve.tensor_tensor(sel, place[:, :, bass.ds(e0, SHARE)].unsqueeze(3).to_broadcast([P, TT, SHARE, SLOTS]),
                                  slots, ALU.is_equal).then_inc(sel_made, 1)
                dve.wait_ge(sel_made, it + 1)
                dve.tensor_tensor(selw, sel, weight[:, :, bass.ds(e0, SHARE)].unsqueeze(3).to_broadcast(
                    [P, TT, SHARE, SLOTS]), ALU.mult).then_inc(sel_set, 1)
                dve.wait_ge(xe_done, it + 1)
                for b in range(2):
                    m = dve.tensor_tensor(xeT[:, 4 * b:4 * b + 4, :], ps[:, 6 + b, :].rearrange("p (k s) -> p k s", k=4),
                                          gain[:, 3, 4 * b:4 * b + 4].unsqueeze(2).to_broadcast([P, 4, P]), ALU.mult)
                m.then_inc(xe_copied, 1)
                dve.wait_ge(silu_set, it + 1)
                dve.wait_ge(actT_done, it + 1)
                dve.tensor_tensor(act_sb, ps[:, 5, :].rearrange("p (q f) -> p f q", f=FC),
                                  silu_sb.rearrange("p (f q) -> p f q", f=FC), ALU.mult).then_inc(act_set, 1)
                dve.wait_ge(actT_done, it + 2)
                dve.tensor_copy(actT.rearrange("p f s -> p (f s)"), ps[:, 6, :]).then_inc(actT_copied, 1)
                dve.wait_ge(chunk_used, it * MOE_CHUNKS + MOE_CHUNKS)
                dve.wait_ge(added, it + 1)
                dve.tensor_copy(y_sb[:, 512:1024], ps[:, 5, :]).then_inc(y_copied_v, 1)

            for signal in (actT_copied, y_copied_v, act_set, moved):
                dve.sem_inc(signal, 1)
            dve.wait_ge(most_set, 1)
            fullest = dve.value_load(most_i[0:1, 0:1], min_val=0, max_val=T)
            with dve.Fori(0, ROUNDS) as r:
                with dve.If(fullest > r * SLOTS):
                    with dve.Fori(0, TURNS) as g:
                        for u in range(UNROLL):
                            expert_step(r * TURNS + g, u, g * (UNROLL * SHARE) + u * SHARE, r)
                    dve.tensor_scalar(place, place, -float(SLOTS), None, ALU.add).then_inc(moved, 1)

            dve.wait_ge(fgain_in, 16)
            dve.wait_ge(moe_done, 1)
            dve.wait_ge(frstd_set, 1)
            for t in range(TT):
                dve.scalar_tensor_tensor(xn[:, t, :].rearrange("p (c n) -> p c n", c=2), ps[:, 2 * t:2 * t + 2, :],
                                         rstd[:, 5, t:t + 1], fgain.rearrange("p (c n) -> p c n", c=2),
                                         ALU.mult, ALU.mult).then_inc(out_set, 1)

        @block.gpsimd
        def _(pool):
            steps = [0]

            def inverse_rms(n, t, width, signal):
                steps[0] += 1
                pool.tensor_scalar(var[:, n, t], ssq[:, n, t], 1.0 / width, EPS, ALU.mult, ALU.add).then_inc(pool_step, 1)
                pool.wait_ge(pool_step, steps[0])
                pool.tensor_tensor(rstd[:, n, t], var[:, n, t], half[:, t], ALU.pow).then_inc(signal, 1)

            def of_d_model(n):
                for t in range(TT):
                    pool.wait_ge(squares[t], n + 1)
                    inverse_rms(n, slice(t, t + 1), D, rstd_set[t])

            pool.wait_ge(half_set, 1)
            of_d_model(0)
            of_d_model(1)
            pool.wait_ge(csq_done, 2)
            inverse_rms(4, slice(0, 2), RANK, crstd_set)
            of_d_model(2)
            of_d_model(3)
            pool.wait_ge(fsq, 2)
            inverse_rms(5, slice(0, 2), D, frstd_set)


NAMES = ["x", "mem", "rel_bias", "final_norm", "norm_mix", "w_in", "ckv_norm", "w_uk", "w_uv", "w_oa", "w_ob",
         "w_out", "norm_x", "mem_norm", "wq_x", "wk_x", "wv_x", "wo_x", "norm_moe", "w_group", "b_group",
         "w_router", "b_router", "w1", "w3", "w2"]


def kernel(**inputs):
    import concourse.bacc as bacc
    from concourse.bass_utils import run_bass_kernel_spmd

    nc = bacc.Bacc("TRN2", target_bir_lowering=False, num_devices=1)
    arrays = {name: np.ascontiguousarray(inputs[name]) for name in NAMES}
    arrays["consts"], arrays["buckets"], arrays["below"] = shape_constants()
    args = [nc.dram_tensor(f"in_{n}", a.shape, mybir.dt.from_np(a.dtype), kind="ExternalInput").ap()
            for n, a in arrays.items()]
    out = nc.dram_tensor("out", (1, T, D), F32, kind="ExternalOutput").ap()
    decoder_layer(nc, *args, out)
    r = run_bass_kernel_spmd(nc, [{f"in_{n}": a for n, a in arrays.items()}], core_ids=[0])
    return r.results[0]["out"]
```

```python
import math
from contextlib import ExitStack

import numpy as np

import concourse.bass as bass
from concourse import mybir

ALU = mybir.AluOpType
ACT = mybir.ActivationFunctionType
AX_X = mybir.AxisListType.X
F32 = mybir.dt.float32
F32R = mybir.dt.float32r
I32 = mybir.dt.int32

P = 128
T, D = 256, 1024
TT = T // P
KD = D // P
HEADS, HD = 8, 64
W_HEADS = HEADS * HD
RANK = 256
IDX_HEADS, IDX_DIM = 8, 32
TOPK = min(256, T // 4)
BUCKETS, MAX_DIST = 32, 128
MEM, X_HEADS = 256, 4
W_X = X_HEADS * HD
GROUPS, PER_GROUP = 4, 8
EXPERTS = GROUPS * PER_GROUP
D_E = 512
FC = D_E // P
N_RT = GROUPS + EXPERTS
EPS = 1e-6
NEG = -1e30
TAKEN = -3e38
SCALE = HD ** -0.5

C_AQ, C_AK, C_AV, C_BQ = (i * W_HEADS for i in range(4))
C_CKV = 4 * W_HEADS
C_IQ = C_CKV + RANK
C_IK = C_IQ + IDX_HEADS * IDX_DIM
C_GA = C_IK + IDX_DIM + IDX_HEADS
C_GB = C_GA + D

SLOTS = 32
SHARE = P // SLOTS
STEPS = EXPERTS // SHARE
ROUNDS = T // SLOTS

RING = 3
MOE_SLOTS = [6, 7, 1, 2, 3, 4, 5, 8, 0]
MOE_RING = len(MOE_SLOTS)
SLOT = 4096
MOE_CHUNKS = 12
UNROLL = 2
TURNS = STEPS // UNROLL
TURN_CHUNKS = UNROLL * MOE_CHUNKS

K_ID, K_LT, K_ONE, K_CAUSAL = 0, P, 2 * P, 3 * P
K_SLOT = K_CAUSAL + 3 * P
K_N = K_SLOT + SLOTS


def shape_constants():
    c = np.zeros((P, K_N), np.float32)
    p = np.arange(P)[:, None]
    i = np.arange(P)[None, :]
    c[:, K_ID:K_ID + P] = p == i
    c[:, K_LT:K_LT + P] = p < i
    c[:, K_ONE:K_ONE + P] = 1.0
    c[:, K_CAUSAL:K_CAUSAL + P] = np.where(i > p, NEG, 0.0)
    c[:, K_CAUSAL + P:K_CAUSAL + 3 * P] = np.where(np.arange(T)[None, :] > p + P, NEG, 0.0)
    c[:, K_SLOT:K_SLOT + SLOTS] = 1 + np.arange(SLOTS)
    dist = T - 1 - np.arange(T + P)
    exact = BUCKETS // 2
    b = np.zeros((BUCKETS, T + P), np.float32)
    for m, n in enumerate(dist):
        if n < 0:
            continue
        if n >= exact:
            n = min(exact + int(math.log(n / exact) / math.log(MAX_DIST / exact) * (BUCKETS - exact)), BUCKETS - 1)
        b[n, m] = 1.0
    below = np.broadcast_to(np.where(dist < 0, NEG, 0.0).astype(np.float32), (2 * HEADS, T + P))
    return c, b, np.ascontiguousarray(below)


JOBS = (["iq", "ikw", "ckv", "ckvT", "aq0", "aq1", "ak0", "ak1", "av0", "av1", "km", "vm"]
        + [f"ga{i}" for i in range(4)]
        + ["kb0", "kb1", "vb0", "vb1", "bq0", "bq1", "gb0", "gb1", "gb2", "oa0", "gb3", "oa1", "oa2", "oa3"]
        + [f"ob{i}" for i in range(4)]
        + [f"out{i}" for i in range(4)] + ["qx", "ox0", "ox1"] + [f"xo{i}" for i in range(4)])

CHUNKS = ["ckv_iq", "aq", "ak", "av", "kx_vx", "ga0", "ga1", "uk_uv", "bq", "gb0", "gb1",
          "oa", "ob", "out0", "out1", "qx_ox"]
LAST_JOB = {"ckv_iq": "ckv", "aq": "aq1", "ak": "ak1", "av": "av1", "kx_vx": "vm", "ga0": "ga1", "ga1": "ga3",
            "uk_uv": "vb1", "bq": "bq1", "gb0": "gb1", "gb1": "gb3", "oa": "oa3", "ob": "ob3", "out0": "out1",
            "out1": "out3", "qx_ox": "xo3"}
PARTS = {"uk_uv": 2, "kx_vx": 2, "qx_ox": 2}
assert (len(CHUNKS) - 1) % RING == MOE_SLOTS[-1]

SPLITS = (["iq", "ikw", "ckv", "aq0", "aq1", "ak0", "ak1", "av0", "av1", "km", "vm"] + [f"ga{i}" for i in range(4)]
          + ["bq0", "bq1", "gb0", "gb1", "gb2", "oa0", "gb3", "oa1", "oa2", "oa3"]
          + [f"ob{i}" for i in range(4)] + [f"out{i}" for i in range(4)] + ["qx"])
SLOT_JOBS = [[], ["km", "vm"], ["ga0", "ga1"], ["ga2", "ga3"], ["bq0", "bq1"], ["gb0", "gb1"], ["gb2", "oa0"],
             ["gb3", "oa1"], ["oa2", "oa3"]]
POOL_LOW = ("oa0", "oa1", "oa3", "ob1", "ob3", "out1")
IKW = 4 * IDX_DIM + IDX_HEADS


def low_parts(name):
    by_pool = name in POOL_LOW
    return by_pool, sum((n in POOL_LOW) == by_pool for n in SPLITS[:SPLITS.index(name) + 1])


def landed(name):
    c = CHUNKS.index(name)
    return c % RING, 16 * sum(PARTS.get(CHUNKS[i], 1) for i in range(c % RING, c + 1, RING))


def is_w2(q):
    return q % MOE_CHUNKS >= 8


def moe_slot(q):
    return MOE_SLOTS[q % MOE_RING]


def moe_landed(q):
    s = moe_slot(q)
    same = [i for i in range(TURN_CHUNKS) if moe_slot(i) == s]
    own = sum(PARTS.get(CHUNKS[i], 1) for i in range(s, len(CHUNKS), RING)) if s < RING else 0
    return (16 * (own + sum(i <= q for i in same)), 16 * sum(i <= q and is_w2(i) for i in same),
            16 * len(same), 16 * sum(is_w2(i) for i in same))


def used_before(q):
    last = [i for i in range(-TURN_CHUNKS, q) if moe_slot(i % TURN_CHUNKS) == moe_slot(q)][-1]
    return last + 1


def decoder_layer(nc, x, mem, rel_bias, final_norm, norm_mix, w_in, ckv_norm, w_uk, w_uv, w_oa, w_ob,
                  w_out, norm_x, mem_norm, wq_x, wk_x, wv_x, wo_x, norm_moe, w_group, b_group,
                  w_router, b_router, w1, w3, w2, consts, buckets, below, out):
    with ExitStack() as ctx:
        def sb(name, shape, dt=F32):
            return ctx.enter_context(nc.sbuf_tensor(name, shape, dt))

        def sem(name):
            return ctx.enter_context(nc.semaphore(name))

        slots_own = sb("slots_own", [P, RING, SLOT])
        with ExitStack() as early:
            def sb_early(name, shape):
                return early.enter_context(nc.sbuf_tensor(name, shape, F32R))

            o_parts = sb_early("o_parts", [P, 4, 4, T])
            w_high = sb_early("w_high", [P, 2, 2048])
            w_low = sb_early("w_low", [P, 2, 2048])
        oA, oB = (o_parts[:, 0], o_parts[:, 1]), (o_parts[:, 2], o_parts[:, 3])
        tT_high, tT_low = (o_parts[:, i:i + 2].rearrange("p a b t -> p (a b) t") for i in (0, 2))
        slots_late = sb("slots_late", [P, 3, SLOT])
        attn_data = sb("attn_data", [P, 2, SLOT])
        x_sb = sb("x_sb", [P, TT, D])
        xn = sb("xn", [P, TT, D])
        with ExitStack() as early:
            h_high, h_low = (early.enter_context(nc.sbuf_tensor(f"h_{p}", [P, KD, T], F32R)) for p in ("high", "low"))
        slot_last = sb("slot_last", [P, SLOT])
        ring = ([slots_own[:, i, :] for i in range(RING)] + [slots_late[:, i, :] for i in range(3)]
                + [attn_data[:, i, :] for i in range(2)] + [slot_last[:]])
        ga = sb("ga", [P, KD, T])
        gb = sb("gb", [P, KD, T])
        bias = attn_data[:, 0, :].rearrange("p (h c) -> p h c", h=2 * HEADS)
        aqT, akT, kbT = (attn_data[:, 1, i * 1024:(i + 1) * 1024].rearrange("p (a b) -> p a b", a=4) for i in range(3))
        av = attn_data[:, 1, 3072:4096].rearrange("p (a b) -> p a b", a=TT)
        bqT = sb("bqT", [P, 4, T])
        vb = sb("vb", [P, TT, W_HEADS])
        iqT = sb("iqT", [P, 2, T])
        ikT = sb("ikT", [P, T])
        iw = sb("iw", [P, TT, IDX_HEADS])
        ckvn = sb("ckvn", [P, TT, RANK])
        memory_kv_data = sb("memory_kv_data", [P, D])
        kmT = memory_kv_data[:, 0:512].rearrange("p (a b) -> p a b", a=2)
        vm = memory_kv_data[:, 512:1024].rearrange("p (a b) -> p a b", a=2)
        score = sb("score", [P, 3 * P])
        logit = xn[:].rearrange("p a b -> p (a b)")[:, 0:12 * P].rearrange("p (i h c) -> p i h c", i=2, h=2)
        probT = sb("probT", [P, 2, 2, 3 * P])
        const = sb("const", [P, K_N])
        w_ikw = sb("w_ikw", [P, KD, IDX_DIM + IDX_HEADS])
        w_rt = sb("w_rt", [P, KD, GROUPS + EXPERTS])
        b_rt = sb("b_rt", [P, GROUPS + EXPERTS])
        gain = sb("gain", [P, 5, KD])
        qscale = sb("qscale", [P, TT])
        gain_c = sb("gain_c", [P, 2])
        rel_sb = sb("rel_sb", [BUCKETS, 2 * HEADS])
        half = sb("half", [P, 2])
        ssq = sb("ssq", [P, 6, 2])
        var = sb("var", [P, 6, 2])
        rstd = sb("rstd", [P, 6, 2])
        top8 = sb("top8", [P, 2, 8])
        nmax = sb("nmax", [P, 8, 4])
        esum = sb("esum", [P, 8, 4])
        erec = sb("erec", [P, 8, 4])
        xnmax = sb("xnmax", [P, X_HEADS, 2])
        xsum = sb("xsum", [P, X_HEADS, 2])
        xrec = sb("xrec", [P, X_HEADS, 2])
        rs = sb("rs", [P, 4, TT])
        rl = sb("rl", [P, TT, GROUPS + EXPERTS])
        wanted = sb("wanted", [P, TT, 2, 8])
        most = sb("most", [P, 1])
        most_i = sb("most_i", [P, 1], I32)
        mem_sb = ga[:].rearrange("p a b -> p (a b)").rearrange("p (t d) -> p t d", t=TT)
        junk = gb
        relu = xn
        relu4 = relu[:].rearrange("p a b -> p (a b)")[:, 0:4 * 3 * P].rearrange("p (h c) -> p h c", h=4)
        bias_rows = probT[0:2 * HEADS, 0, 0, :]
        one_hot = probT[0:BUCKETS, 1, 0, :]
        below_sb = probT[0:2 * HEADS, 1, 1, :]
        ckvT = iqT
        qxT = iqT
        unpicked = score
        oxT = ckvn
        def flat(buf):
            return buf.rearrange("p a b -> p (a b)")

        xprob = flat(ga[:]).rearrange("p (h t m) -> p h t m", h=X_HEADS, t=TT)
        xprobT = flat(gb[:]).rearrange("p (h m t) -> p h m t", h=X_HEADS, m=2)
        rt = flat(gb[:])[:, 0:14 * TT * EXPERTS].rearrange(
            "p (n t e) -> p n t e", n=14, t=TT)
        fgain = memory_kv_data[:]
        xT = ga
        rlT = probT[0:N_RT, 0, 0, 0:T]
        xeT = flat(ga[:, 0:4]).rearrange("p (k s) -> p k s", k=KD)
        y_sb = flat(ga[:, 4:8])
        silu_sb = flat(bqT[:])[:, 0:D_E]
        act_sb = flat(bqT[:])[:, D_E:2 * D_E]
        actT = flat(vb[:])[:, 0:D_E].rearrange("p (f s) -> p f s", f=FC)
        selwT = flat(vb[:])[:, D_E:D_E + T]
        sel = iqT[:, 0].rearrange("p (t e s) -> p t e s", t=TT, e=SHARE)
        selw = iqT[:, 1].rearrange("p (t e s) -> p t e s", t=TT, e=SHARE)
        ident = const[:, K_ID:K_ID + P]

        ps = ctx.enter_context(nc.psum_tensor("ps", [P, 8, 512], F32))
        turned = ps[:, 2:6, :].rearrange("p b (k t) -> p (b k) t", k=2)

        bias_dram = nc.dram_tensor("bias_rows_dram", [2 * HEADS, T + P], F32).ap()
        bias_rep = nc.dram_tensor("bias_rep_dram", [2 * HEADS, P, T + P], F32).ap()

        mem_in, ident_in, const_in, gain_in = sem("mem_in"), sem("ident_in"), sem("const_in"), sem("gain_in")
        iq_in = sem("iq_in")
        x_in = [sem(f"x_in{t}") for t in range(TT)]
        gain0_in = sem("gain0_in")
        small_in, tab_in, bias_out, bias_repeated, bias_in, fgain_in = (
            sem("small_in"), sem("tab_in"), sem("bias_out"), sem("bias_repeated"), sem("bias_in"), sem("fgain_in"))
        slot_in = [sem(f"slot_in{i}") for i in range(MOE_RING)]
        right_in = [sem(f"right_in{i}") for i in range(MOE_RING)]
        chunk_used = sem("chunk_used")
        half_set = sem("half_set")
        squares = [sem(f"squares{t}") for t in range(TT)]
        rstd_set = [sem(f"rstd_set{t}") for t in range(TT)]
        xn_set = [sem(f"xn_set{t}") for t in range(TT)]
        mem_scaled = [sem(f"mem_scaled{t}") for t in range(TT)]
        turn_done = sem("turn_done")
        h_high_set, h_low_set = sem("h_high_set"), sem("h_low_set")
        split_high = sem("split_high")
        low_set = (sem("low_set_v"), sem("low_set_p"))
        o_split, merge_added, merge_high = sem("o_split"), sem("merge_added"), sem("merge_high")
        biasrow_done, biasrow_set = sem("biasrow_done"), sem("biasrow_set")
        proj_done = [sem(f"proj_done{i}") for i in range(2)]
        proj_free = [sem(f"proj_free{i}") for i in range(2)]
        idx_done, relu_set, idx_added = sem("idx_done"), sem("relu_set"), sem("idx_added")
        csq_done, crstd_set = sem("csq_done"), sem("crstd_set")
        s_done, s_read, max_set, exp_set, prob_set = (
            sem("s_done"), sem("s_read"), sem("max_set"), sem("exp_set"), sem("prob_set"))
        probT_done, probT_copied_a, probT_copied_v = (
            sem("probT_done"), sem("probT_copied_a"), sem("probT_copied_v"))
        o_done, o_copied = sem("o_done"), sem("o_copied")
        gates_set = sem("gates_set")
        merged_set = sem("merged_set")
        resid_set = sem("resid_set")
        xs_done, xmax_set, xexp_set, xprob_set = (
            sem("xs_done"), sem("xmax_set"), sem("xexp_set"), sem("xprob_set"))
        xpT_done, xpT_copied_a, xpT_copied_v = sem("xpT_done"), sem("xpT_copied_a"), sem("xpT_copied_v")
        xresid_set = sem("xresid_set")
        router_set, xturned, xT_copied = sem("router_set"), sem("xturned"), sem("xT_copied")
        logitsT_done, logitsT_copied, logits_done, count_done, count_read, qscale_set = (
            sem("logitsT_done"), sem("logitsT_copied"), sem("logits_done"), sem("count_done"), sem("count_read"),
            sem("qscale_set"))
        rexp_asked, rexp_set = sem("rexp_asked"), sem("rexp_set")
        routed, most_set = sem("routed"), sem("most_set")
        sel_set, xe_done, xe_copied, selwT_done, selwT_copied = (
            sem("sel_set"), sem("xe_done"), sem("xe_copied"), sem("selwT_done"), sem("selwT_copied"))
        silu_set, act_set, actT_done, actT_copied = (
            sem("silu_set"), sem("act_set"), sem("actT_done"), sem("actT_copied"))
        y_left_done, y_copied_a, y_copied_v, added = (
            sem("y_left_done"), sem("y_copied_a"), sem("y_copied_v"), sem("added"))
        moe_done, fsq, frstd_set, gained, out_written = (
            sem("moe_done"), sem("fsq"), sem("frstd_set"), sem("gained"), sem("out_written"))
        out_set = [sem(f"out_set{t}") for t in range(TT)]
        dve_step, pool_step = sem("dve_step"), sem("pool_step")
        sel_made, moved = sem("sel_made"), sem("moved")
        ikw_in = sem("ikw_in")
        chunk_asked = sem("chunk_asked")

        def job(name):
            j = JOBS.index(name)
            return j % 2, j // 2 + 1

        def job_computed(eng, name):
            b, n = job(name)
            eng.wait_ge(proj_done[b], n)
            return ps[:, b, :]

        def job_evacuated(eng, name):
            b, n = job(name)
            eng.wait_ge(proj_free[b], n)

        def evacuates(ins, name):
            ins.then_inc(proj_free[job(name)[0]], 1)

        def chunk(name):
            return ring[CHUNKS.index(name) % RING]

        def w512(name):
            return chunk(name).rearrange("p (k n) -> p k n", k=KD)

        def halves(name):
            return chunk(name).rearrange("p (a k n) -> p a k n", a=2, k=KD)

        def weights(name):
            if name in ("iq", "ckv"):
                return "ckv_iq", halves("ckv_iq")[:, ("iq", "ckv").index(name)]
            if name in ("km", "vm"):
                return "kx_vx", halves("kx_vx")[:, ("km", "vm").index(name)]
            if name == "qx":
                return "qx_ox", halves("qx_ox")[:, 0]
            stem, i = name[:-1], int(name[-1])
            if stem in ("oa", "ob"):
                return stem, chunk(stem).rearrange("p (k n) -> p k n", k=4)[:, :, 256 * i:256 * i + 256]
            c = f"{stem}{i // 2}" if stem in ("ga", "gb", "out") else stem
            return c, w512(c)[:, :, 256 * (i % 2):256 * (i % 2) + 256]

        def part(buf, name):
            k, n = (KD, IKW) if name == "ikw" else weights(name)[1].shape[1:]
            return buf[:, SPLITS.index(name) % 2, 0:k * n].rearrange("p (k n) -> p k n", k=k)

        def pieces(name, buf):
            dst = part(buf, name)
            if name != "ikw":
                return [(weights(name)[1], dst)]
            keys = w_ikw[:, :, 0:IDX_DIM].unsqueeze(2).to_broadcast([P, KD, 4, IDX_DIM])
            return [(keys, dst[:, :, 0:4 * IDX_DIM].rearrange("p k (j d) -> p k j d", j=4)),
                    (w_ikw[:, :, IDX_DIM:], dst[:, :, 4 * IDX_DIM:])]

        def chunk_landed(eng, name):
            s, v = landed(name)
            eng.wait_ge(slot_in[s], v)

        def weights_landed(eng, name):
            if name == "ikw":
                eng.wait_ge(ikw_in, 16)
            elif name == "iq":
                eng.wait_ge(iq_in, 16)
            else:
                chunk_landed(eng, weights(name)[0])

        def weights_split(eng, name):
            by_pool, n = low_parts(name)
            eng.wait_ge(low_set[by_pool], n)

        def low_weights(eng, name):
            eng.wait_ge(split_high, SPLITS.index(name) + 1)
            for (src, low), (_, high) in zip(pieces(name, w_low), pieces(name, w_high)):
                m = eng.tensor_tensor(low, src, high.bitcast(F32), ALU.subtract)
            m.then_inc(low_set[low_parts(name)[0]], 1)

        w_in2, w_out2 = w_in[0], w_out[0]
        block = ctx.enter_context(nc.Block())

        @block.sync
        def _(sp):
            def cols(c0, n):
                return w_in2.rearrange("(p k) n -> p k n", k=KD)[:, :, c0:c0 + n]

            def chunk_done(name):
                if name in SPLITS:
                    weights_split(sp, SPLITS[SPLITS.index(name) - 1])
                    weights_split(sp, name)
                else:
                    job_computed(sp, name)

            def fill(name, parts):
                c = CHUNKS.index(name)
                if c >= RING:
                    chunk_done(LAST_JOB[CHUNKS[c - RING]])
                at = 0
                for src in parts:
                    n = src.shape[1] * src.shape[2]
                    dst = chunk(name)[:, at:at + n].rearrange("p (k n) -> p k n", n=src.shape[2])
                    sp.dma_start(dst, src).then_inc(slot_in[c % RING], 16)
                    at += n

            x_v = x[0].rearrange("(t p) d -> p t d", p=P)
            sp.dma_start(x_sb[:, 0, :], x_v[:, 0, :]).then_inc(x_in[0], 16)
            sp.dma_start(x_sb[:, 1, :], x_v[:, 1, :]).then_inc(x_in[1], 16)
            sp.dma_start(ident, consts[:, 0:P]).then_inc(ident_in, 16)
            sp.dma_start(gain[:, 0, :], norm_mix[0].rearrange("(p k) -> p k", k=KD)).then_inc(gain0_in, 16)
            sp.dma_start(halves("ckv_iq")[:, 0], cols(C_IQ, 256)).then_inc(iq_in, 16)
            sp.dma_start(w_ikw[:], cols(C_IK, IDX_DIM + IDX_HEADS)).then_inc(ikw_in, 16)
            sp.dma_start(rel_sb[:], rel_bias).then_inc(tab_in, 16)
            sp.dma_start(one_hot, buckets).then_inc(tab_in, 16)
            sp.dma_start(below_sb, below).then_inc(tab_in, 16)
            sp.dma_start(halves("ckv_iq")[:, 1], cols(C_CKV, 256)).then_inc(slot_in[0], 16)
            sp.dma_start(mem_sb, mem[0].rearrange("(t p) d -> p t d", p=P)).then_inc(mem_in, 16)
            sp.dma_start(const[:, P:], consts[:, P:]).then_inc(const_in, 16)
            sp.dma_start(gain_c[:], ckv_norm[0].rearrange("(p k) -> p k", k=2)).then_inc(gain_in, 16)
            with nc.allow_non_contiguous_dma(reason="gains of 1024 numbers, once"):
                sp.dma_start(gain[:, 1, :], mem_norm[0].rearrange("(k p) -> p k", p=P)).then_inc(gain_in, 16)
            fill("aq", [cols(C_AQ, 512)])
            fill("ak", [cols(C_AK, 512)])
            with nc.allow_non_contiguous_dma(reason="gains of 1024 numbers, once"):
                sp.dma_start(gain[:, 2, :], norm_x[0].rearrange("(k p) -> p k", p=P)).then_inc(small_in, 16)
                sp.dma_start(gain[:, 4, :], norm_moe[0].rearrange("(k p) -> p k", p=P)).then_inc(small_in, 16)
                sp.dma_start(w_rt[:, :, 0:GROUPS], w_group[0].rearrange("(k p) n -> p k n", k=KD)).then_inc(small_in, 16)
            sp.dma_start(w_rt[:, :, GROUPS:], w_router[0].rearrange("(k p) n -> p k n", k=KD)).then_inc(small_in, 16)
            sp.dma_start(gain[:, 3, :], norm_moe[0].rearrange("(p k) -> p k", k=KD)).then_inc(small_in, 16)
            sp.dma_start(b_rt[:, 0:GROUPS], b_group.to_broadcast([P, GROUPS])).then_inc(small_in, 16)
            sp.dma_start(b_rt[:, GROUPS:], b_router.to_broadcast([P, EXPERTS])).then_inc(small_in, 16)
            sp.wait_ge(biasrow_set, 1)
            sp.dma_start(bias_dram, bias_rows).then_inc(bias_out, 16)
            fill("av", [cols(C_AV, 512)])
            sp.wait_ge(bias_out, 16)
            sp.dma_start(bias_rep, bias_dram.unsqueeze(1).to_broadcast([2 * HEADS, P, T + P])).then_inc(bias_repeated, 16)
            fill("kx_vx", [w[0].rearrange("(k p) n -> p k n", k=KD) for w in (wk_x, wv_x)])
            sp.wait_ge(bias_repeated, 16)
            toeplitz = bass.AP(tensor=bias_rep.tensor, offset=P - 1,
                               ap=[[T + P - 1, P], [P * (T + P), 2 * HEADS], [1, T]])
            sp.dma_start(bias, toeplitz).then_inc(bias_in, 16)
            fill("ga0", [cols(C_GA, 512)])
            fill("ga1", [cols(C_GA + 512, 512)])
            fill("uk_uv", [w[0].rearrange("(p k) n -> p k n", k=2) for w in (w_uk, w_uv)])
            fill("bq", [cols(C_BQ, 512)])
            fill("gb0", [cols(C_GB, 512)])
            fill("gb1", [cols(C_GB + 512, 512)])
            fill("oa", [w_oa[0].rearrange("(k p) n -> p k n", p=P)])
            fill("ob", [w_ob[0].rearrange("(k p) n -> p k n", p=P)])
            for i in range(2):
                fill(f"out{i}", [w_out2.rearrange("(k p) n -> p k n", p=P)[:, :, 512 * i:512 * i + 512]])
            fill("qx_ox", [wq_x[0].rearrange("(k p) n -> p k n", k=KD), wo_x[0].rearrange("(k p) n -> p k n", p=P)])

            w1v = w1[0].rearrange("e (p k) n -> p e (k n)", k=KD)
            w3v = w3[0].rearrange("e (p k) n -> p e (k n)", k=KD)
            w2v = w2[0].rearrange("e (p f) n -> p e (f n)", f=FC)

            def load(q, e0):
                e = e0 + (q // MOE_CHUNKS) * SHARE
                j = q % MOE_CHUNKS
                if j < 8:
                    src = (w1v, w3v)[j % 2][:, bass.ds(e, SHARE), (j // 2) * 2 * D_E:(j // 2 + 1) * 2 * D_E]
                else:
                    src = w2v[:, bass.ds(e, SHARE), (j - 8) * D:(j - 7) * D]
                s = moe_slot(q)
                dst = ring[s].rearrange("p (e n) -> p e n", e=SHARE)
                if j < 8:
                    sp.dma_start(dst, src).then_inc(slot_in[s], 16)
                else:
                    sp.dma_start(dst[:, :, 0:512], src[:, :, 0:512]).then_inc(slot_in[s], 16)
                    sp.dma_start(dst[:, :, 512:D], src[:, :, 512:D]).then_inc(right_in[s], 16)

            def load_part(turn, expert, first, end):
                used = [sp.snap(turn * TURN_CHUNKS + used_before(q)) for q in range(first, end)]
                e0 = sp.snap(expert)
                for q in range(first, end):
                    sp.wait_ge(chunk_used, used[q - first])
                    sp.sem_inc(chunk_asked, 1)
                    load(q, e0)

            def load_rest(r, first_part_loaded):
                per_turn = UNROLL * SHARE
                if not first_part_loaded:
                    load_part(r * TURNS, 0, 0, MOE_RING)
                with sp.Fori(0, TURNS - 1) as g:
                    load_part(r * TURNS + g, g * per_turn, MOE_RING, TURN_CHUNKS)
                    load_part(r * TURNS + g + 1, g * per_turn + per_turn, 0, MOE_RING)
                load_part(r * TURNS + (TURNS - 1), (TURNS - 1) * per_turn, MOE_RING, TURN_CHUNKS)

            for q in range(MOE_RING):
                s = MOE_SLOTS[q]
                if s < RING:
                    chunk_done(LAST_JOB[[c for i, c in enumerate(CHUNKS) if i % RING == s][-1]])
                elif s == 8 or s < 6:
                    job_computed(sp, "qx")
                elif s == 6:
                    sp.wait_ge(s_read, 8)
                else:
                    sp.wait_ge(s_done, 8)
                    sp.wait_ge(o_done, 4)
                load(q, 0)
            job_computed(sp, "xo3")
            sp.dma_start(fgain, final_norm.rearrange("(a d) -> a d", a=1).to_broadcast([P, D])).then_inc(fgain_in, 16)
            load_rest(0, True)
            sp.wait_ge(most_set, 1)
            fullest = sp.value_load(most_i[0:1, 0:1], min_val=0, max_val=T)
            with sp.If(fullest > SLOTS):
                with sp.Fori(1, ROUNDS) as r:
                    with sp.If(fullest > r * SLOTS):
                        load_rest(r, False)
            out_v = out[0].rearrange("(t p) d -> p t d", p=P)
            for t in range(TT):
                sp.wait_ge(out_set[t], 1)
                sp.dma_start(out_v[:, t, :], xn[:, t, :]).then_inc(out_written, 16)
            sp.wait_ge(out_written, 16 * TT)

        @block.tensor
        def _(pe):
            def turn(src, ready):
                for t in range(TT):
                    pe.wait_ge(ready[t], 1)
                    for b in range(4):
                        for k in range(2 * b, 2 * b + 2):
                            m = pe.transpose(turned[:, k, t * P:(t + 1) * P], src[:, t, k * P:(k + 1) * P], ident)
                        if t == TT - 1:
                            m.then_inc(turn_done, 1)

            def turn_residual(b):
                pe.wait_ge(resid_set, b + 1)
                for k in range(2 * b, 2 * b + 2):
                    for t in range(TT):
                        m = pe.transpose(turned[:, k, t * P:(t + 1) * P], x_sb[:, t, k * P:(k + 1) * P], ident)
                m.then_inc(turn_done, 1)

            h = (h_high, h_low)

            def h_ready(n):
                def ready(k):
                    if k % 2 == 0:
                        pe.wait_ge(h_low_set, 4 * n + k // 2 + 1)
                return ready

            def begin(name):
                b, n = job(name)
                if n > 1:
                    pe.wait_ge(proj_free[b], n - 1)
                return ps[:, b, :]

            def end(ins, name):
                ins.then_inc(proj_done[job(name)[0]], 1)

            def columns(name, w, src, blocks, width):
                o = begin(name)
                kk = w.shape[1]
                for i, c in enumerate(blocks):
                    for k in range(kk):
                        m = pe.matmul(o[:, i * width:(i + 1) * width], w[:, k, c * P:(c + 1) * P], src[:, k, :],
                                      start=(k == 0), stop=(k == kk - 1))
                end(m, name)
                return m

            def rows(name, w, src, tiles, c0, n):
                o = begin(name)
                kk = w.shape[1]
                for i, t in enumerate(tiles):
                    for k in range(kk):
                        m = pe.matmul(o[:, i * n:(i + 1) * n], src[:, k, t * P:(t + 1) * P], w[:, k, c0:c0 + n],
                                      start=(k == 0), stop=(k == kk - 1))
                end(m, name)
                return m

            def split_columns(name, src, ready=None):
                o = begin(name)
                weights_split(pe, name)
                wh, wl = part(w_high, name), part(w_low, name)
                kk = wh.shape[1]
                for i in range(2):
                    for k in range(kk):
                        if ready and i == 0:
                            ready(k)
                        c = slice(i * P, i * P + P)
                        for j, (w, x_) in enumerate(((wh, src[0]), (wh, src[1]), (wl, src[0]))):
                            m = pe.matmul(o[:, i * T:(i + 1) * T], w[:, k, c], x_[:, k, :],
                                          start=(k + j == 0), stop=(k == kk - 1 and j == 2))
                end(m, name)

            def split_rows(name, src, ready=None):
                o = begin(name)
                weights_split(pe, name)
                wh, wl = part(w_high, name), part(w_low, name)
                for t in range(TT):
                    for k in range(KD):
                        if ready and t == 0:
                            ready(k)
                        for j, (w, x_) in enumerate(((wh, src[0]), (wl, src[0]), (wh, src[1]))):
                            m = pe.matmul(o[:, t * 256:(t + 1) * 256], x_[:, k, t * P:(t + 1) * P], w[:, k, :],
                                          start=(k + j == 0), stop=(k == KD - 1 and j == 2))
                end(m, name)

            pe.wait_ge(ident_in, 16)
            turn(xn, xn_set)
            pe.wait_ge(tab_in, 48)
            m = pe.matmul(ps[0:2 * HEADS, 7, 0:3 * P], rel_sb[:], one_hot, start=True, stop=True)
            m.then_inc(biasrow_done, 1)
            o = begin("iq")
            wh, wl = part(w_high, "iq"), part(w_low, "iq")
            for j, (w, x_) in enumerate(((wh, h_high), (wl, h_high), (wh, h_low))):
                if j == 1:
                    weights_split(pe, "iq")
                for k in range(KD):
                    if k % 2 == 0 and j != 1:
                        pe.wait_ge((h_high_set, None, h_low_set)[j], k // 2 + 1)
                    for i in range(2):
                        m = pe.matmul(o[:, i * T:(i + 1) * T], w[:, k, i * P:i * P + P], x_[:, k, :],
                                      start=(i + k + j == 0), stop=(k == KD - 1 and j == 2), skip_group_check=True)
            end(m, "iq")
            o = begin("ikw")
            weights_split(pe, "ikw")
            wh, wl = part(w_high, "ikw"), part(w_low, "ikw")
            for k in range(KD):
                for j, (w, x_) in enumerate(((wh, h_high), (wh, h_low), (wl, h_high))):
                    pe.matmul(o[:, 0:T], w[:, k, 0:P], x_[:, k, :], start=(k + j == 0), stop=(k == KD - 1 and j == 2))
            for t in range(TT):
                for k in range(KD):
                    for j, (w, x_) in enumerate(((wh, h_high), (wl, h_high), (wh, h_low))):
                        m = pe.matmul(o[:, T + 8 * t:T + 8 * t + 8], x_[:, k, t * P:(t + 1) * P], w[:, k, P:IKW],
                                      start=(k + j == 0), stop=(k == KD - 1 and j == 2))
            end(m, "ikw")

            def index_logits(b):
                for h in range(4):
                    q = 32 * h
                    pe.matmul(ps[:, 2 + h, 0:P], iqT[q:q + 32, b, 0:P], ikT[q:q + 32, 0:P], start=True, stop=True)
                    m = pe.matmul(ps[:, 2 + h, P:3 * P], iqT[q:q + 32, b, P:T], ikT[q:q + 32, :],
                                  start=True, stop=True)
                m.then_inc(idx_done, 1)

            job_evacuated(pe, "iq")
            job_evacuated(pe, "ikw")
            index_logits(0)
            split_rows("ckv", h)
            pe.wait_ge(relu_set, 1)
            index_logits(1)
            pe.wait_ge(relu_set, 2)
            turn(mem_sb, mem_scaled)
            job_evacuated(pe, "ckv")
            o = begin("ckvT")
            for r in range(2):
                for t in range(TT):
                    m = pe.transpose(o[:, r * T + t * P:r * T + (t + 1) * P],
                                     ckvn[:, t, r * P:(r + 1) * P], ident)
            end(m, "ckvT")
            for name in ("aq0", "aq1", "ak0", "ak1"):
                split_columns(name, h)
            split_rows("av0", h)
            split_rows("av1", h)
            pe.wait_ge(h_low_set, 8)

            def scores(n):
                if n == 0:
                    for name in ("aq0", "aq1", "ak0", "ak1"):
                        job_evacuated(pe, name)
                if n == 4:
                    for name in ("bq0", "bq1", "kb0", "kb1"):
                        job_evacuated(pe, name)
                if n >= 2:
                    pe.wait_ge(s_read, n - 1)
                q, k = (aqT, akT) if n < 4 else (bqT, kbT)
                for h in range(2):
                    r, b = HD * h, 2 + 2 * (n % 2) + h
                    pe.matmul(ps[:, b, 0:P], q[r:r + HD, n % 4, 0:P], k[r:r + HD, n % 4, 0:P], start=True, stop=True)
                    m = pe.matmul(ps[:, b, P:3 * P], q[r:r + HD, n % 4, P:T], k[r:r + HD, n % 4, :],
                                  start=True, stop=True)
                m.then_inc(s_done, 1)

            def turn_probs(n):
                pe.wait_ge(prob_set, n + 1)
                if n >= 1:
                    pe.wait_ge(o_split, n)
                for h in range(2):
                    if n >= 1:
                        pe.wait_ge((probT_copied_a, probT_copied_v)[h], n)
                    for c in range(3):
                        m = pe.transpose(ps[:, 6 + h, c * P:(c + 1) * P], logit[:, n % 2, h, c * P:(c + 1) * P], ident)
                    m.then_inc(probT_done, 1)

            def weigh(n):
                if n == 0:
                    job_evacuated(pe, "av0")
                    job_evacuated(pe, "av1")
                if n == 4:
                    job_evacuated(pe, "vb0")
                    job_evacuated(pe, "vb1")
                pe.wait_ge(probT_copied_a, n + 1)
                pe.wait_ge(probT_copied_v, n + 1)
                v = av if n < 4 else vb
                c0 = (n % 4) * P
                for h in range(2):
                    r = slice(HD * h, HD * h + HD)
                    vs = [v[:, s, c0 + HD * h:c0 + HD * h + HD] for s in range(2)]
                    pT = probT[:, n % 2, h, :]
                    pe.matmul(ps[r, 6, 3 * P:4 * P], vs[0], pT[:, 0:P], start=True, stop=True)
                    pe.matmul(ps[r, 7, 3 * P:4 * P], vs[0], pT[:, P:2 * P], start=True, stop=False)
                    m = pe.matmul(ps[r, 7, 3 * P:4 * P], vs[1], pT[:, 2 * P:3 * P], start=False, stop=True)
                m.then_inc(o_done, 1)

            def latent():
                job_evacuated(pe, "ckvT")
                chunk_landed(pe, "uk_uv")
                w = chunk("uk_uv")[:, 0:2048].rearrange("p (a k n) -> p a k n", a=2, k=2)
                columns("kb0", w[:, 0], ckvT, (0, 1), T)
                columns("kb1", w[:, 0], ckvT, (2, 3), T)
                rows("vb0", w[:, 1], ckvT, (0,), 0, 512)
                rows("vb1", w[:, 1], ckvT, (1,), 0, 512)

            for n in range(9):
                if n == 4:
                    latent()
                if n == 6:
                    pe.wait_ge(o_split, 4)
                for name in SLOT_JOBS[n]:
                    if name == "vm":
                        split_rows(name, (tT_high, tT_low))
                    else:
                        split_columns(name, {"oa": oA, "km": (tT_high, tT_low)}.get(name[:2], h))
                if n >= 1:
                    turn_probs(n - 1)
                if n < 8:
                    scores(n)
                if n >= 1:
                    weigh(n - 1)
            pe.wait_ge(o_split, 8)
            for i in range(4):
                split_columns(f"ob{i}", oB)

            def merged_ready(k):
                if k % 2 == 0:
                    pe.wait_ge(merged_set, k // 2 + 1)

            for i in range(4):
                split_rows(f"out{i}", h, merged_ready if i == 0 else None)
                if i:
                    turn_residual(i - 1)
            turn_residual(3)

            split_columns("qx", (tT_high, tT_low), h_ready(2))
            wo = chunk("qx_ox")[:, 2048:4096].rearrange("p (k n) -> p k n", k=2)
            for name in ("qx", "km", "vm"):
                job_evacuated(pe, name)
            for h in range(X_HEADS):
                r = HD * (h % 2)
                for t in range(TT):
                    m = pe.matmul(ps[:, 2 + h, t * MEM:(t + 1) * MEM], qxT[r:r + HD, h // 2, t * P:(t + 1) * P],
                                  kmT[r:r + HD, h // 2, :], start=True, stop=True)
                m.then_inc(xs_done, 1)
            for h in range(X_HEADS):
                pe.wait_ge(xprob_set, h + 1)
                if h >= 2:
                    pe.wait_ge((xpT_copied_a, xpT_copied_v)[h % 2], 1)
                for j in range(2):
                    for t in range(TT):
                        m = pe.transpose(ps[:, 6 + h % 2, j * T + t * P:j * T + (t + 1) * P],
                                         xprob[:, h, t, j * P:(j + 1) * P], ident)
                m.then_inc(xpT_done, 1)
            for c in range(2):
                o = begin(f"ox{c}")
                pe.wait_ge(xpT_copied_a, c + 1)
                pe.wait_ge(xpT_copied_v, c + 1)
                for h in range(2):
                    for j in range(2):
                        m = pe.matmul(o[HD * h:HD * h + HD, 0:T], vm[:, j, c * P + HD * h:c * P + HD * h + HD],
                                      xprobT[:, 2 * c + h, j, :], start=(j == 0), stop=(j == 1))
                end(m, f"ox{c}")
            job_evacuated(pe, "ox0")
            job_evacuated(pe, "ox1")
            chunk_landed(pe, "qx_ox")

            def turn_for_router(i):
                pe.wait_ge(xresid_set, i + 1)
                for j in range(4):
                    k = 4 * (i % 2) + j
                    m = pe.transpose(ps[:, 2 + i, j * P:(j + 1) * P], x_sb[:, i // 2, k * P:(k + 1) * P], ident)
                m.then_inc(xturned, 1)

            def route(t):
                for k in range(KD):
                    if k % 4 == 0:
                        pe.wait_ge(xT_copied, 2 * t + k // 4 + 1)
                    m = pe.matmul(ps[0:N_RT, 6 + t, 0:P], w_rt[:, k, :], xT[:, k, t * P:(t + 1) * P],
                                  start=(k == 0), stop=(k == KD - 1))
                m.then_inc(logitsT_done, 1)

            rows("xo0", wo, oxT, (0,), 0, 512)
            rows("xo1", wo, oxT, (0,), 512, 512)
            pe.wait_ge(xexp_set, X_HEADS)
            pe.wait_ge(xprob_set, X_HEADS)
            turn_for_router(0)
            rows("xo2", wo, oxT, (1,), 0, 512)
            turn_for_router(1)
            rows("xo3", wo, oxT, (1,), 512, 512)
            turn_for_router(2)
            pe.wait_ge(router_set, 1)
            route(0)
            turn_for_router(3)
            route(1)
            for t in range(TT):
                pe.wait_ge(logitsT_copied, t + 1)
                m = pe.transpose(ps[:, 6 + t, P:P + N_RT], rlT[:, t * P:(t + 1) * P], ident[0:N_RT, 0:N_RT])
                m.then_inc(logits_done, 1)
            job_evacuated(pe, "xo3")
            job_evacuated(pe, "xo2")
            def start_sum(t):
                for c in range(2):
                    pe.matmul(ps[:, 2 * t + c, :], ident, x_sb[:, t, 512 * c:512 * c + 512],
                              start=True, stop=True, skip_group_check=True)

            start_sum(0)
            pe.wait_ge(const_in, 16)
            pe.wait_ge(routed, 1)
            lt, one = const[:, K_LT:K_LT + P], const[:, K_ONE:K_ONE + P]
            chosen = rt[:, 8]
            pe.matmul(ps[:, 6, 0:EXPERTS], lt, chosen[:, 0, :], start=True, stop=True)
            pe.matmul(ps[:, 6, EXPERTS:2 * EXPERTS], lt, chosen[:, 1, :], start=True, stop=False)
            pe.matmul(ps[:, 6, EXPERTS:2 * EXPERTS], one, chosen[:, 0, :], start=False, stop=True)
            pe.matmul(ps[:, 6, 2 * EXPERTS:3 * EXPERTS], one, chosen[:, 0, :], start=True, stop=False)
            pe.matmul(ps[:, 6, 2 * EXPERTS:3 * EXPERTS], one, chosen[:, 1, :], start=False,
                      stop=True).then_inc(count_done, 1)
            start_sum(1)
            pe.wait_ge(count_read, 1)
            for t in range(TT):
                pe.wait_ge(xn_set[t], 2)

            def expert_step(turn, u):
                it = turn * UNROLL + u
                pe.wait_ge(sel_made, it + 1)
                pe.wait_ge(actT_copied, it + 1)
                pe.wait_ge(selwT_copied, it + 1)

                def gather(k):
                    for t in range(TT):
                        m = pe.matmul(ps[:, 6 + k // 4, (k % 4) * P:(k % 4 + 1) * P], xn[:, t, k * P:(k + 1) * P],
                                      sel[:, t], start=(t == 0), stop=(t == TT - 1))
                    if k % 4 == 3:
                        m.then_inc(xe_done, 1)

                for k in range(6):
                    gather(k)
                pe.wait_ge(y_copied_a, it + 1)
                pe.wait_ge(y_copied_v, it + 1)
                for q in range(8):
                    if q == 0:
                        pe.wait_ge(xe_copied, it * 2 + 1)
                    if q == 2:
                        gather(6)
                        gather(7)
                    if q == 4:
                        pe.wait_ge(xe_copied, it * 2 + 2)
                        pe.wait_ge(sel_set, it + 1)
                        for t in range(TT):
                            m = pe.transpose(ps[:, 7, t * P:(t + 1) * P], selw[:, t], ident)
                        m.then_inc(selwT_done, 1)
                    s = moe_slot(u * MOE_CHUNKS + q)
                    value, _, per_turn, _ = moe_landed(u * MOE_CHUNKS + q)
                    pe.wait_ge(slot_in[s], turn * per_turn + value)
                    w = ring[s].rearrange("p (e k n) -> p e k n", e=SHARE, k=2)
                    for kk in range(2):
                        k = 2 * (q // 2) + kk
                        for e in range(SHARE):
                            m = pe.matmul(ps[SLOTS * e:SLOTS * e + SLOTS, 4 + q % 2, :],
                                          xeT[:, k, SLOTS * e:SLOTS * e + SLOTS], w[:, e, kk, :],
                                          start=(k == 0), stop=(k == KD - 1), skip_group_check=True)
                    m.then_inc(chunk_used, 1)
                pe.wait_ge(act_set, it + 2)
                for f in range(FC):
                    m = pe.transpose(ps[:, 6, f * P:(f + 1) * P], act_sb[:, f * P:(f + 1) * P], ident)
                m.then_inc(actT_done, 1)
                pe.wait_ge(actT_copied, it + 2)
                for f in range(FC):
                    s = moe_slot(u * MOE_CHUNKS + 8 + f)
                    value, right, per_turn, right_per_turn = moe_landed(u * MOE_CHUNKS + 8 + f)
                    pe.wait_ge(slot_in[s], turn * per_turn + value)
                    w = ring[s].rearrange("p (e n) -> p e n", e=SHARE)
                    for c in range(2):
                        if c == 1:
                            pe.wait_ge(right_in[s], turn * right_per_turn + right)
                        for e in range(SHARE):
                            m = pe.matmul(ps[SLOTS * e:SLOTS * e + SLOTS, 4 + c, :],
                                          actT[:, f, SLOTS * e:SLOTS * e + SLOTS], w[:, e, 512 * c:512 * c + 512],
                                          start=(f == 0), stop=(f == FC - 1), skip_group_check=True)
                        if c == 0 and f == FC - 1:
                            m.then_inc(y_left_done, 1)
                    m.then_inc(chunk_used, 1)
                pe.wait_ge(selwT_copied, it + 2)
                for c in range(2):
                    pe.wait_ge((y_copied_a, y_copied_v)[c], it + 2)
                    for t in range(TT):
                        m = pe.matmul(ps[:, 2 * t + c, :], selwT[:, t * P:(t + 1) * P], y_sb[:, 512 * c:512 * c + 512],
                                      start=False, stop=True, skip_group_check=True)
                m.then_inc(added, 1)

            for signal in (added, actT_done, selwT_done):
                pe.sem_inc(signal, 1)
            def round_of_steps(r):
                with pe.Fori(0, TURNS) as g:
                    for u in range(UNROLL):
                        expert_step(g + r * TURNS, u)

            pe.wait_ge(most_set, 1)
            fullest = pe.value_load(most_i[0:1, 0:1], min_val=0, max_val=T)
            round_of_steps(0)
            with pe.If(fullest > SLOTS):
                with pe.Fori(1, ROUNDS) as r:
                    with pe.If(fullest > r * SLOTS):
                        round_of_steps(r)
            pe.matmul(ps[0:1, 6, 0:1], ident[:, 0:1], ident[:, 0:1], start=True, stop=True).then_inc(moe_done, 1)

        @block.scalar
        def _(act):
            def square(src, n, t, junk, signal):
                return act.activation(junk, src, ACT.Square, accum_out=ssq[:, n, t:t + 1]).then_inc(signal, 1)

            def scaled(src, n, t):
                return act.activation(xn[:, t, :].rearrange("p (k q) -> p k q", k=KD),
                                      src.rearrange("p (q k) -> p k q", k=KD), ACT.Copy, scale=rstd[:, n, t:t + 1])

            def split_turned(n, b, g, high):
                act.wait_ge(turn_done, 4 * n + b + 1)
                for k in range(2 * b, 2 * b + 2):
                    m = act.activation(high[:, k, :], turned[:, k, :], ACT.Copy, scale=gain[:, g, k:k + 1])
                m.then_inc(h_high_set, 1)

            def split_weights(u):
                name = SPLITS[u]
                weights_landed(act, name)
                if u >= 2:
                    job_computed(act, SPLITS[u - 2])
                for src, dst in pieces(name, w_high):
                    m = act.activation(dst, src, ACT.Copy)
                m.then_inc(split_high, 1)

            def after(name):
                u = SPLITS.index(name) + 2
                if u < len(SPLITS):
                    split_weights(u)

            def copy_job(name, dst, src=None):
                o = job_computed(act, name)
                evacuates(act.activation(dst, o if src is None else src(o), ACT.Copy), name)

            act.wait_ge(x_in[0], 16)
            square(x_sb[:, 0, :], 0, 0, xn[:, 0, :], squares[0])
            act.wait_ge(rstd_set[0], 1)
            scaled(x_sb[:, 0, :], 0, 0).then_inc(xn_set[0], 1)
            act.wait_ge(gain0_in, 16)
            split_weights(0)
            for b in range(4):
                split_turned(0, b, 0, h_high)
            split_weights(1)
            act.wait_ge(mem_in, 16)
            square(mem_sb[:, 0, :], 1, 0, junk[:, 0:4, :].rearrange("p a b -> p (a b)"), squares[0])
            copy_job("iq", iqT[:].rearrange("p a b -> p (a b)"))
            after("iq")
            after("ikw")
            act.wait_ge(idx_done, 1)
            act.activation(relu4, ps[:, 2:6, 0:3 * P], ACT.Relu).then_inc(relu_set, 1)
            act.wait_ge(rstd_set[0], 2)
            act.activation(mem_sb[:, 0, :], mem_sb[:, 0, :], ACT.Copy, scale=rstd[:, 1, 0:1]).then_inc(mem_scaled[0], 1)
            act.wait_ge(gain_in, 16 * 2)
            o = job_computed(act, "ckv")
            for t in range(TT):
                square(o[:, t * RANK:(t + 1) * RANK], 4, t, junk[:, 4 + t, :], csq_done)
            after("ckv")
            act.wait_ge(idx_done, 2)
            act.wait_ge(idx_added, 1)
            act.activation(relu4, ps[:, 2:6, 0:3 * P], ACT.Relu).then_inc(relu_set, 1)
            act.wait_ge(crstd_set, 1)
            for t in range(TT):
                m = act.activation(ckvn[:, t, :].rearrange("p (k q) -> p k q", k=2),
                                   o[:, t * RANK:(t + 1) * RANK].rearrange("p (q k) -> p k q", k=2),
                                   ACT.Copy, scale=rstd[:, 4, t:t + 1])
            evacuates(m, "ckv")
            for b in range(4):
                split_turned(1, b, 1, tT_high)
            o = job_computed(act, "ckvT")
            for r in range(2):
                m = act.activation(ckvT[:, r, :], o[:, r * T:(r + 1) * T], ACT.Copy, scale=gain_c[:, r:r + 1])
            evacuates(m, "ckvT")

            def pair(buf, i):
                return buf[:, 2 * i:2 * i + 2, :].rearrange("p a b -> p (a b)")

            def by_rows(o):
                return o.rearrange("p (t n) -> p t n", t=TT)

            for name, buf in (("aq", aqT), ("ak", akT)):
                for i in range(2):
                    copy_job(f"{name}{i}", pair(buf, i))
                    after(f"{name}{i}")
            for i in range(2):
                copy_job(f"av{i}", av[:, :, 256 * i:256 * i + 256], by_rows)
                after(f"av{i}")

            def exps(n):
                act.wait_ge(max_set, n + 1)
                for h in range(2):
                    for t in range(TT):
                        seg = slice(0, P) if t == 0 else slice(P, 3 * P)
                        j = 2 * h + t
                        m = act.activation(logit[:, n % 2, h, seg], logit[:, n % 2, h, seg], ACT.Exp,
                                           bias=nmax[:, n, j:j + 1], accum_out=esum[:, n, j:j + 1])
                m.then_inc(exp_set, 1)

            def copy_probT(n):
                act.wait_ge(probT_done, 2 * n + 1)
                if n >= 2:
                    act.wait_ge(o_done, n - 1)
                act.activation(probT[:, n % 2, 0, :], ps[:, 6, 0:3 * P], ACT.Copy).then_inc(probT_copied_a, 1)

            def copy_o(n):
                act.wait_ge(o_done, n + 1)
                dst = (oA if n < 4 else oB)[0][:, n % 4, :]
                act.activation(dst.rearrange("p (t c) -> p t c", t=TT), ps[:, 6:8, 3 * P:4 * P],
                               ACT.Copy).then_inc(o_copied, 1)

            def gate_job(branch, i):
                o = job_computed(act, f"{branch}{i}")
                buf = ga if branch == "ga" else gb
                m = act.activation(pair(buf, i), o, ACT.Tanh, scale=0.5)
                evacuates(m, f"{branch}{i}")

            for n in range(9):
                if n == 4:
                    copy_job("kb0", pair(kbT, 0))
                    copy_job("kb1", pair(kbT, 1))
                    copy_job("vb0", vb[:, 0, :])
                    copy_job("vb1", vb[:, 1, :])
                names = SLOT_JOBS[n]
                for i, name in enumerate(names):
                    if name[0] == "g":
                        gate_job(name[:2], int(name[2]))
                    elif name[0] == "b":
                        copy_job(name, pair(bqT, i))
                    elif name in ("km", "vm"):
                        copy_job(name, (kmT if name == "km" else vm).rearrange("p a b -> p (a b)"))
                    if i == 0:
                        after(name)
                if n >= 1:
                    copy_probT(n - 1)
                    copy_o(n - 1)
                if names:
                    after(names[1])
                if n < 8:
                    exps(n)
            for i in range(4):
                after(f"ob{i}")
                act.wait_ge(merge_added, i + 1)
                act.activation(pair(h_high, i), pair(ga, i), ACT.Copy).then_inc(merge_high, 1)
            act.wait_ge(small_in, 16 * 7)
            for i in range(4):
                after(f"out{i}")
                if i:
                    split_turned(2, i - 1, 2, tT_high)
            split_turned(2, 3, 2, tT_high)
            square(x_sb[:, 0, :], 2, 0, xn[:, 0, :], squares[0])
            copy_job("qx", qxT[:].rearrange("p a b -> p (a b)"))

            def cross_exp(h):
                act.wait_ge(xmax_set, h + 1)
                for t in range(TT):
                    m = act.activation(xprob[:, h, t, :], ps[:, 2 + h, t * MEM:(t + 1) * MEM], ACT.Exp,
                                       scale=qscale[:, t:t + 1], bias=xnmax[:, h, t:t + 1],
                                       accum_out=xsum[:, h, t:t + 1])
                m.then_inc(xexp_set, 1)

            def cross_copy(h):
                act.wait_ge(xpT_done, h + 1)
                act.activation(xprobT[:, h].rearrange("p a b -> p (a b)"), ps[:, 6, :], ACT.Copy).then_inc(xpT_copied_a, 1)

            cross_exp(0)
            cross_exp(1)
            cross_exp(2)
            cross_copy(0)
            cross_exp(3)
            cross_copy(2)
            for c in range(2):
                copy_job(f"ox{c}", oxT[:].rearrange("p a b -> p (a b)")[:, c * T:(c + 1) * T], lambda o: o[:, 0:T])
            for i in range(4):
                act.wait_ge(xturned, i + 1)
                act.activation(xT[:, 4 * (i % 2):4 * (i % 2) + 4, (i // 2) * P:(i // 2 + 1) * P],
                               ps[:, 2 + i, :].rearrange("p (k t) -> p k t", k=4), ACT.Copy).then_inc(xT_copied, 1)
                if i == 2:
                    square(x_sb[:, 0, :], 3, 0, xn[:, 0, :], squares[0])
            act.wait_ge(logitsT_done, 1)
            act.activation(rlT[:, 0:P], ps[0:N_RT, 6, 0:P], ACT.Copy).then_inc(logitsT_copied, 1)
            act.wait_ge(logitsT_done, 2)
            act.activation(rlT[:, P:T], ps[0:N_RT, 7, 0:P], ACT.Copy).then_inc(logitsT_copied, 1)
            act.wait_ge(rstd_set[0], 4)
            scaled(x_sb[:, 0, :], 3, 0).then_inc(xn_set[0], 1)
            act.wait_ge(rstd_set[1], 4)
            scaled(x_sb[:, 1, :], 3, 1).then_inc(xn_set[1], 1)
            act.wait_ge(rexp_asked, 1)
            act.activation(rt[:, 7], rt[:, 10], ACT.Exp)
            act.activation(rt[:, 13, :, 0:GROUPS], rt[:, 12, :, 0:GROUPS], ACT.Exp).then_inc(rexp_set, 1)

            def expert_step(turn, u):
                it = turn * UNROLL + u
                act.wait_ge(selwT_done, it + 2)
                act.wait_ge(added, it + 1)
                act.activation(selwT, ps[:, 7, 0:T], ACT.Copy).then_inc(selwT_copied, 1)
                act.wait_ge(chunk_used, it * MOE_CHUNKS + 8)
                act.wait_ge(act_set, it + 1)
                act.activation(silu_sb, ps[:, 4, :].rearrange("p (q f) -> p f q", f=FC), ACT.Silu).then_inc(silu_set, 1)
                act.wait_ge(y_left_done, it + 1)
                act.activation(y_sb[:, 0:512], ps[:, 4, :], ACT.Copy).then_inc(y_copied_a, 1)

            for signal in (selwT_copied, y_copied_a):
                act.sem_inc(signal, 1)
            def round_of_steps(r):
                with act.Fori(0, TURNS) as g:
                    for u in range(UNROLL):
                        expert_step(g + r * TURNS, u)

            act.wait_ge(most_set, 1)
            fullest = act.value_load(most_i[0:1, 0:1], min_val=0, max_val=T)
            round_of_steps(0)
            with act.If(fullest > SLOTS):
                with act.Fori(1, ROUNDS) as r:
                    with act.If(fullest > r * SLOTS):
                        round_of_steps(r)
            act.wait_ge(moe_done, 1)
            square(ps[:, 0:2, :], 5, 0, x_sb[:, 0, :].rearrange("p (a b) -> p a b", a=2), fsq)
            act.wait_ge(gained, 1)
            square(ps[:, 2:4, :], 5, 1, x_sb[:, 1, :].rearrange("p (a b) -> p a b", a=2), fsq)
            act.wait_ge(frstd_set, 2)
            act.activation(xn[:, 1, :], xn[:, 1, :], ACT.Copy, scale=rstd[:, 5, 1:2]).then_inc(out_set[1], 1)

        @block.vector
        def _(dve):
            steps = [0]

            def mark(ins):
                steps[0] += 1
                ins.then_inc(dve_step, 1)

            def then(ins):
                mark(ins)
                dve.wait_ge(dve_step, steps[0])

            def wait_marked():
                dve.wait_ge(dve_step, steps[0])

            def square(src, n, junk):
                dve.tensor_tensor_reduce(junk, src, src, 1.0, 0.0, ALU.mult, ALU.add,
                                         ssq[:, n, 1:2]).then_inc(squares[1], 1)

            def scaled(src, n):
                return dve.tensor_scalar(xn[:, 1, :].rearrange("p (k q) -> p k q", k=KD),
                                         src.rearrange("p (q k) -> p k q", k=KD), rstd[:, n, 1:2], None, ALU.mult)

            def split_turned(i, b, g, high, low):
                dve.wait_ge(h_high_set, 4 * i + b + 1)
                for k in range(2 * b, 2 * b + 2):
                    m = dve.scalar_tensor_tensor(low[:, k, :], turned[:, k, :], gain[:, g, k:k + 1],
                                                 high[:, k, :].bitcast(F32), ALU.mult, ALU.subtract)
                m.then_inc(h_low_set, 1)

            def after(name):
                u = SPLITS.index(name) + 2
                if u < len(SPLITS) and SPLITS[u] not in POOL_LOW:
                    low_weights(dve, SPLITS[u])

            dve.memset(half[:], -0.5).then_inc(half_set, 1)
            dve.memset(wanted[:], -TAKEN)
            dve.wait_ge(x_in[1], 16)
            square(x_sb[:, 1, :], 0, xn[:, 1, :])
            dve.wait_ge(rstd_set[1], 1)
            scaled(x_sb[:, 1, :], 0).then_inc(xn_set[1], 1)
            dve.wait_ge(gain0_in, 16)
            low_weights(dve, SPLITS[0])
            for b in range(4):
                split_turned(0, b, 0, h_high, h_low)
            low_weights(dve, SPLITS[1])
            dve.wait_ge(tab_in, 48)
            dve.wait_ge(biasrow_done, 1)
            dve.tensor_tensor(bias_rows, ps[0:2 * HEADS, 7, 0:3 * P], below_sb, ALU.add).then_inc(biasrow_set, 1)
            dve.wait_ge(mem_in, 16)
            square(mem_sb[:, 1, :], 1, junk[:, 4:8, :].rearrange("p a b -> p (a b)"))
            after("iq")
            o = job_computed(dve, "ikw")
            dve.tensor_copy(ikT[:], o[:, 0:T])
            evacuates(dve.tensor_scalar(iw[:], o[:, T:T + 16].rearrange("p (t h) -> p t h", t=TT),
                                        IDX_HEADS ** -0.5 * IDX_DIM ** -0.5, None, ALU.mult), "ikw")
            after("ikw")
            dve.wait_ge(rstd_set[1], 2)
            dve.tensor_scalar(mem_sb[:, 1, :], mem_sb[:, 1, :], rstd[:, 1, 1:2], None, ALU.mult).then_inc(mem_scaled[1], 1)
            dve.wait_ge(gain_in, 16 * 2)
            dve.wait_ge(const_in, 16)
            job_evacuated(dve, "ikw")
            for b in range(2):
                dve.wait_ge(relu_set, b + 1)
                for h in range(4):
                    if b + h:
                        wait_marked()
                    for t in range(TT):
                        seg = slice(0, P) if t == 0 else slice(P, 3 * P)
                        first = const[:, K_CAUSAL:K_CAUSAL + 3 * P][:, seg]
                        m = dve.scalar_tensor_tensor(score[:, seg], relu4[:, h, seg], iw[:, t, 4 * b + h:4 * b + h + 1],
                                                     first if b + h == 0 else score[:, seg], ALU.mult, ALU.add)
                    if h < 3 or b == 1:
                        mark(m)
                    else:
                        m.then_inc(idx_added, 1)
                        dve.wait_ge(idx_added, 1)
                        after("ckv")
            wait_marked()
            for b in range(4):
                split_turned(1, b, 1, tT_high, tT_low)
            segs = (slice(0, P), slice(P, 3 * P))
            for i in range(TOPK // 8):
                for t in range(TT):
                    m = dve.max(top8[:, t, :], score[:, segs[t]])
                mark(m)
                wait_marked()
                for t in range(TT):
                    m = dve.match_replace(score[:, segs[t]], top8[:, t, :], score[:, segs[t]], TAKEN)
                mark(m)
                wait_marked()
                if i % 2:
                    after(("aq0", "aq1", "ak0", "ak1")[i // 2])
            then(dve.tensor_scalar(unpicked[:], score[:], TAKEN / 2, NEG, ALU.is_gt, ALU.mult))
            after("av0")
            after("av1")

            def logits(n):
                if n == 0:
                    dve.wait_ge(bias_in, 16)
                dve.wait_ge(s_done, n + 1)
                if n >= 2:
                    dve.wait_ge(probT_done, 2 * (n - 1))
                b0 = 2 + 2 * (n % 2)
                buf = logit[:, n % 2]
                dve.scalar_tensor_tensor(buf[:, :, P:3 * P], ps[:, b0:b0 + 2, P:3 * P], SCALE,
                                         bias[:, 2 * n:2 * n + 2, :], ALU.mult, ALU.add)
                dve.scalar_tensor_tensor(buf[:, :, 0:P], ps[:, b0:b0 + 2, 0:P], SCALE,
                                         bias[:, 2 * n:2 * n + 2, P:T], ALU.mult, ALU.add).then_inc(s_read, 1)
                dve.wait_ge(s_read, n + 1)
                if n >= 4:
                    then(dve.tensor_tensor(buf, buf, unpicked[:].unsqueeze(1).to_broadcast([P, 2, 3 * P]), ALU.add))
                dve.tensor_reduce(nmax[:, n, 0:4:2], buf[:, :, 0:P], AX_X, ALU.max, negate=True)
                dve.tensor_reduce(nmax[:, n, 1:4:2], buf[:, :, P:3 * P], AX_X, ALU.max, negate=True).then_inc(max_set, 1)

            def normalise(n):
                dve.wait_ge(exp_set, n + 1)
                then(dve.reciprocal(erec[:, n, :], esum[:, n, :]))
                for h in range(2):
                    for t in range(TT):
                        m = dve.tensor_scalar(logit[:, n % 2, h, segs[t]], logit[:, n % 2, h, segs[t]],
                                              erec[:, n, 2 * h + t:2 * h + t + 1], None, ALU.mult)
                m.then_inc(prob_set, 1)

            def copy_probT(n):
                dve.wait_ge(probT_done, 2 * n + 2)
                if n >= 2:
                    dve.wait_ge(o_done, n - 1)
                dve.tensor_copy(probT[:, n % 2, 1, :], ps[:, 7, 0:3 * P]).then_inc(probT_copied_v, 1)

            def split_o(n):
                dve.wait_ge(o_copied, n + 1)
                high, low = oA if n < 4 else oB
                dve.tensor_tensor(low[:, n % 4, :].rearrange("p (t c) -> p t c", t=TT), ps[:, 6:8, 3 * P:4 * P],
                                  high[:, n % 4, :].bitcast(F32).rearrange("p (t c) -> p t c", t=TT),
                                  ALU.subtract).then_inc(o_split, 1)

            def pair(buf, i):
                return buf[:, 2 * i:2 * i + 2, :].rearrange("p a b -> p (a b)")

            for n in range(9):
                names = SLOT_JOBS[n]
                if n == 6:
                    dve.wait_ge(gates_set, 1)
                for i, name in enumerate(names):
                    if name[:2] == "oa":
                        o = job_computed(dve, name)
                        part_a = pair(ga, int(name[2]))
                        evacuates(dve.tensor_tensor(part_a, o, part_a, ALU.mult), name)
                    if i == 0:
                        after(name)
                if n >= 1:
                    copy_probT(n - 1)
                if n < 8:
                    logits(n)
                if n >= 1:
                    split_o(n - 1)
                if names:
                    after(names[1])
                if n < 8:
                    normalise(n)
            dve.wait_ge(gates_set, 2)
            for i in range(4):
                o = job_computed(dve, f"ob{i}")
                evacuates(dve.tensor_tensor(pair(gb, i), o, pair(gb, i), ALU.mult), f"ob{i}")
                job_evacuated(dve, f"ob{i}")
                job_evacuated(dve, f"oa{i}")
                dve.tensor_tensor(pair(ga, i), pair(ga, i), pair(gb, i), ALU.add).then_inc(merge_added, 1)
                after(f"ob{i}")
                dve.wait_ge(merge_high, i + 1)
                dve.tensor_tensor(pair(h_low, i), pair(ga, i), pair(h_high, i).bitcast(F32),
                                  ALU.subtract).then_inc(merged_set, 1)

            def add_residual(name, part_x, signal, shaped=lambda o: o):
                o = job_computed(dve, name)
                evacuates(dve.tensor_tensor(part_x, shaped(o), part_x, ALU.add), name)
                job_evacuated(dve, name)
                dve.sem_inc(signal, 1)

            dve.wait_ge(small_in, 16 * 7)
            dve.tensor_tensor(w_rt[:], w_rt[:], gain[:, 4, :].unsqueeze(2).to_broadcast([P, KD, N_RT]),
                              ALU.mult).then_inc(router_set, 1)
            for i in range(4):
                add_residual(f"out{i}", x_sb[:, :, 256 * i:256 * i + 256], resid_set,
                             lambda o: o.rearrange("p (t n) -> p t n", t=TT))
                after(f"out{i}")
                if i:
                    split_turned(2, i - 1, 2, tT_high, tT_low)
            split_turned(2, 3, 2, tT_high, tT_low)
            square(x_sb[:, 1, :], 2, xn[:, 1, :])
            for t in range(TT):
                dve.wait_ge(rstd_set[t], 3)
            dve.tensor_scalar(qscale[:], rstd[:, 2, :], SCALE, None, ALU.mult).then_inc(qscale_set, 1)
            dve.wait_ge(qscale_set, 1)

            def cross_max(h):
                dve.wait_ge(xs_done, h + 1)
                then(dve.tensor_reduce(xnmax[:, h, :], ps[:, 2 + h, :].rearrange("p (t m) -> p t m", t=TT), AX_X,
                                       ALU.max, negate=True))
                dve.tensor_tensor(xnmax[:, h, :], xnmax[:, h, :], qscale[:], ALU.mult).then_inc(xmax_set, 1)

            def cross_normalise(h):
                dve.wait_ge(xexp_set, h + 1)
                then(dve.reciprocal(xrec[:, h, :], xsum[:, h, :]))
                for t in range(TT):
                    m = dve.tensor_scalar(xprob[:, h, t, :], xprob[:, h, t, :], xrec[:, h, t:t + 1], None, ALU.mult)
                m.then_inc(xprob_set, 1)

            def cross_copy(h):
                dve.wait_ge(xpT_done, h + 1)
                dve.tensor_copy(xprobT[:, h].rearrange("p a b -> p (a b)"), ps[:, 7, :]).then_inc(xpT_copied_v, 1)

            cross_max(0)
            cross_max(1)
            cross_normalise(0)
            cross_max(2)
            cross_normalise(1)
            cross_max(3)
            cross_normalise(2)
            cross_copy(1)
            cross_normalise(3)
            cross_copy(3)
            for i in range(4):
                add_residual(f"xo{i}", x_sb[:, i // 2, 512 * (i % 2):512 * (i % 2) + 512], xresid_set)
            square(x_sb[:, 1, :], 3, xn[:, 1, :])

            dve.memset(rt[:, 0, :, 0:8], 2 * NEG)
            for t in range(TT):
                dve.wait_ge(rstd_set[t], 4)
                dve.wait_ge(logits_done, t + 1)
                m = dve.scalar_tensor_tensor(rl[:, t, :], ps[:, 6 + t, P:P + N_RT], rstd[:, 3, t:t + 1], b_rt[:],
                                             ALU.mult, ALU.add)
            then(m)
            group = rl[:, :, 0:GROUPS]
            padded, em, picked = rt[:, 0, :, 0:8], rt[:, 1], rt[:, 2]
            dve.tensor_copy(rt[:, 0, :, 0:GROUPS], group)
            then(dve.tensor_reduce(wanted[:, :, 0, 0], group, AX_X, ALU.max))
            for t in range(TT):
                m = dve.match_replace(rt[:, 4, t, 0:8], wanted[:, t, 0, :], padded[:, t, :], TAKEN)
            then(m)
            then(dve.tensor_scalar(rt[:, 3, :, 0:GROUPS], rt[:, 4, :, 0:GROUPS], TAKEN / 2, NEG, ALU.is_gt, ALU.mult))
            then(dve.tensor_tensor(em.rearrange("p t (g e) -> p t g e", g=GROUPS),
                                   rl[:, :, GROUPS:].rearrange("p t (g e) -> p t g e", g=GROUPS),
                                   rt[:, 3, :, 0:GROUPS].unsqueeze(3).to_broadcast([P, TT, GROUPS, PER_GROUP]), ALU.add))
            for t in range(TT):
                m = dve.max(rt[:, 5, t, 0:8], em[:, t, :])
            then(m)
            then(dve.tensor_copy(wanted[:, :, 1, 0:2], rt[:, 5, :, 0:2]))
            for t in range(TT):
                m = dve.match_replace(picked[:, t, :], wanted[:, t, 1, :], em[:, t, :], TAKEN)
            then(m)
            chosen = rt[:, 8]
            dve.tensor_scalar(chosen, picked, TAKEN / 2, None, ALU.is_lt).then_inc(routed, 1)
            dve.tensor_tensor(rt[:, 12, :, 0:GROUPS], group, wanted[:, :, 0, 0:1].to_broadcast([P, TT, GROUPS]),
                              ALU.subtract)
            dve.tensor_tensor(rt[:, 10], em, wanted[:, :, 1, 0:1].to_broadcast([P, TT, EXPERTS]),
                              ALU.subtract).then_inc(rexp_asked, 1)
            dve.wait_ge(rexp_set, 1)
            dve.wait_ge(routed, 1)
            dve.tensor_reduce(rs[:, 0, :], rt[:, 13, :, 0:GROUPS], AX_X, ALU.add)
            then(dve.tensor_tensor(rt[:, 6], rt[:, 7], chosen, ALU.mult))
            then(dve.tensor_reduce(rs[:, 1, :], rt[:, 6], AX_X, ALU.add))
            then(dve.tensor_tensor(rs[:, 2, :], rs[:, 0, :], rs[:, 1, :], ALU.mult))
            then(dve.reciprocal(rs[:, 3, :], rs[:, 2, :]))
            weight = rt[:, 11]
            then(dve.tensor_tensor(weight, rt[:, 6], rs[:, 3, :].unsqueeze(2).to_broadcast([P, TT, EXPERTS]), ALU.mult))
            dve.wait_ge(count_done, 1)
            place = rt[:, 9]
            dve.scalar_tensor_tensor(place, ps[:, 6, 0:2 * EXPERTS].rearrange("p (t e) -> p t e", t=TT), 1.0,
                                     rt[:, 8], ALU.add, ALU.mult).then_inc(moved, 1)
            dve.tensor_reduce(most[:], ps[:, 6, 2 * EXPERTS:3 * EXPERTS], AX_X, ALU.max).then_inc(count_read, 1)
            dve.wait_ge(count_read, 1)
            dve.tensor_copy(most_i[:], most[:]).then_inc(most_set, 1)

            slots = const[:, K_SLOT:K_SLOT + SLOTS].unsqueeze(1).unsqueeze(1).to_broadcast([P, TT, SHARE, SLOTS])

            def expert_step(turn, u, expert, r):
                it = turn * UNROLL + u
                e0 = dve.snap(expert)
                dve.wait_ge(moved, r + 1)
                dve.wait_ge(selwT_done, it + 1)
                dve.tensor_tensor(sel, place[:, :, bass.ds(e0, SHARE)].unsqueeze(3).to_broadcast([P, TT, SHARE, SLOTS]),
                                  slots, ALU.is_equal).then_inc(sel_made, 1)
                dve.wait_ge(sel_made, it + 1)
                dve.tensor_tensor(selw, sel, weight[:, :, bass.ds(e0, SHARE)].unsqueeze(3).to_broadcast(
                    [P, TT, SHARE, SLOTS]), ALU.mult).then_inc(sel_set, 1)
                for b in range(2):
                    dve.wait_ge(xe_done, it * 2 + b + 1)
                    dve.tensor_tensor(xeT[:, 4 * b:4 * b + 4, :], ps[:, 6 + b, :].rearrange("p (k s) -> p k s", k=4),
                                          gain[:, 3, 4 * b:4 * b + 4].unsqueeze(2).to_broadcast([P, 4, P]),
                                      ALU.mult).then_inc(xe_copied, 1)
                dve.wait_ge(silu_set, it + 1)
                dve.wait_ge(actT_done, it + 1)
                dve.tensor_tensor(act_sb, ps[:, 5, :].rearrange("p (q f) -> p f q", f=FC),
                                  silu_sb.rearrange("p (f q) -> p f q", f=FC), ALU.mult).then_inc(act_set, 1)
                dve.wait_ge(actT_done, it + 2)
                dve.tensor_copy(actT.rearrange("p f s -> p (f s)"), ps[:, 6, :]).then_inc(actT_copied, 1)
                dve.wait_ge(chunk_used, it * MOE_CHUNKS + MOE_CHUNKS)
                dve.wait_ge(added, it + 1)
                dve.tensor_copy(y_sb[:, 512:1024], ps[:, 5, :]).then_inc(y_copied_v, 1)

            for signal in (actT_copied, y_copied_v, act_set):
                dve.sem_inc(signal, 1)
            def round_of_steps(r):
                with dve.Fori(0, TURNS) as g:
                    for u in range(UNROLL):
                        expert_step(g + r * TURNS, u, g * (UNROLL * SHARE) + u * SHARE, r)

            round_of_steps(0)
            dve.wait_ge(most_set, 1)
            fullest = dve.value_load(most_i[0:1, 0:1], min_val=0, max_val=T)
            with dve.If(fullest > SLOTS):
                with dve.Fori(1, ROUNDS) as r:
                    with dve.If(fullest > r * SLOTS):
                        dve.tensor_scalar(place, place, -float(SLOTS), None, ALU.add).then_inc(moved, 1)
                        round_of_steps(r)

            dve.wait_ge(fgain_in, 16)
            dve.wait_ge(moe_done, 1)
            for t in (1, 0):
                if t == 0:
                    dve.wait_ge(fsq, 1)
                dve.tensor_tensor(xn[:, t, :].rearrange("p (c n) -> p c n", c=2), ps[:, 2 * t:2 * t + 2, :],
                                  fgain.rearrange("p (c n) -> p c n", c=2), ALU.mult).then_inc(gained, 1)
            dve.wait_ge(gained, 2)
            dve.wait_ge(frstd_set, 1)
            dve.tensor_scalar(xn[:, 0, :], xn[:, 0, :], rstd[:, 5, 0:1], None, ALU.mult).then_inc(out_set[0], 1)

        @block.gpsimd
        def _(pool):
            steps = [0]

            def inverse_rms(n, t, width, signal):
                steps[0] += 1
                pool.tensor_scalar(var[:, n, t], ssq[:, n, t], 1.0 / width, EPS, ALU.mult, ALU.add).then_inc(pool_step, 1)
                pool.wait_ge(pool_step, steps[0])
                pool.tensor_tensor(rstd[:, n, t], var[:, n, t], half[:, t], ALU.pow).then_inc(signal, 1)

            def of_d_model(n):
                for t in range(TT):
                    pool.wait_ge(squares[t], n + 1)
                    inverse_rms(n, slice(t, t + 1), D, rstd_set[t])

            pool.wait_ge(half_set, 1)
            of_d_model(0)
            of_d_model(1)
            pool.wait_ge(csq_done, 2)
            inverse_rms(4, slice(0, 2), RANK, crstd_set)
            def finish_gates(buf, branch):
                for i in range(4):
                    job_evacuated(pool, f"{branch}{i}")
                pool.tensor_scalar(buf[:], buf[:], 0.5, 0.5, ALU.mult, ALU.add).then_inc(gates_set, 1)

            finish_gates(ga, "ga")
            for name in POOL_LOW:
                low_weights(pool, name)
                if name == "oa3":
                    finish_gates(gb, "gb")
            of_d_model(2)
            of_d_model(3)
            for t in range(TT):
                pool.wait_ge(fsq, t + 1)
                inverse_rms(5, slice(t, t + 1), D, frstd_set)


NAMES = ["x", "mem", "rel_bias", "final_norm", "norm_mix", "w_in", "ckv_norm", "w_uk", "w_uv", "w_oa", "w_ob",
         "w_out", "norm_x", "mem_norm", "wq_x", "wk_x", "wv_x", "wo_x", "norm_moe", "w_group", "b_group",
         "w_router", "b_router", "w1", "w3", "w2"]


def kernel(**inputs):
    import concourse.bacc as bacc
    from concourse.bass_utils import run_bass_kernel_spmd

    nc = bacc.Bacc("TRN2", target_bir_lowering=False, num_devices=1)
    arrays = {name: np.ascontiguousarray(inputs[name]) for name in NAMES}
    arrays["consts"], arrays["buckets"], arrays["below"] = shape_constants()
    args = [nc.dram_tensor(f"in_{n}", a.shape, mybir.dt.from_np(a.dtype), kind="ExternalInput").ap()
            for n, a in arrays.items()]
    out = nc.dram_tensor("out", (1, T, D), F32, kind="ExternalOutput").ap()
    decoder_layer(nc, *args, out)
    r = run_bass_kernel_spmd(nc, [{f"in_{n}": a for n, a in arrays.items()}], core_ids=[0])
    return r.results[0]["out"]
```
